# Optimizing a Trainium2 kernel written in Bass

```python
import math
import jax, jax.numpy as jnp
from jax import lax
import numpy as np

D_MODEL = 1024
BATCH = 1
SEQ = 256
DEPTH = 2

HEAD_DIM = 64
N_HEADS_A = D_MODEL // (2 * HEAD_DIM)
N_HEADS_B = D_MODEL // (2 * HEAD_DIM)
N_HEADS_C = D_MODEL // (2 * HEAD_DIM)
A_WIDTH = N_HEADS_A * HEAD_DIM
B_WIDTH = N_HEADS_B * HEAD_DIM
HYB_IN = 3 * A_WIDTH + 3 * B_WIDTH + N_HEADS_B
DIFF_QK = 2 * N_HEADS_C * HEAD_DIM
DIFF_V = N_HEADS_C * 2 * HEAD_DIM
D_FF = 2816
CONV_WIDTH = 3
ROPE_THETA = 10000.0
DILATED_PATTERNS = ((128, 1), (512, 4), (2048, 16))
BLOCK_Q = 128
NORM_EPS = 1e-6
SUBLN_EPS = 1e-5
N_EVEN = (DEPTH + 1) // 2
N_ODD = DEPTH // 2


def rms_norm(x, g, eps=NORM_EPS):
    xf = x.astype(jnp.float32)
    y = xf * lax.rsqrt(jnp.mean(xf * xf, axis=-1, keepdims=True) + eps)
    return (y * g.astype(jnp.float32)).astype(x.dtype)

def rope_tables(seq):
    inv = 1.0 / (ROPE_THETA ** (jnp.arange(0, HEAD_DIM, 2, dtype=jnp.float32) / HEAD_DIM))
    ang = jnp.arange(seq, dtype=jnp.float32)[:, None] * inv[None, :]
    ang = jnp.concatenate([ang, ang], axis=-1)
    return jnp.cos(ang)[None, :, None, :], jnp.sin(ang)[None, :, None, :]

def apply_rope(x, cos, sin):
    x1, x2 = jnp.split(x, 2, axis=-1)
    rot = jnp.concatenate([-x2, x1], axis=-1)
    return (x.astype(jnp.float32) * cos + rot.astype(jnp.float32) * sin).astype(x.dtype)

def local_window_attention(q, k, v, span):
    n, L, h, dh = q.shape
    nb = -(-L // BLOCK_Q)
    lp = nb * BLOCK_Q
    pad = lp - L
    padt = lambda t: jnp.pad(t, ((0, 0), (0, pad), (0, 0), (0, 0)))
    q, k, v = padt(q), padt(k), padt(v)

    def blocks_with_prev(t):
        te = jnp.pad(t, ((0, 0), (BLOCK_Q, 0), (0, 0), (0, 0)))
        prev = te[:, :lp].reshape(n, nb, BLOCK_Q, h, t.shape[-1])
        cur = te[:, BLOCK_Q:].reshape(n, nb, BLOCK_Q, h, t.shape[-1])
        return jnp.concatenate([prev, cur], axis=2)

    kb, vb = blocks_with_prev(k), blocks_with_prev(v)
    qb = q.reshape(n, nb, BLOCK_Q, h, dh)
    s = jnp.einsum('nbqhd,nbkhd->nbhqk', qb, kb, preferred_element_type=jnp.float32)
    i = jnp.arange(BLOCK_Q)[:, None]
    j = jnp.arange(2 * BLOCK_Q)[None, :]
    delta = i - j + BLOCK_Q
    band = (delta >= 0) & (delta <= span)
    blk = jnp.arange(nb)[:, None, None]
    valid = band[None] & (blk * BLOCK_Q - BLOCK_Q + j[None] >= 0)
    s = jnp.where(valid[None, :, None], s, -jnp.inf)
    m = jnp.max(s, axis=-1, keepdims=True)
    p = jnp.exp(s - m)
    denom = jnp.sum(p, axis=-1, keepdims=True)
    o = jnp.einsum('nbhqk,nbkhd->nbqhd', (p / denom).astype(v.dtype), vb)
    lse = (m + jnp.log(denom))[..., 0]
    lse = jnp.transpose(lse, (0, 1, 3, 2)).reshape(n, lp, h)[:, :L]
    o = o.reshape(n, lp, h, dh)[:, :L]
    return o, lse

def dilated_attention(q, k, v):
    b, s, h, dh = q.shape
    outs, lses = [], []
    for window, dil in DILATED_PATTERNS:
        L = s // dil

        def to_sub(t):
            t = t.reshape(b, L, dil, *t.shape[2:])
            return jnp.swapaxes(t, 1, 2).reshape(b * dil, L, *t.shape[3:])

        def from_sub(t):
            t = t.reshape(b, dil, L, *t.shape[2:])
            return jnp.swapaxes(t, 1, 2).reshape(b, s, *t.shape[3:])

        o, lse = local_window_attention(to_sub(q), to_sub(k), to_sub(v), window // dil)
        outs.append(from_sub(o))
        lses.append(from_sub(lse))
    alpha = jax.nn.softmax(jnp.stack(lses, axis=0), axis=0)
    out = jnp.sum(alpha[..., None] * jnp.stack(outs, axis=0).astype(jnp.float32), axis=0)
    return out.astype(q.dtype)

def to_blocks(t):
    b, s = t.shape[:2]
    return jnp.moveaxis(t.reshape(b, s // BLOCK_Q, BLOCK_Q, *t.shape[2:]), 1, 0)

def from_blocks(t):
    nb, b, bq = t.shape[:3]
    return jnp.moveaxis(t, 0, 1).reshape(b, nb * bq, *t.shape[3:])

def causal_block_probs(qb, k, q_start, bias=None):
    s = jnp.einsum('bqhd,bkhd->bhqk', qb, k, preferred_element_type=jnp.float32)
    if bias is not None:
        s = s + bias
    qpos = q_start + jnp.arange(qb.shape[1])
    kpos = jnp.arange(k.shape[1])
    s = jnp.where(kpos[None, :] <= qpos[:, None], s, -jnp.inf)
    return jax.nn.softmax(s, axis=-1)

def forgetting_attention(q, k, v, logf):
    c = jnp.cumsum(logf, axis=1)
    ck = jnp.transpose(c, (0, 2, 1))
    nb = q.shape[1] // BLOCK_Q

    def step(args):
        start, qb, cb = args
        bias = jnp.transpose(cb, (0, 2, 1))[..., :, None] - ck[:, :, None, :]
        p = causal_block_probs(qb, k, start, bias)
        return jnp.einsum('bhqk,bkhd->bqhd', p.astype(v.dtype), v)

    out = lax.map(step, (jnp.arange(nb) * BLOCK_Q, to_blocks(q), to_blocks(c)))
    return from_blocks(out)

def differential_attention(q1, q2, k1, k2, v, lam):
    nb = q1.shape[1] // BLOCK_Q

    def step(args):
        start, q1b, q2b = args
        a = causal_block_probs(q1b, k1, start) - lam * causal_block_probs(q2b, k2, start)
        return jnp.einsum('bhqk,bkhd->bqhd', a.astype(v.dtype), v)

    out = lax.map(step, (jnp.arange(nb) * BLOCK_Q, to_blocks(q1), to_blocks(q2)))
    return from_blocks(out)

def hybrid_mixer(n, w_in, b_f, w_out, cos, sin):
    b, s, _ = n.shape
    proj = n @ w_in
    cuts = [A_WIDTH, 2 * A_WIDTH, 3 * A_WIDTH,
            3 * A_WIDTH + B_WIDTH, 3 * A_WIDTH + 2 * B_WIDTH, 3 * A_WIDTH + 3 * B_WIDTH]
    qa, ka, va, qb, kb, vb, fb = jnp.split(proj, cuts, axis=-1)
    heads = lambda t: t.reshape(b, s, -1, HEAD_DIM)
    scale = HEAD_DIM ** -0.5
    oa = dilated_attention(apply_rope(heads(qa), cos, sin) * scale,
                           apply_rope(heads(ka), cos, sin), heads(va))
    logf = jax.nn.log_sigmoid((fb + b_f).astype(jnp.float32))
    ob = forgetting_attention(heads(qb) * scale, heads(kb), heads(vb), logf)
    o = jnp.concatenate([oa.reshape(b, s, A_WIDTH), ob.reshape(b, s, B_WIDTH)], axis=-1)
    return o @ w_out

def diff_mixer(n, w_qkv, lam_params, subln_g, w_out, cos, sin, layer_idx):
    b, s, _ = n.shape
    q, k, v = jnp.split(n @ w_qkv, [DIFF_QK, 2 * DIFF_QK], axis=-1)
    scale = HEAD_DIM ** -0.5
    q = (apply_rope(q.reshape(b, s, 2 * N_HEADS_C, HEAD_DIM), cos, sin) * scale).reshape(b, s, N_HEADS_C, 2, HEAD_DIM)
    k = apply_rope(k.reshape(b, s, 2 * N_HEADS_C, HEAD_DIM), cos, sin).reshape(b, s, N_HEADS_C, 2, HEAD_DIM)
    v = v.reshape(b, s, N_HEADS_C, 2 * HEAD_DIM)
    lam_init = 0.8 - 0.6 * math.exp(-0.3 * layer_idx)
    lp = lam_params.astype(jnp.float32)
    lam = jnp.exp(jnp.sum(lp[0] * lp[1])) - jnp.exp(jnp.sum(lp[2] * lp[3])) + lam_init
    o = differential_attention(q[:, :, :, 0], q[:, :, :, 1], k[:, :, :, 0], k[:, :, :, 1], v, lam)
    o = rms_norm(o, subln_g, SUBLN_EPS) * (1.0 - lam_init)
    return o.reshape(b, s, DIFF_V) @ w_out

def conv_glu_ffn(n, w_up, conv_w, conv_b, w_down):
    s = n.shape[1]
    gate, up = jnp.split(n @ w_up, 2, axis=-1)
    gp = jnp.pad(gate, ((0, 0), (CONV_WIDTH - 1, 0), (0, 0)))
    conv = conv_b
    for j in range(CONV_WIDTH):
        conv = conv + gp[:, j:j + s] * conv_w[j]
    return (jax.nn.silu(conv) * up) @ w_down

def first_inputs(seed: int = 0) -> dict:
    key = jax.random.key(seed)
    ks = jax.random.split(key, 20)
    nrm = lambda k, shape, fan_in: jax.random.normal(k, shape, jnp.float32) * fan_in ** -0.5
    return {
        "x": jax.random.normal(ks[0], (BATCH, SEQ, D_MODEL), jnp.float32),
        "attn_norm": 1.0 + 0.02 * jax.random.normal(ks[1], (DEPTH, D_MODEL), jnp.float32),
        "ffn_norm": 1.0 + 0.02 * jax.random.normal(ks[2], (DEPTH, D_MODEL), jnp.float32),
        "final_norm": 1.0 + 0.02 * jax.random.normal(ks[3], (D_MODEL,), jnp.float32),
        "hyb_w_in": nrm(ks[4], (N_EVEN, D_MODEL, HYB_IN), D_MODEL),
        "hyb_b_f": 2.0 + 0.5 * jax.random.normal(ks[5], (N_EVEN, N_HEADS_B), jnp.float32),
        "hyb_w_out": nrm(ks[6], (N_EVEN, A_WIDTH + B_WIDTH, D_MODEL), A_WIDTH + B_WIDTH),
        "diff_w_qkv": nrm(ks[7], (N_ODD, D_MODEL, 2 * DIFF_QK + DIFF_V), D_MODEL),
        "diff_lambda": 0.1 * jax.random.normal(ks[8], (N_ODD, 4, HEAD_DIM), jnp.float32),
        "diff_subln": 1.0 + 0.02 * jax.random.normal(ks[9], (N_ODD, 2 * HEAD_DIM), jnp.float32),
        "diff_w_out": nrm(ks[10], (N_ODD, DIFF_V, D_MODEL), DIFF_V),
        "ffn_w_up": nrm(ks[11], (DEPTH, D_MODEL, 2 * D_FF), D_MODEL),
        "ffn_conv_w": nrm(ks[12], (DEPTH, CONV_WIDTH, D_FF), CONV_WIDTH),
        "ffn_conv_b": 0.01 * jax.random.normal(ks[13], (DEPTH, D_FF), jnp.float32),
        "ffn_w_down": nrm(ks[14], (DEPTH, D_FF, D_MODEL), D_FF),
    }

def first_block(x, attn_norm, ffn_norm, final_norm, hyb_w_in, hyb_b_f, hyb_w_out,
              diff_w_qkv, diff_lambda, diff_subln, diff_w_out,
              ffn_w_up, ffn_conv_w, ffn_conv_b, ffn_w_down):
    cos, sin = rope_tables(x.shape[1])
    h = x
    for l in range(DEPTH):
        n = rms_norm(h, attn_norm[l])
        if l % 2 == 0:
            e = l // 2
            h = h + hybrid_mixer(n, hyb_w_in[e], hyb_b_f[e], hyb_w_out[e], cos, sin)
        else:
            o = l // 2
            h = h + diff_mixer(n, diff_w_qkv[o], diff_lambda[o], diff_subln[o], diff_w_out[o], cos, sin, l)
        h = h + conv_glu_ffn(rms_norm(h, ffn_norm[l]), ffn_w_up[l], ffn_conv_w[l], ffn_conv_b[l], ffn_w_down[l])
    return rms_norm(h, final_norm)


CHUNK = 64
Q_BLOCK = 128
EPS = 1e-6

A_HEADS = 8
A_NOPE = 64
A_ROPE = 32
A_VDIM = 64
A_QLORA = 256
A_KVLORA = 128

B_HEADS = 4
B_DIM = 64

POOL_WINDOWS = (2, 4, 8, 16)
POOL_CH = 64

A_WIDTH_2 = A_HEADS * A_VDIM
B_WIDTH_2 = B_HEADS * B_DIM
C_WIDTH = len(POOL_WINDOWS) * POOL_CH
D_MIX = A_WIDTH_2 + B_WIDTH_2 + C_WIDTH

A_IN = A_QLORA + A_KVLORA + A_ROPE
B_IN = 3 * B_WIDTH_2
D_IN = A_IN + B_IN + C_WIDTH

N_GROUPS = 4
EXPERTS_PER_GROUP = 8
TOP_K_INNER = 2
D_EXPERT = 256


def rms_norm_2(x, g):
    xf = x.astype(jnp.float32)
    y = xf * lax.rsqrt(jnp.mean(xf * xf, axis=-1, keepdims=True) + EPS)
    return (y * g.astype(jnp.float32)).astype(x.dtype)

def rope_tables_2(seq):
    pos = jnp.arange(seq, dtype=jnp.float32)
    inv = ROPE_THETA ** (-jnp.arange(0, A_ROPE, 2, dtype=jnp.float32) / A_ROPE)
    ang = pos[:, None] * inv[None, :]
    return jnp.cos(ang), jnp.sin(ang)

def apply_rope_2(x, cos, sin):
    half = x.shape[-1] // 2
    x1 = x[..., :half].astype(jnp.float32)
    x2 = x[..., half:].astype(jnp.float32)
    out = jnp.concatenate([x1 * cos - x2 * sin, x2 * cos + x1 * sin], axis=-1)
    return out.astype(x.dtype)

def mla_mixer(c_q, c_kv, k_r, q_norm_g, w_uq, kv_norm_g, w_ukv):
    B, S, _ = c_q.shape
    cos, sin = rope_tables_2(S)
    q = jnp.einsum('bsr,rf->bsf', rms_norm_2(c_q, q_norm_g), w_uq).reshape(B, S, A_HEADS, A_NOPE + A_ROPE)
    q = jnp.concatenate([q[..., :A_NOPE], apply_rope_2(q[..., A_NOPE:], cos[None, :, None], sin[None, :, None])], axis=-1)
    kv = jnp.einsum('bsr,rf->bsf', rms_norm_2(c_kv, kv_norm_g), w_ukv).reshape(B, S, A_HEADS, A_NOPE + A_VDIM)
    k_rope = apply_rope_2(k_r, cos[None], sin[None])
    k = jnp.concatenate([kv[..., :A_NOPE], jnp.broadcast_to(k_rope[:, :, None, :], (B, S, A_HEADS, A_ROPE))], axis=-1)
    v = kv[..., A_NOPE:]
    scale = (A_NOPE + A_ROPE) ** -0.5
    chunk_id = jnp.arange(S) // CHUNK
    outs = []
    for i in range(S // Q_BLOCK):
        q0, q1 = i * Q_BLOCK, (i + 1) * Q_BLOCK
        s = jnp.einsum('bqhd,bkhd->bhqk', q[:, q0:q1], k[:, :q1]).astype(jnp.float32) * scale
        allowed = chunk_id[:q1][None, :] <= chunk_id[q0:q1][:, None]
        s = jnp.where(allowed, s, -1e30)
        p = jax.nn.softmax(s, axis=-1).astype(v.dtype)
        outs.append(jnp.einsum('bhqk,bkhd->bqhd', p, v[:, :q1]))
    return jnp.concatenate(outs, axis=1).reshape(B, S, A_WIDTH_2)

def stick_breaking_mixer(q, k, v):
    B, S = q.shape[0], q.shape[1]
    pos = jnp.arange(S)
    scale = B_DIM ** -0.5
    outs = []
    for i in range(S // Q_BLOCK):
        q0, q1 = i * Q_BLOCK, (i + 1) * Q_BLOCK
        z = jnp.einsum('bqhd,bkhd->bhqk', q[:, q0:q1], k[:, :q1]).astype(jnp.float32) * scale
        strict = pos[:q1][None, :] < pos[q0:q1][:, None]
        log_1m_beta = jnp.where(strict, -jax.nn.softplus(z), 0.0)
        between = lax.cumsum(log_1m_beta, axis=3, reverse=True) - log_1m_beta
        a = jnp.where(strict, jnp.exp(jax.nn.log_sigmoid(z) + between), 0.0).astype(v.dtype)
        outs.append(jnp.einsum('bhqk,bkhd->bqhd', a, v[:, :q1]))
    return jnp.concatenate(outs, axis=1).reshape(B, S, B_WIDTH_2)

def pool_mixer(u, pool_w, pool_scale):
    B, S, _ = u.shape
    uf = u.astype(jnp.float32)
    cs = jnp.concatenate([jnp.zeros((B, 1, C_WIDTH), jnp.float32), jnp.cumsum(uf, axis=1)], axis=1)
    pos = jnp.arange(S, dtype=jnp.float32)
    groups = []
    for g, w in enumerate(POOL_WINDOWS):
        c = cs[..., g * POOL_CH:(g + 1) * POOL_CH]
        lag = jnp.pad(c[:, :S - w + 1], ((0, 0), (w - 1, 0), (0, 0)))
        count = jnp.minimum(pos + 1.0, float(w))[None, :, None]
        mean = (c[:, 1:] - lag) / count
        groups.append(mean - uf[..., g * POOL_CH:(g + 1) * POOL_CH])
    d = jnp.stack(groups, axis=2).astype(u.dtype)
    y = jnp.einsum('bsgc,gcd->bsgd', d, pool_w).reshape(B, S, C_WIDTH)
    return y * pool_scale

def hier_moe(h, w_group, b_group, w_expert, b_expert, w_gate, w_up, w_down):
    B, S, D = h.shape
    t = h.reshape(B * S, D)
    g_prob = jax.nn.softmax((t @ w_group + b_group).astype(jnp.float32), axis=-1)
    p_sel, g_idx = lax.top_k(g_prob, 1)
    p_sel, g_idx = p_sel[:, 0], g_idx[:, 0]
    e_logits = (t @ w_expert + b_expert).astype(jnp.float32).reshape(B * S, N_GROUPS, EXPERTS_PER_GROUP)
    e_in = jnp.take_along_axis(e_logits, g_idx[:, None, None], axis=1)[:, 0]
    e_prob = jax.nn.softmax(e_in, axis=-1)
    w_k, i_k = lax.top_k(e_prob, TOP_K_INNER)
    w_k = w_k / jnp.sum(w_k, axis=-1, keepdims=True)
    inner = jnp.sum(jax.nn.one_hot(i_k, EXPERTS_PER_GROUP, dtype=jnp.float32) * w_k[..., None], axis=1)
    combine = (p_sel[:, None, None] * jax.nn.one_hot(g_idx, N_GROUPS, dtype=jnp.float32)[:, :, None]
               * inner[:, None, :]).astype(t.dtype)
    y = jnp.zeros_like(t)
    for g in range(N_GROUPS):
        a = jnp.einsum('nd,edf->nef', t, w_gate[g])
        b = jnp.einsum('nd,edf->nef', t, w_up[g])
        hid = jax.nn.silu(a) * b * combine[:, g, :, None]
        y = y + jnp.einsum('nef,efd->nd', hid, w_down[g])
    return y.reshape(B, S, D)

def hybrid_layer(x, norm1_g, w_in, q_norm_g, w_uq, kv_norm_g, w_ukv, pool_w, pool_scale, w_out,
                 norm2_g, w_group, b_group, w_expert, b_expert, w_gate, w_up, w_down):
    B, S, _ = x.shape
    hn = rms_norm_2(x, norm1_g)
    proj = jnp.einsum('bsd,df->bsf', hn, w_in)
    o1 = A_QLORA
    o2 = o1 + A_KVLORA
    o3 = o2 + A_ROPE
    o4 = o3 + B_IN
    ya = mla_mixer(proj[..., :o1], proj[..., o1:o2], proj[..., o2:o3], q_norm_g, w_uq, kv_norm_g, w_ukv)
    qkv_b = proj[..., o3:o4].reshape(B, S, 3, B_HEADS, B_DIM)
    yb = stick_breaking_mixer(qkv_b[:, :, 0], qkv_b[:, :, 1], qkv_b[:, :, 2])
    yc = pool_mixer(proj[..., o4:], pool_w, pool_scale)
    mixed = jnp.concatenate([ya, yb, yc], axis=-1)
    x = x + jnp.einsum('bsm,md->bsd', mixed, w_out)
    x = x + hier_moe(rms_norm_2(x, norm2_g), w_group, b_group, w_expert, b_expert, w_gate, w_up, w_down)
    return x

def second_inputs(seed: int = 0) -> dict:
    key = jax.random.key(seed)
    ks = jax.random.split(key, 20)
    L, D = DEPTH, D_MODEL

    def nrm(k, shape, fan_in):
        return jax.random.normal(k, shape, jnp.float32) * (fan_in ** -0.5)

    def gain(k, shape):
        return 1.0 + 0.02 * jax.random.normal(k, shape, jnp.float32)

    return {
        'x': jax.random.normal(ks[0], (BATCH, SEQ, D), jnp.float32),
        'norm1_g': gain(ks[1], (L, D)),
        'w_in': nrm(ks[2], (L, D, D_IN), D),
        'q_norm_g': gain(ks[3], (L, A_QLORA)),
        'w_uq': nrm(ks[4], (L, A_QLORA, A_HEADS * (A_NOPE + A_ROPE)), A_QLORA),
        'kv_norm_g': gain(ks[5], (L, A_KVLORA)),
        'w_ukv': nrm(ks[6], (L, A_KVLORA, A_HEADS * (A_NOPE + A_VDIM)), A_KVLORA),
        'pool_w': nrm(ks[7], (L, len(POOL_WINDOWS), POOL_CH, POOL_CH), POOL_CH),
        'pool_scale': gain(ks[8], (L, C_WIDTH)),
        'w_out': nrm(ks[9], (L, D_MIX, D), D_MIX),
        'norm2_g': gain(ks[10], (L, D)),
        'w_group': nrm(ks[11], (L, D, N_GROUPS), D),
        'b_group': 0.01 * jax.random.normal(ks[12], (L, N_GROUPS), jnp.float32),
        'w_expert': nrm(ks[13], (L, D, N_GROUPS * EXPERTS_PER_GROUP), D),
        'b_expert': 0.01 * jax.random.normal(ks[14], (L, N_GROUPS * EXPERTS_PER_GROUP), jnp.float32),
        'w_gate': nrm(ks[15], (L, N_GROUPS, EXPERTS_PER_GROUP, D, D_EXPERT), D),
        'w_up': nrm(ks[16], (L, N_GROUPS, EXPERTS_PER_GROUP, D, D_EXPERT), D),
        'w_down': nrm(ks[17], (L, N_GROUPS, EXPERTS_PER_GROUP, D_EXPERT, D), D_EXPERT),
        'final_g': gain(ks[18], (D,)),
    }

def second_block(x, norm1_g, w_in, q_norm_g, w_uq, kv_norm_g, w_ukv, pool_w, pool_scale, w_out,
              norm2_g, w_group, b_group, w_expert, b_expert, w_gate, w_up, w_down, final_g):
    for l in range(DEPTH):
        x = hybrid_layer(x, norm1_g[l], w_in[l], q_norm_g[l], w_uq[l], kv_norm_g[l], w_ukv[l],
                         pool_w[l], pool_scale[l], w_out[l], norm2_g[l], w_group[l], b_group[l],
                         w_expert[l], b_expert[l], w_gate[l], w_up[l], w_down[l])
    return rms_norm_2(x, final_g)


def setup_inputs(seed=0):
    out = dict(first_inputs(seed))
    for name, value in second_inputs(seed + 1).items():
        if name != "x":
            out[name + "_2"] = value
    return out


def reference(
    x, attn_norm, ffn_norm, final_norm, hyb_w_in, hyb_b_f, hyb_w_out, diff_w_qkv, diff_lambda,
    diff_subln, diff_w_out, ffn_w_up, ffn_conv_w, ffn_conv_b, ffn_w_down, norm1_g_2, w_in_2,
    q_norm_g_2, w_uq_2, kv_norm_g_2, w_ukv_2, pool_w_2, pool_scale_2, w_out_2, norm2_g_2,
    w_group_2, b_group_2, w_expert_2, b_expert_2, w_gate_2, w_up_2, w_down_2, final_g_2,
):
    x = first_block(
        x, attn_norm, ffn_norm, final_norm, hyb_w_in, hyb_b_f, hyb_w_out, diff_w_qkv,
        diff_lambda, diff_subln, diff_w_out, ffn_w_up, ffn_conv_w, ffn_conv_b, ffn_w_down,
    )
    return second_block(
        x, norm1_g_2, w_in_2, q_norm_g_2, w_uq_2, kv_norm_g_2, w_ukv_2, pool_w_2, pool_scale_2,
        w_out_2, norm2_g_2, w_group_2, b_group_2, w_expert_2, b_expert_2, w_gate_2, w_up_2,
        w_down_2, final_g_2,
    )


_drawn_inputs = setup_inputs


def setup_inputs(seed=0):
    import zlib

    import numpy as np

    out = dict(_drawn_inputs(seed))
    spreads = {}
    factors = {'q_norm_g_2': 5.3,
     'kv_norm_g_2': 3.049,
     'final_g_2': 21.821,
     'pool_scale_2': 2.824,
     'b_group_2': 15.222}
    for name, (base, spread) in spreads.items():
        noise = np.random.default_rng([zlib.crc32(name.encode()), seed]).standard_normal(out[name].shape)
        drawn = base * np.exp(spread * noise) if base else spread * noise
        out[name] = __import__('jax').numpy.asarray(drawn.astype(out[name].dtype))
    for name, factor in factors.items():
        out[name] = (out[name] * factor).astype(out[name].dtype)
    return out
```

```python
import math

import numpy as np
import concourse.bass as bass
from concourse import mybir
from contextlib import ExitStack

F32 = mybir.dt.float32
F32R = mybir.dt.float32r
ALU = mybir.AluOpType
ACT = mybir.ActivationFunctionType
AX = mybir.AxisListType

P = 128
S = 256
NT = S // P
D = 1024
KT = D // P
HD = 64
DFF = 2816
FT = DFF // P
NFB = FT // 2
NE = 32
NG = 4
EG = NE // NG
DE = 256
LAYERS = 2
CH = 2048
RING = 3
AHEAD = 2
NEG = -1e30
EPS = 1e-6
SUB_EPS = 1e-5
LAM_INIT = 0.8 - 0.6 * math.exp(-0.3 * 1)
MLA_QK = 96
MLA_SCALE = float(MLA_QK) ** -0.5
G0W, G1W, G2W = 416, 512, 512

C_FB = 0
C_HYB = 1
C_HYB_OUT = C_HYB + 12
C_FFN = [C_HYB_OUT + 4, 0]
C_DIFF = C_FFN[0] + 3 * NFB
C_DIFF_OUT = C_DIFF + 12
C_FFN[1] = C_DIFF_OUT + 4
C_LAYER = [C_FFN[1] + 3 * NFB, 0]
C_IN2, C_UQ, C_UKV, C_OUT2, C_ROUTER, C_MOE = 0, 6, 7, 8, 12, 13
C_PER_LAYER = C_MOE + 3 * NE
C_LAYER[1] = C_LAYER[0] + C_PER_LAYER
NCHUNK = C_LAYER[1] + C_PER_LAYER



def _columns(fields):
    at, out = 0, {}
    for name, n in fields:
        out[name] = (at, at + n)
        at += n
    return out, at


SMALL, SMALL_N = _columns([
    ("attn_g", 2 * KT), ("ffn_g", 2 * KT), ("norm1_g", 2 * KT), ("norm2_g", 2 * KT), ("c_g", 2 * 3),
    ("subln", 1), ("conv_b", 2 * FT), ("conv_w", 2 * 3 * FT), ("b_f", 1), ("router_b", 2 * (NG + NE)),
    ("pool_scale", 2 * 256), ("lam", 4 * HD), ("pool_w", 2 * 2 * HD)])
CONST, CONST_N = _columns([
    ("ident", P), ("upper", P), ("ones", P), ("dilated", 384), ("causal", 384), ("chunked", 384),
    ("strict", 384), ("cos_q", NT * HD), ("sin_q", NT * HD), ("cos_k", NT * HD), ("sin_k", NT * HD),
    ("cos_m", NT * 32), ("sin_m", NT * 32), ("pool", 4 * 384), ("sel", 8 * P), ("iota", 8), ("iota64", 8),
    ("minus_half", 16), ("inv_c", 4)])

T_BANKS = [4, 4, 4, 4, 4, 4] + [4, 2, 4, 4] * LAYERS
T_BASE = [sum(T_BANKS[:q]) for q in range(len(T_BANKS) + 1)]
T_L0, T_L0O, T_F0, T_L1, T_L1O, T_F1 = range(6)


def t_layer(l, j):
    return 6 + 4 * l + j


def build(nc, x, stream, small, const, fgain, out):
    es = ExitStack()
    with es:
        def sb(name, shape, dt=F32):
            return es.enter_context(nc.sbuf_tensor(name, shape, dt))

        def sem(name):
            return es.enter_context(nc.semaphore(name))

        raw = sb("raw", [P, RING, CH])
        wh = sb("w_high", [P, RING, CH], F32R)
        wl = sb("w_low", [P, RING, CH], F32R)
        h = sb("residual", [P, NT, D])
        tok = sb("tok", [P, NT, D])
        xh = sb("x_high", [P, KT, S], F32R)
        xl = sb("x_low", [P, KT, S], F32R)
        ch = sb("c_high", [P, 3, S], F32R)
        cl = sb("c_low", [P, 3, S], F32R)
        qT = sb("qT", [P, 8, S])
        kT = sb("kT", [P, 8, S])
        sT = sb("stick_qkT", [P, 4, S])
        v = sb("v", [P, NT, D])
        qk_tok = sb("qk_tok", [P, NT, 512])
        rope_a = sb("rope_a", [P, NT, 512])
        rope_b = sb("rope_b", [P, NT, 512])
        c_tok = sb("c_tok", [P, NT, 384])
        kr_tok = sb("kr_tok", [P, NT, 32])
        sm = sb("scores_masked", [P, 2, 384])
        pr = sb("probs", [P, 2, 384])
        prT = sb("probsT", [P, 2, 384])
        nmax = sb("neg_max", [P, 16, NT])
        den = sb("den", [P, 16, NT])
        rden = sb("rden", [P, 16, NT])
        zm, sw, sp = sm, pr, prT
        sd = sb("stick_d", [P, 2, 384])
        conv, gate = rope_a[:, :, 0:S], rope_a[:, :, S:2 * S]
        hid, dT = rope_b[:, :, 0:S], rope_b[:, :, S:2 * S]
        gh = sb("hid_high", [P, 2, 2, S], F32R)
        gl = sb("hid_low", [P, 2, 2, S], F32R)
        sml = sb("small_sb", [P, SMALL_N])
        con = sb("const_sb", [P, CONST_N])
        fg = sb("final_gain", [P, D])
        ssq = sb("ssq", [P, NT])
        rstd = sb("rstd", [P, NT])
        msq = sb("msq", [P, 16])
        cssq = sb("c_ssq", [P, 4])
        crs = sb("c_rstd", [P, 4])
        hss = sb("head_ssq", [P, 16])
        hrs = sb("head_rstd", [P, 16])
        gain_sub = sb("gain_sub", [P, 1])
        lamb = sb("lam", [P, 8])
        lamw = sb("lam_work", [P, HD])
        f_tok = sb("forget_tok", [P, NT, 8])
        spare_c, spare_s = (a[0:8, :, :].rearrange("p t d -> p (t d)") for a in (c_tok, sm))
        f_w = [s[:, i * S:(i + 1) * S] for s, i in ((spare_c, 1), (spare_c, 2), (spare_s, 0), (spare_s, 1),
                                                    (spare_c, 0), (spare_s, 2))]
        spare_q = qk_tok[:, :, :].rearrange("p t d -> p (t d)")
        rw = spare_q[:, 0:384].rearrange("p (j n) -> p j n", j=24)
        rl = spare_q[:, 384:384 + NT * (NG + NE)].rearrange("p (t n) -> p t n", t=NT)
        rbig = spare_q[:, 512:512 + NT * NE].rearrange("p (t n) -> p t n", t=NT)
        comb = sb("combine", [P, NT, NE])
        zero = sb("zero", [P, 512], F32R)

        B = [es.enter_context(nc.psum_tensor(f"bank{i}", [P, 512], F32)) for i in range(8)]

        x_in, const_in, small_in, fg_in, out_done = map(sem, ("x_in", "const_in", "small_in", "fg_in", "out_done"))
        chunk_in = [sem(f"chunk_in{i}") for i in range(RING)]
        w_high, w_low, chunk_used = map(sem, ("w_high_ready", "w_low_ready", "chunk_used"))
        ssq_ready, rstd_ready, tok_ready = map(sem, ("ssq_ready", "rstd_ready", "tok_ready"))
        pool_step = sem("pool_step")
        t_done, t_high, t_low = map(sem, ("t_done", "t_high_ready", "t_low_ready"))
        h_ready = sem("h_ready")
        dve_step, act_step = sem("dve_step"), sem("act_step")
        qk_tok_ready, qk_tr, qkT_ready, v_ready = map(sem, ("qk_tok_ready", "qk_transposed", "qkT_ready", "v_ready"))
        rope_ready = sem("rope_ready")
        f_done, f_tok_ready, f_trans, f_z, f_neg, f_ln, negc_ready = map(sem, (
            "forget_done", "forget_tok_ready", "forget_transposed", "forget_z_ready", "forget_neg_ready",
            "forget_ln_ready", "neg_c_ready"))
        s_done, nm_ready, p_ready, p_tr, pT_ready, pv_done, o_done = map(sem, (
            "scores_done", "neg_max_ready", "probs_ready", "probs_transposed", "probsT_ready", "pv_done", "o_done"))
        hss_ready, hrs_ready, lam_sum, lam_exp = map(sem, ("head_ssq_ready", "head_rstd_ready", "lam_sum", "lam_exp"))
        conv_init, conv_ready, silu_ready, hid_ready, g_high, g_low = map(sem, (
            "conv_init", "conv_ready", "silu_ready", "hid_ready", "hid_high_ready", "hid_low_ready"))
        m_silu, m_hid, m_tr, m_high, m_low = map(sem, (
            "expert_silu_ready", "expert_hid_ready", "expert_hid_transposed", "expert_high_ready", "expert_low_ready"))
        zero_ready = sem("zero_ready")
        c_ssq_ready, c_rstd_ready, c_tok_ready, mla_group, mla_q_copied = map(sem, (
            "c_ssq_ready", "c_rstd_ready", "c_tok_ready", "mla_group_done", "mla_q_copied"))
        z_done, na_ready, ln_ready, sp_ready, cum_done, d_ready, a_ready, spv_done, so_done = map(sem, (
            "stick_z_done", "stick_na_ready", "stick_ln_ready", "stick_sp_ready", "stick_cum_done",
            "stick_d_ready", "stick_a_ready", "stick_pv_done", "stick_o_done"))
        pool_d, pool_dT, pool_y = map(sem, ("pool_d_done", "pool_dT_ready", "pool_y_done"))
        r_done, r_sub, r_exp, r_dif, r_exp2, comb_ready = map(sem, (
            "router_done", "router_sub_ready", "router_exp_ready", "router_dif_ready", "router_exp2_ready", "combine_ready"))
        block = es.enter_context(nc.Block())

        def cs(name, a=0, b=None):
            lo, hi = CONST[name]
            return con[:, lo + a:hi if b is None else lo + b]

        def ps(name, a=0, b=None):
            lo, hi = SMALL[name]
            return sml[:, lo + a:hi if b is None else lo + b]

        ident = cs("ident")

        @block.sync
        def _(sync):
            sync.dma_start(h[:, :, :], x.rearrange("(t p) d -> p t d", p=P)).then_inc(x_in, 16)
            sync.dma_start(con[:, :], const).then_inc(const_in, 16)
            sync.dma_start(sml[:, :], small).then_inc(small_in, 16)
            for c in range(RING):
                sync.dma_start(raw[:, c, :], stream[c]).then_inc(chunk_in[c], 16)
            sync.dma_start(fg[:, :], fgain[0]).then_inc(fg_in, 16)

            def load(c, u):
                sync.wait_ge(w_low, c - RING + 1)
                sync.dma_start(raw[:, u, :], stream[bass.ds(c, 1)].squeeze(0) if not isinstance(c, int) else stream[c])\
                    .then_inc(chunk_in[u], 16)

            whole = NCHUNK // RING
            with sync.Fori(1, whole) as i:
                for u in range(RING):
                    load(i * RING + u, u)
            for c in range(whole * RING, NCHUNK):
                load(c, c % RING)

        @block.gpsimd
        def _(pool):
            step = [0]

            def link(ins):
                step[0] += 1
                ins.then_inc(pool_step, 1)
                pool.wait_ge(pool_step, step[0])

            def power(dst, src, n, scale, eps, ready):
                link(nc.gpsimd.tensor_scalar(msq[:, 0:n], src, scale, eps, ALU.mult, ALU.add))
                nc.gpsimd.tensor_tensor(dst, msq[:, 0:n], cs("minus_half", 0, n), ALU.pow).then_inc(ready, 1)

            pool.wait_ge(const_in, 16)
            norm = [0]

            def rms():
                pool.wait_ge(ssq_ready, 2 * norm[0] + 2)
                norm[0] += 1
                power(rstd[:, :], ssq[:, :], NT, 1.0 / D, EPS, rstd_ready)

            rms()
            rms()
            rms()
            pool.wait_ge(hss_ready, 1)
            power(hrs[:, :], hss[:, :], 16, 1.0 / P, SUB_EPS, hrs_ready)
            rms()
            rms()
            for l in range(LAYERS):
                rms()
                pool.wait_ge(c_ssq_ready, l + 1)
                link(nc.gpsimd.tensor_tensor(msq[:, 0:4], cssq[:, :], cs("inv_c"), ALU.mult))
                link(nc.gpsimd.tensor_scalar(msq[:, 4:8], msq[:, 0:4], 1.0, EPS, ALU.mult, ALU.add))
                nc.gpsimd.tensor_tensor(crs[:, :], msq[:, 4:8], cs("minus_half", 0, 4), ALU.pow).then_inc(c_rstd_ready, 1)
                rms()
            rms()

        @block.scalar
        def _(act):
            step = [0]
            norm = [0]

            def link(ins):
                step[0] += 1
                ins.then_inc(act_step, 1)
                act.wait_ge(act_step, step[0])

            def split(c, off=0):
                if isinstance(off, int) and c + RING * off >= NCHUNK:
                    return
                u = c % RING
                act.wait_ge(chunk_in[u], (off + c // RING) * 16 + 16)
                if c >= RING or not isinstance(off, int):
                    act.wait_ge(chunk_used, off * RING + (c - RING + 1))
                nc.scalar.activation(wh[:, u, :], raw[:, u, :], ACT.Copy).then_inc(w_high, 1)

            def rms(residual):
                for t in range(NT):
                    if residual:
                        act.wait_ge(h_ready, 2 * (residual - 1) + t + 1)
                    elif t == 0:
                        act.wait_ge(x_in, 16)
                    nc.scalar.activation(tok[:, t, :], h[:, t, :], ACT.Square,
                                         accum_out=ssq[:, t:t + 1]).then_inc(ssq_ready, 1)
                norm[0] += 1

            def high(q, dst, gain, free):
                act.wait_ge(chunk_used, free) if free else None
                nk = dst.shape[1]
                for b in range(T_BANKS[q]):
                    act.wait_ge(t_done, T_BASE[q] + b + 1)
                    for k in range(2 * b, min(2 * b + 2, nk)):
                        ins = nc.scalar.activation(dst[:, k, :], B[4 + b][:, (k % 2) * S:(k % 2) * S + S], ACT.Copy,
                                                   scale=gain(k))
                    ins.then_inc(t_high, 1)

            def one(k):
                return cs("ones", 0, 1)

            def qkT_copy(n, dst, tile, rows=P):
                for t in range(NT):
                    act.wait_ge(qk_tr, 2 * n + t + 1)
                    nc.scalar.activation(dst[0:rows, tile:tile + 4, t * P:(t + 1) * P],
                                         B[6 + t][0:rows, :].rearrange("p (a s) -> p a s", a=4), ACT.Copy)\
                        .then_inc(qkT_ready, 1)

            def copy_v(c, banks, at, src=None):
                act.wait_ge(chunk_used, c + 1)
                for t in range(NT):
                    nc.scalar.activation(v[:, t, at:at + 512], B[banks + t][:, :], ACT.Copy).then_inc(v_ready, 1)

            def softmaxes(first, n, scale):
                for a in range(n):
                    act.wait_ge(nm_ready, first + a + 1)
                    if a >= 2:
                        act.wait_ge(p_tr, first + a - 1)
                    for t, lo, hi in ((0, 0, 128), (1, 128, 384)):
                        ins = nc.scalar.activation(pr[:, a % 2, lo:hi], sm[:, a % 2, lo:hi], ACT.Exp,
                                                   bias=nmax[:, a, t:t + 1], scale=-1.0,
                                                   accum_out=den[:, a, t:t + 1])
                    ins.then_inc(p_ready, 1)

            def projections(c0, qk_first, attention):
                for g in range(6):
                    c = c0 + 2 * g
                    split(c + AHEAD)
                    if 1 <= g <= 4:
                        n = qk_first + g - 1
                        qkT_copy(n, (qT, kT)[(g - 1) % 2], 4 * ((g - 1) // 2))
                    split(c + 1 + AHEAD)
                    if g >= 4:
                        copy_v(c + 1, 2 * (g % 2), 512 * (g - 4))

            def plain(c0, n):
                for c in range(c0, c0 + n):
                    split(c + AHEAD)

            def glu(l):
                c0 = C_FFN[l]
                nc_b, nc_w = SMALL["conv_b"][0] + l * FT, SMALL["conv_w"][0] + l * 3 * FT

                def tile(f, fi, u, c, off, lookahead):
                    act.wait_ge(chunk_used, off * RING + (c + 1))
                    if not isinstance(f, int) or f >= 2 or l:
                        act.wait_ge(hid_ready, fi - 1)
                    wcol = sml[:, bass.ds(f + (nc_w + 2 * FT), 1)]
                    bcol = sml[:, bass.ds(f + nc_b, 1)]
                    nc.scalar.activation(conv[:, u, :], B[4 + u][:, 0:S], ACT.Identity, bias=bcol,
                                         scale=wcol).then_inc(conv_init, 1)
                    if lookahead is not None:
                        split(lookahead, off)
                    act.wait_ge(conv_ready, fi * 2 + 2)
                    nc.scalar.activation(gate[:, u, :], conv[:, u, :], ACT.Silu).then_inc(silu_ready, 1)

                def high_part(fi, u, buf, free):
                    act.wait_ge(hid_ready, fi + 1)
                    if free is not None:
                        act.wait_ge(chunk_used, free)
                    nc.scalar.activation(gh[:, buf, u, :], hid[:, u, :], ACT.Copy).then_inc(g_high, 1)

                f0 = l * FT
                plain(c0, 1)
                tile(0, f0, 0, c0, 0, c0 + 1 + AHEAD)
                high_part(f0, 0, 0, c0)
                tile(1, f0 + 1, 1, c0 + 1, 0, None)
                high_part(f0 + 1, 1, 0, c0)
                with act.Fori(0, (NFB - 1) // 2) as i:
                    for j in range(2):
                        c = c0 + 2 + 3 * j
                        for u in range(2):
                            fi = i * 4 + (f0 + 2 + 2 * j + u)
                            f = i * 4 + (2 + 2 * j + u)
                            if u == 0:
                                split(c + AHEAD, i * 2)
                            tile(f, fi, u, c + u, i * 2, c + 1 + AHEAD if u == 0 else None)
                            high_part(fi, u, (1 + j) % 2, i * 6 + (c - 3))
                        split(c + 2 + AHEAD, i * 2)
                plain(c0 + 3 * NFB - 1, 1)

            def moe(l):
                c0 = C_LAYER[l] + C_MOE
                e0 = l * NE

                def silus(e, c, off):
                    act.wait_ge(chunk_used, off * RING + (c + 1))
                    if not isinstance(e, int) or e > 0:
                        act.wait_ge(m_hid, e * 2)
                    for t in range(NT):
                        nc.scalar.activation(gate[:, t, :], B[4 + t][:, 0:DE], ACT.Silu).then_inc(m_silu, 1)

                def high_part(e):
                    act.wait_ge(m_tr, e + 1)
                    nc.scalar.activation(gh[:, 0, :, :], B[6][:, :].rearrange("p (k s) -> p k s", k=2), ACT.Copy)\
                        .then_inc(m_high, 1)

                def turn(i, c, off):
                    split(c + AHEAD, off)
                    high_part(i + e0)
                    split(c + 1 + AHEAD, off)
                    silus(i + (e0 + 1), c + 1, off)
                    split(c + 2 + AHEAD, off)

                plain(c0, 2)
                silus(e0, c0 + 1, 0)
                with act.Fori(0, NE - 2) as i:
                    turn(i, c0 + 2, i)
                turn(NE - 2, c0 + 2 + 3 * (NE - 2), 0)
                split(c0 + 3 * NE - 1 + AHEAD)
                high_part(e0 + NE - 1)

            split(0)
            split(1)
            rms(0)
            act.wait_ge(const_in, 16)
            act.wait_ge(small_in, 16)
            high(T_L0, xh, lambda k: ps("attn_g", k, k + 1), 0)

            split(AHEAD)
            act.wait_ge(f_trans, 1)
            nc.scalar.activation(f_w[0], B[4][0:8, 0:S], ACT.Identity,
                                 bias=sml[0:8, SMALL["b_f"][0]:SMALL["b_f"][1]]).then_inc(f_z, 1)
            act.wait_ge(f_neg, 1)
            link(nc.scalar.activation(f_w[2], f_w[1], ACT.Exp))
            nc.scalar.activation(f_w[3], f_w[2], ACT.Ln, bias=1.0).then_inc(f_ln, 1)

            projections(C_HYB, 0, 0)
            softmaxes(0, 16, 1.0)
            high(T_L0O, xh, one, C_HYB_OUT)
            plain(C_HYB_OUT, 4)
            rms(1)
            high(T_F0, xh, lambda k: ps("ffn_g", k, k + 1), C_FFN[0])
            glu(0)

            rms(2)
            high(T_L1, xh, lambda k: ps("attn_g", KT + k, KT + k + 1), C_DIFF)
            act.wait_ge(lam_sum, 1)
            nc.scalar.activation(lamb[:, 2:4], lamb[:, 0:2], ACT.Exp).then_inc(lam_exp, 1)
            projections(C_DIFF, 4, 0)
            softmaxes(16, 16, 1.0)
            high(T_L1O, xh, lambda k: gain_sub[:, 0:1], C_DIFF_OUT)
            plain(C_DIFF_OUT, 4)
            rms(3)
            high(T_F1, xh, lambda k: ps("ffn_g", KT + k, KT + k + 1), C_FFN[1])
            glu(1)
            rms(4)

            for l in range(LAYERS):
                c0 = C_LAYER[l]
                rms(5 + 2 * l)
                high(t_layer(l, 0), xh, lambda k: ps("norm1_g", l * KT + k, l * KT + k + 1), c0)
                plain(c0, 2)
                act.wait_ge(chunk_used, c0 + 2)
                for t in range(NT):
                    for j, (a, b) in enumerate(((0, 256), (256, 384))):
                        ins = nc.scalar.activation(c_tok[:, t, a:b], B[t][:, a:b], ACT.Square,
                                                   accum_out=cssq[:, 2 * t + j:2 * t + j + 1])
                ins.then_inc(c_ssq_ready, 1)
                plain(c0 + 2, 2)
                high(t_layer(l, 1), ch, lambda k: ps("c_g", l * 3 + k, l * 3 + k + 1), c0)
                n = 8 + 5 * l
                qkT_copy(n, sT, 0)
                plain(c0 + 4, 2)
                copy_v(c0 + 5, 0, 512)
                split(c0 + C_UQ + AHEAD)
                for g in range(2):
                    act.wait_ge(*((mla_group, 2 * l + 1) if g == 0 else (chunk_used, c0 + C_UQ + 1)))
                    act.wait_ge(qk_tr, 2 * (n + g) + 2)
                    for t in range(NT):
                        nc.scalar.activation(
                            qk_tok[:, t, 0:384].rearrange("p (a d) -> p a d", a=4)[:, :, 0:HD],
                            B[2 * g + t][:, 0:384].rearrange("p (a d) -> p a d", a=4)[:, :, 0:HD],
                            ACT.Copy).then_inc(mla_q_copied, 1)
                    qkT_copy(n + 1 + g, qT, 4 * g, MLA_QK)
                split(c0 + C_UKV + AHEAD)
                for g in range(2):
                    act.wait_ge(*((mla_group, 2 * l + 2) if g == 0 else (chunk_used, c0 + C_UKV + 1)))
                    act.wait_ge(qk_tr, 2 * (n + 2 + g) + 2)
                    for t in range(NT):
                        kv = B[2 * g + t][:, :].rearrange("p (a d) -> p a d", a=4)
                        nc.scalar.activation(v[:, t, 256 * g:256 * g + 256].rearrange("p (a d) -> p a d", a=4),
                                             kv[:, :, HD:2 * HD], ACT.Copy).then_inc(v_ready, 1)
                        nc.scalar.activation(
                            qk_tok[:, t, 0:384].rearrange("p (a d) -> p a d", a=4)[:, :, 0:HD],
                            kv[:, :, 0:HD], ACT.Copy).then_inc(mla_q_copied, 1)
                    qkT_copy(n + 3 + g, kT, 4 * g, MLA_QK)
                softmaxes(32 + 8 * l, 8, MLA_SCALE)
                for s in range(4):
                    k = 4 * l + s
                    act.wait_ge(na_ready, k + 1)
                    link(nc.scalar.activation(sw[:, s % 2, :], sw[:, s % 2, :], ACT.Exp))
                    nc.scalar.activation(sw[:, s % 2, :], sw[:, s % 2, :], ACT.Ln, bias=1.0).then_inc(ln_ready, 1)
                    act.wait_ge(d_ready, k + 1)
                    nc.scalar.activation(sd[:, s % 2, :], sd[:, s % 2, :], ACT.Exp).then_inc(a_ready, 1)
                act.wait_ge(pool_d, l + 1)
                nc.scalar.activation(dT[:, :, :], B[6][:, :].rearrange("p (a s) -> p a s", a=2), ACT.Copy)\
                    .then_inc(pool_dT, 1)
                high(t_layer(l, 2), xh, one, c0 + C_OUT2)
                plain(c0 + C_OUT2, 4)
                rms(6 + 2 * l)
                high(t_layer(l, 3), xh, lambda k: ps("norm2_g", l * KT + k, l * KT + k + 1), c0 + C_ROUTER)
                plain(c0 + C_ROUTER, 1)
                act.wait_ge(r_sub, l + 1)
                nc.scalar.activation(rw[:, 2, 0:8], rw[:, 1, 0:8], ACT.Exp).then_inc(r_exp, 1)
                act.wait_ge(r_dif, l + 1)
                nc.scalar.activation(rw[:, 13, 0:2], rw[:, 12, 0:2], ACT.Exp).then_inc(r_exp2, 1)
                moe(l)
            rms(9)

        @block.vector
        def _(dve):
            step = [0]
            tt, ts, stt = nc.vector.tensor_tensor, nc.vector.tensor_scalar, nc.vector.scalar_tensor_tensor

            def link(ins):
                step[0] += 1
                ins.then_inc(dve_step, 1)
                dve.wait_ge(dve_step, step[0])

            def split(c, off=0):
                if isinstance(off, int) and c + RING * off >= NCHUNK:
                    return
                u = c % RING
                dve.wait_ge(w_high, off * RING + (c + 1))
                tt(wl[:, u, :], raw[:, u, :], wh[:, u, :].bitcast(F32), ALU.subtract).then_inc(w_low, 1)

            def plain(c0, n):
                for c in range(c0, c0 + n):
                    split(c + AHEAD)

            def normed(n):
                dve.wait_ge(rstd_ready, n + 1)
                for t in range(NT):
                    ts(tok[:, t, :], h[:, t, :], rstd[:, t:t + 1], None, ALU.mult).then_inc(tok_ready, 1)

            def low(q, dst, hi, gain):
                nk = dst.shape[1]
                for b in range(T_BANKS[q]):
                    dve.wait_ge(t_high, T_BASE[q] + b + 1)
                    for k in range(2 * b, min(2 * b + 2, nk)):
                        ins = stt(dst[:, k, :], B[4 + b][:, (k % 2) * S:(k % 2) * S + S], gain(k),
                                  hi[:, k, :].bitcast(F32), ALU.mult, ALU.subtract)
                    ins.then_inc(t_low, 1)

            def one(k):
                return cs("ones", 0, 1)

            def rope(n, c, banks, cos, sin):
                dve.wait_ge(chunk_used, c + 1)
                for t in range(NT):
                    src = B[banks + t][:, :].rearrange("p (a d) -> p a d", a=8)
                    co = cs(cos, t * HD, (t + 1) * HD).unsqueeze(1).broadcast_to([P, 8, HD])
                    si = cs(sin, t * HD, (t + 1) * HD).unsqueeze(1).broadcast_to([P, 8, HD])
                    a = rope_a[:, t, :].rearrange("p (a d) -> p a d", a=8)
                    b = rope_b[:, t, :].rearrange("p (a d) -> p a d", a=8)
                    tt(a, src, co, ALU.mult)
                    tt(b[:, :, 0:32], src[:, :, 32:64], si[:, :, 0:32], ALU.mult)
                    link(tt(b[:, :, 32:64], src[:, :, 0:32], si[:, :, 32:64], ALU.mult))
                    if n:
                        dve.wait_ge(qk_tr, 2 * (n - 1) + t + 1)
                    tt(qk_tok[:, t, :], rope_a[:, t, :], rope_b[:, t, :], ALU.add).then_inc(qk_tok_ready, 1)

            def scaled(n, c, banks, parts):
                dve.wait_ge(chunk_used, c + 1)
                for t in range(NT):
                    dve.wait_ge(qk_tr, 2 * (n - 1) + t + 1)
                    for a, b, f in parts:
                        ins = ts(qk_tok[:, t, a:b], B[banks + t][:, a:b], f, None, ALU.mult)
                    ins.then_inc(qk_tok_ready, 1)

            def attention(first, n, masks, scale, dv, diff, last):
                def scores(a):
                    dve.wait_ge(s_done, first + a + 1)
                    if a >= 2:
                        dve.wait_ge(p_ready, first + a - 1)
                    for t, lo, hi in ((0, 0, 128), (1, 128, 384)):
                        ins = nc.vector.tensor_tensor_reduce(
                            sm[:, a % 2, lo:hi], B[a % 2][:, lo:hi], cs(masks(a), lo, hi), -scale, 3e38,
                            ALU.add, ALU.min, nmax[:, a, t:t + 1])
                    ins.then_inc(nm_ready, 1)

                def probs(a):
                    dve.wait_ge(p_tr, first + a + 1)
                    if a >= 2:
                        dve.wait_ge(pv_done, first + a - 1)
                    nc.vector.tensor_copy(prT[:, a % 2, :], B[2 + a % 2][:, 0:384]).then_inc(pT_ready, 1)

                def outputs(a):
                    link(nc.vector.reciprocal(rden[:, a, :], den[:, a, :]))
                    if diff and a % 2:
                        link(ts(rden[:, a, :], rden[:, a, :], lamb[:, 6:7], None, ALU.mult))
                    dve.wait_ge(pv_done, first + a + 1)
                    for t in range(NT):
                        z = B[4 + a % 2][:, t * dv:(t + 1) * dv]
                        col = (a // 2 if diff else a) * dv
                        o = tok[:, t, col:col + dv]
                        if diff and a % 2:
                            ins = stt(o, z, rden[:, a, t:t + 1], o, ALU.mult, ALU.add)
                        else:
                            ins = ts(o, z, rden[:, a, t:t + 1], None, ALU.mult)
                    ins.then_inc(o_done, 1)
                    dve.wait_ge(o_done, first + a + 1)

                scores(0)
                scores(1)
                probs(0)
                for a in range(n):
                    if a + 2 < n:
                        scores(a + 2)
                    if a + 1 < n:
                        probs(a + 1)
                    outputs(a)

            def residual(c_of_half):
                for half in range(2):
                    dve.wait_ge(chunk_used, c_of_half[half] + 1)
                    for t in range(NT):
                        cols = slice(half * 512, half * 512 + 512)
                        ins = tt(h[:, t, cols], h[:, t, cols], B[2 * half + t][:, :], ALU.add)
                        if half:
                            ins.then_inc(h_ready, 1)

            def glu(l):
                c0 = C_FFN[l]
                cw = SMALL["conv_w"][0] + l * 3 * FT

                def tile(f, fi, u, buf):
                    w0 = sml[:, bass.ds(f + cw, 1)]
                    w1 = sml[:, bass.ds(f + (cw + FT), 1)]
                    dve.wait_ge(conv_init, fi + 1)
                    stt(conv[:, u, 1:S], B[4 + u][:, 0:S - 1], w1, conv[:, u, 1:S], ALU.mult, ALU.add)\
                        .then_inc(conv_ready, 1)
                    dve.wait_ge(conv_ready, fi * 2 + 1)
                    stt(conv[:, u, 2:S], B[4 + u][:, 0:S - 2], w0, conv[:, u, 2:S], ALU.mult, ALU.add)\
                        .then_inc(conv_ready, 1)
                    dve.wait_ge(silu_ready, fi + 1)
                    tt(hid[:, u, :], gate[:, u, :], B[4 + u][:, S:2 * S], ALU.mult).then_inc(hid_ready, 1)
                    dve.wait_ge(g_high, fi + 1)
                    tt(gl[:, buf, u, :], hid[:, u, :], gh[:, buf, u, :].bitcast(F32), ALU.subtract).then_inc(g_low, 1)

                f0 = l * FT
                plain(c0, 1)
                split(c0 + 1 + AHEAD)
                tile(0, f0, 0, 0)
                tile(1, f0 + 1, 1, 0)
                with dve.Fori(0, (NFB - 1) // 2) as i:
                    for j in range(2):
                        c = c0 + 2 + 3 * j
                        split(c + AHEAD, i * 2)
                        split(c + 1 + AHEAD, i * 2)
                        for u in range(2):
                            tile(i * 4 + (2 + 2 * j + u), i * 4 + (f0 + 2 + 2 * j + u), u, (1 + j) % 2)
                        split(c + 2 + AHEAD, i * 2)
                plain(c0 + 3 * NFB - 1, 1)
                residual([c0 + 3 * NFB - 1] * 2)

            def route(l):
                A3 = lambda j, n: rw[:, j, 0:NT * n].rearrange("p (t e) -> p t e", t=NT)
                col = lambda j: rw[:, j, 0:NT]
                wide = lambda j, n: col(j).unsqueeze(2).broadcast_to([P, NT, n])
                io = lambda name, n: cs(name, 0, n).unsqueeze(1).broadcast_to([P, NT, n])

                def one_hot(src, best, eq, at, dst, n):
                    link(tt(A3(eq, n), src, wide(best, n), ALU.is_equal))
                    link(stt(A3(eq, n), A3(eq, n), -64.0, io("iota", n), ALU.mult, ALU.add))
                    link(nc.vector.tensor_reduce(col(at), A3(eq, n), AX.X, ALU.min))
                    link(tt(A3(dst, n), io("iota64", n), wide(at, n), ALU.is_equal))

                dve.wait_ge(r_done, l + 1)
                n = NG + NE
                for t in range(NT):
                    ins = tt(rl[:, t, :], B[7][:, t * n:(t + 1) * n], ps("router_b", l * n, l * n + n), ALU.add)
                link(ins)
                g_log = rl[:, :, 0:NG]
                link(nc.vector.tensor_reduce(col(0), g_log, AX.X, ALU.max))
                tt(A3(1, NG), g_log, wide(0, NG), ALU.subtract).then_inc(r_sub, 1)
                one_hot(g_log, 0, 3, 4, 5, NG)
                big = rbig[:, :, :].rearrange("p t (g e) -> p t g e", g=NG)
                link(tt(big, rl[:, :, NG:].rearrange("p t (g e) -> p t g e", g=NG),
                        A3(5, NG).unsqueeze(3).broadcast_to([P, NT, NG, EG]), ALU.mult))
                link(nc.vector.tensor_reduce(A3(6, EG), rbig[:, :, :].rearrange("p t (g e) -> p t e g", g=NG), AX.X, ALU.add))
                link(nc.vector.tensor_reduce(col(7), A3(6, EG), AX.X, ALU.max))
                one_hot(A3(6, EG), 7, 8, 9, 10, EG)
                link(stt(A3(11, EG), A3(10, EG), NEG, A3(6, EG), ALU.mult, ALU.add))
                link(nc.vector.tensor_reduce(col(14), A3(11, EG), AX.X, ALU.max))
                tt(col(12), col(14), col(7), ALU.subtract).then_inc(r_dif, 1)
                one_hot(A3(11, EG), 14, 15, 16, 17, EG)
                dve.wait_ge(r_exp, l + 1)
                link(nc.vector.tensor_reduce(col(18), A3(2, NG), AX.X, ALU.add))
                link(nc.vector.reciprocal(col(18), col(18)))
                dve.wait_ge(r_exp2, l + 1)
                link(ts(col(19), col(13), 1.0, None, ALU.add))
                link(nc.vector.reciprocal(col(19), col(19)))
                link(tt(col(20), col(19), col(18), ALU.mult))
                link(tt(col(21), col(20), col(13), ALU.mult))
                tt(A3(22, EG), A3(10, EG), wide(20, EG), ALU.mult)
                link(tt(A3(23, EG), A3(17, EG), wide(21, EG), ALU.mult))
                link(tt(A3(22, EG), A3(22, EG), A3(23, EG), ALU.add))
                link(tt(comb[:, :, :].rearrange("p t (g e) -> p t g e", g=NG),
                        A3(5, NG).unsqueeze(3).broadcast_to([P, NT, NG, EG]),
                        A3(22, EG).unsqueeze(2).broadcast_to([P, NT, NG, EG]), ALU.mult))

            def moe(l):
                c0 = C_LAYER[l] + C_MOE
                e0 = l * NE

                def hids(e, el):
                    for t in range(NT):
                        dve.wait_ge(m_silu, e * 2 + (t + 1))
                        stt(hid[:, t, :], gate[:, t, :], comb[:, t, bass.ds(el, 1)], B[4 + t][:, DE:2 * DE],
                            ALU.mult, ALU.mult).then_inc(m_hid, 1)

                def low_part(e):
                    dve.wait_ge(m_high, e + 1)
                    tt(gl[:, 0, :, :], B[6][:, :].rearrange("p (k s) -> p k s", k=2),
                       gh[:, 0, :, :].bitcast(F32), ALU.subtract).then_inc(m_low, 1)

                def turn(i, c, off):
                    split(c + AHEAD, off)
                    low_part(i + e0)
                    split(c + 1 + AHEAD, off)
                    hids(i + (e0 + 1), i + 1)
                    split(c + 2 + AHEAD, off)

                plain(c0, 2)
                hids(e0, 0)
                with dve.Fori(0, NE - 2) as i:
                    turn(i, c0 + 2, i)
                turn(NE - 2, c0 + 2 + 3 * (NE - 2), 0)
                split(c0 + 3 * NE - 1 + AHEAD)
                low_part(e0 + NE - 1)
                residual([c0 + 3 * NE - 1] * 2)

            def gained(n, ready):
                dve.wait_ge(rstd_ready, n + 1)
                dve.wait_ge(fg_in, 16 * ready)
                for t in range(NT):
                    stt(h[:, t, :], h[:, t, :], rstd[:, t:t + 1], fg[:, :], ALU.mult, ALU.mult).then_inc(h_ready, 1)

            nc.vector.memset(zero[:, :].bitcast(F32), 0.0).then_inc(zero_ready, 1)
            split(0)
            split(1)
            dve.wait_ge(const_in, 16)
            dve.wait_ge(small_in, 16)
            dve.wait_ge(x_in, 16)
            for j in range(2):
                lo = SMALL["lam"][0] + 2 * j * HD
                link(nc.vector.tensor_tensor_reduce(lamw[:, :], sml[:, lo:lo + HD], sml[:, lo + HD:lo + 2 * HD], 1.0, 0.0,
                                                    ALU.mult, ALU.add, lamb[:, j:j + 1]))
            ts(gain_sub[:, :], ps("subln"), 1.0 - LAM_INIT, None, ALU.mult).then_inc(lam_sum, 1)

            normed(0)
            low(T_L0, xl, xh, lambda k: ps("attn_g", k, k + 1))
            split(AHEAD)
            dve.wait_ge(f_done, 1)
            nc.vector.tensor_copy(f_tok[:, :, :], B[5][:, 0:16].rearrange("p (t e) -> p t e", t=NT)).then_inc(f_tok_ready, 1)
            dve.wait_ge(f_z, 1)
            stt(f_w[1], f_w[0], -1.0, f_w[0], ALU.mult, ALU.min).then_inc(f_neg, 1)
            link(ts(f_w[4], f_w[0], -1.0, 0.0, ALU.mult, ALU.max))
            dve.wait_ge(f_ln, 1)
            dve.wait_ge(f_neg, 1)
            link(tt(f_w[5], f_w[4], f_w[3], ALU.add))
            link(nc.vector.memset(f_w[2], 1.0))
            nc.vector.tensor_tensor_scan(f_w[4], f_w[2], f_w[5], 0.0, ALU.mult, ALU.add)\
                .then_inc(negc_ready, 1)

            def projections(c0, qk_first, kinds):
                for g in range(6):
                    c = c0 + 2 * g
                    plain(c, 2)
                    if g < 4:
                        kinds(g, qk_first + g, c + 1, 2 * (g % 2))

            def kinds0(g, n, c, banks):
                if g < 2:
                    rope(n, c, banks, *(("cos_q", "sin_q"), ("cos_k", "sin_k"))[g])
                else:
                    scaled(n, c, banks, [(0, 512, HD ** -0.5 if g == 2 else 1.0)])

            def kinds1(g, n, c, banks):
                rope(n, c, banks, *(("cos_q", "sin_q"), ("cos_k", "sin_k"))[g % 2])

            projections(C_HYB, 0, kinds0)
            attention(0, 16, lambda a: "dilated" if a < 8 else "causal", 1.0, HD, False, 0)
            nc.vector.engine_nop().then_inc(tok_ready, 2)
            low(T_L0O, xl, xh, one)
            plain(C_HYB_OUT, 4)
            residual([C_HYB_OUT + 1, C_HYB_OUT + 3])
            normed(1)
            low(T_F0, xl, xh, lambda k: ps("ffn_g", k, k + 1))
            glu(0)

            normed(2)
            low(T_L1, xl, xh, lambda k: ps("attn_g", KT + k, KT + k + 1))
            dve.wait_ge(lam_exp, 1)
            link(tt(lamb[:, 5:6], lamb[:, 3:4], lamb[:, 2:3], ALU.subtract))
            link(ts(lamb[:, 6:7], lamb[:, 5:6], -LAM_INIT, None, ALU.add))
            projections(C_DIFF, 4, kinds1)
            attention(16, 16, lambda a: "causal", 1.0, P, True, 0)
            for t in range(NT):
                sq = rope_a[:, :, :].rearrange("p a b -> p (a b)")
                link(tt(sq, tok[:, t, :], tok[:, t, :], ALU.mult))
                ins = nc.vector.tensor_reduce(hss[:, 8 * t:8 * t + 8], sq.rearrange("p (a d) -> p a d", a=8), AX.X, ALU.add)
                link(ins) if t == 0 else ins.then_inc(hss_ready, 1)
            dve.wait_ge(hrs_ready, 1)
            for t in range(NT):
                o = tok[:, t, :].rearrange("p (a d) -> p a d", a=8)
                tt(o, o, hrs[:, 8 * t:8 * t + 8].unsqueeze(2).broadcast_to([P, 8, P]), ALU.mult).then_inc(tok_ready, 1)
            low(T_L1O, xl, xh, lambda k: gain_sub[:, 0:1])
            plain(C_DIFF_OUT, 4)
            residual([C_DIFF_OUT + 1, C_DIFF_OUT + 3])
            normed(3)
            low(T_F1, xl, xh, lambda k: ps("ffn_g", KT + k, KT + k + 1))
            glu(1)
            gained(4, 1)

            for l in range(LAYERS):
                c0 = C_LAYER[l]
                n = 8 + 5 * l
                normed(5 + 2 * l)
                low(t_layer(l, 0), xl, xh, lambda k: ps("norm1_g", l * KT + k, l * KT + k + 1))
                plain(c0, 4)
                dve.wait_ge(c_rstd_ready, l + 1)
                for t in range(NT):
                    ts(c_tok[:, t, 0:256], B[t][:, 0:256], crs[:, 2 * t:2 * t + 1], None, ALU.mult)
                    ts(c_tok[:, t, 256:384], B[t][:, 256:384], crs[:, 2 * t + 1:2 * t + 2], None, ALU.mult)
                    kr = B[t][:, 384:416]
                    tt(rope_a[:, t, 0:32], kr, cs("cos_m", 32 * t, 32 * t + 32), ALU.mult)
                    tt(rope_b[:, t, 0:16], kr[:, 16:32], cs("sin_m", 32 * t, 32 * t + 16), ALU.mult)
                    link(tt(rope_b[:, t, 16:32], kr[:, 0:16], cs("sin_m", 32 * t + 16, 32 * t + 32), ALU.mult))
                    tt(kr_tok[:, t, :], rope_a[:, t, 0:32], rope_b[:, t, 0:32], ALU.add).then_inc(c_tok_ready, 1)
                scaled(n, c0 + 3, 2, [(0, 256, HD ** -0.5), (256, 512, 1.0)])
                low(t_layer(l, 1), cl, ch, lambda k: ps("c_g", l * 3 + k, l * 3 + k + 1))
                plain(c0 + 4, 3)
                for g in range(2):
                    dve.wait_ge(*((mla_group, 2 * l + 1) if g == 0 else (chunk_used, c0 + C_UQ + 1)))
                    for t in range(NT):
                        dve.wait_ge(mla_q_copied, 8 * l + 2 * g + t + 1)
                        src = B[2 * g + t][:, 0:384].rearrange("p (a d) -> p a d", a=4)
                        a = rope_a[:, t, 0:128].rearrange("p (a d) -> p a d", a=4)
                        b = rope_b[:, t, 0:128].rearrange("p (a d) -> p a d", a=4)
                        co = cs("cos_m", 32 * t, 32 * t + 32).unsqueeze(1).broadcast_to([P, 4, 32])
                        si = cs("sin_m", 32 * t, 32 * t + 32).unsqueeze(1).broadcast_to([P, 4, 32])
                        tt(a, src[:, :, 64:96], co, ALU.mult)
                        tt(b[:, :, 0:16], src[:, :, 80:96], si[:, :, 0:16], ALU.mult)
                        link(tt(b[:, :, 16:32], src[:, :, 64:80], si[:, :, 16:32], ALU.mult))
                        tt(qk_tok[:, t, 0:384].rearrange("p (a d) -> p a d", a=4)[:, :, 64:96], a, b, ALU.add)\
                            .then_inc(qk_tok_ready, 1)
                split(c0 + C_UKV + AHEAD)
                for g in range(2):
                    for t in range(NT):
                        dve.wait_ge(mla_q_copied, 8 * l + 4 + 2 * g + t + 1)
                        nc.vector.tensor_copy(qk_tok[:, t, 0:384].rearrange("p (a d) -> p a d", a=4)[:, :, 64:96],
                                              kr_tok[:, t, :].unsqueeze(1).broadcast_to([P, 4, 32]))\
                            .then_inc(qk_tok_ready, 1)
                attention(32 + 8 * l, 8, lambda a: "chunked", MLA_SCALE, HD, False, 0)
                for s in range(4):
                    k = 4 * l + s
                    b = s % 2
                    dve.wait_ge(z_done, k + 1)
                    link(tt(zm[:, b, :], B[b][:, 0:384], cs("strict"), ALU.add))
                    stt(sw[:, b, :], zm[:, b, :], -1.0, zm[:, b, :], ALU.mult, ALU.min).then_inc(na_ready, 1)
                    dve.wait_ge(ln_ready, k + 1)
                    stt(sp[:, b, :], zm[:, b, :], 0.0, sw[:, b, :], ALU.max, ALU.add).then_inc(sp_ready, 1)
                    dve.wait_ge(cum_done, k + 1)
                    tt(sd[:, b, :], zm[:, b, :], B[2 + b][:, 0:384], ALU.subtract).then_inc(d_ready, 1)
                    dve.wait_ge(spv_done, k + 1)
                    col = 512 + s * HD
                    nc.vector.tensor_copy(tok[:, :, col:col + HD], B[4 + b][:, 0:128].rearrange("p (t d) -> p t d", t=NT))\
                        .then_inc(so_done, 1)
                dve.wait_ge(pool_y, l + 1)
                for t in range(NT):
                    for r in range(2):
                        o, f = (w.rearrange("p (j r d) -> p j r d", j=2, r=2)[:, :, r, :]
                                for w in (tok[:, t, 768:1024], ps("pool_scale", l * 256, l * 256 + 256)))
                        ins = tt(o, B[5 if r else 7][:, t * P:(t + 1) * P].rearrange("p (j d) -> p j d", j=2), f, ALU.mult)
                    ins.then_inc(tok_ready, 1)
                low(t_layer(l, 2), xl, xh, one)
                plain(c0 + C_OUT2, 4)
                residual([c0 + C_OUT2 + 1, c0 + C_OUT2 + 3])
                normed(6 + 2 * l)
                low(t_layer(l, 3), xl, xh, lambda k: ps("norm2_g", l * KT + k, l * KT + k + 1))
                plain(c0 + C_ROUTER, 1)
                route(l)
                moe(l)
            gained(9, 2)

        @block.tensor
        def _(pe):
            mm = nc.tensor.matmul

            def product(o, ah, al, bh, bl, start, stop, **kw):
                mm(o, ah, bh, start=start, stop=False, **kw)
                mm(o, ah, bl, start=False, stop=False, **kw)
                return mm(o, al, bh, start=False, stop=stop, **kw)

            def group(c0, n, banks, width, kt=4, k_all=KT, a=(xh, xl), at=0, off=0):
                for j in range(n):
                    u = (c0 + j) % RING
                    pe.wait_ge(w_low, off * RING + (c0 + j + 1))
                    for t in range(NT):
                        for kk in range(kt):
                            k = j * kt + kk
                            ins = product(banks[t], a[0][:, k, t * P:(t + 1) * P], a[1][:, k, t * P:(t + 1) * P],
                                          wh[:, u, kk * width:(kk + 1) * width], wl[:, u, kk * width:(kk + 1) * width],
                                          k == 0, k == n * kt - 1)
                    ins.then_inc(chunk_used, 1)
                    yield j

            def run(steps):
                for _ in steps:
                    pass

            def transposes(q, src, need, nk=KT, sem=None):
                pe.wait_ge(tok_ready if sem is None else sem, need)
                for b in range(T_BANKS[q]):
                    for k in range(2 * b, min(2 * b + 2, nk)):
                        for t in range(NT):
                            at = (k % 2) * S + t * P
                            ins = nc.tensor.transpose(B[4 + b][:, at:at + P], src[:, t, k * P:(k + 1) * P], ident)
                    ins.then_inc(t_done, 1)

            def ready(q):
                pe.wait_ge(t_low, T_BASE[q + 1])

            def qk_transposes(n, width=P):
                for t in range(NT):
                    pe.wait_ge(qk_tok_ready, 2 * n + t + 1)
                    if n:
                        pe.wait_ge(qkT_ready, 2 * (n - 1) + t + 1)
                    for j in range(4):
                        ins = nc.tensor.transpose(B[6 + t][0:width, j * P:(j + 1) * P],
                                                  qk_tok[:, t, j * width:(j + 1) * width], ident)
                    ins.then_inc(qk_tr, 1)

            def projections(c0, n0):
                for g in range(6):
                    if g in (2, 3):
                        pe.wait_ge(qk_tok_ready, 2 * (n0 + g - 2) + 2)
                    if g in (4, 5):
                        pe.wait_ge(qk_tok_ready, 2 * (n0 + g - 2) + 2)
                    b = 2 * (g % 2)
                    for j in group(c0 + 2 * g, 2, [B[b][:, :], B[b + 1][:, :]], 512):
                        if j == 0 and 1 <= g <= 4:
                            qk_transposes(n0 + g - 1)

            def attention(first, n, operands, v_of, dv, forget=None):
                def scores(a):
                    if a >= 2:
                        pe.wait_ge(nm_ready, first + a - 1)
                    o = B[a % 2]
                    q, k = operands(a)
                    f = forget(a) if forget else None
                    for lo, hi, t in ((0, 128, 0), (128, 384, 1)):
                        ins = mm(o[:, lo:hi], q[:, t * P:(t + 1) * P], k[:, 0:hi - lo], start=True, stop=f is None)
                        if f is not None:
                            ins = mm(o[:, lo:hi], f, f_w[4][:, 0:hi - lo], start=False, stop=True)
                    ins.then_inc(s_done, 1)

                def turn(a):
                    pe.wait_ge(p_ready, first + a + 1)
                    if a >= 2:
                        pe.wait_ge(pT_ready, first + a - 1)
                    for j in range(3):
                        ins = nc.tensor.transpose(B[2 + a % 2][:, j * P:(j + 1) * P], pr[:, a % 2, j * P:(j + 1) * P], ident)
                    ins.then_inc(p_tr, 1)

                def values(a):
                    pe.wait_ge(pT_ready, first + a + 1)
                    if a >= 2:
                        pe.wait_ge(o_done, first + a - 1)
                    z = B[4 + a % 2]
                    pt = prT[:, a % 2, :]
                    mm(z[:, 0:dv], pt[:, 0:P], v_of(a, 0), start=True, stop=True)
                    mm(z[:, dv:2 * dv], pt[:, P:2 * P], v_of(a, 0), start=True, stop=False)
                    mm(z[:, dv:2 * dv], pt[:, 2 * P:3 * P], v_of(a, 1), start=False, stop=True).then_inc(pv_done, 1)

                scores(0)
                scores(1)
                turn(0)
                for a in range(n):
                    if a + 2 < n:
                        scores(a + 2)
                    if a + 1 < n:
                        turn(a + 1)
                    values(a)

            def out_projection(c0):
                for half in range(2):
                    run(group(c0 + 2 * half, 2, [B[2 * half][:, :], B[2 * half + 1][:, :]], 512))

            def clear():
                for i in range(4):
                    mm(B[i][:, :], zero[:, 0:P], zero[:, :], start=True, stop=False, skip_group_check=True)

            def down(c, off, buf, last):
                u = c % RING
                pe.wait_ge(w_low, off * RING + (c + 1))
                for half in range(2):
                    for t in range(NT):
                        for k in range(2):
                            lo = k * D + half * 512
                            ins = product(B[2 * half + t][:, :], gh[:, buf, k, t * P:(t + 1) * P],
                                          gl[:, buf, k, t * P:(t + 1) * P], wh[:, u, lo:lo + 512], wl[:, u, lo:lo + 512],
                                          False, last and k == 1, skip_group_check=True)
                ins.then_inc(chunk_used, 1)

            def glu(l):
                c0 = C_FFN[l]
                f0 = l * FT

                def up(fi, u, c, off):
                    if u is not None and (not isinstance(off, int) or c >= c0 + 2):
                        pe.wait_ge(hid_ready, fi - 1)
                    s = c % RING
                    pe.wait_ge(w_low, off * RING + (c + 1))
                    for g in range(2):
                        for k in range(KT):
                            lo = k * 2 * P + g * P
                            ins = product(B[4 + u][:, g * S:(g + 1) * S], wh[:, s, lo:lo + P], wl[:, s, lo:lo + P],
                                          xh[:, k, :], xl[:, k, :], k == 0, k == KT - 1)
                    ins.then_inc(chunk_used, 1)

                clear()
                up(f0, 0, c0, 0)
                up(f0 + 1, 1, c0 + 1, 0)
                with pe.Fori(0, (NFB - 1) // 2) as i:
                    for j in range(2):
                        c = c0 + 2 + 3 * j
                        for u in range(2):
                            up(i * 4 + (f0 + 2 + 2 * j + u), u, c + u, i * 2)
                        pe.wait_ge(g_low, i * 4 + (f0 + 2 * j + 2))
                        down(c + 2, i * 2, j, False)
                pe.wait_ge(g_low, f0 + FT)
                down(c0 + 3 * NFB - 1, 0, 0, True)

            def moe(l):
                c0 = C_LAYER[l] + C_MOE
                e0 = l * NE

                def up(e, c, off, between=None):
                    for j in range(2):
                        s = (c + j) % RING
                        pe.wait_ge(w_low, off * RING + (c + j + 1))
                        if j == 0 and e is not None:
                            pe.wait_ge(m_hid, e * 2)
                        for t in range(NT):
                            for kk in range(4):
                                k = 4 * j + kk
                                ins = product(B[4 + t][:, :], xh[:, k, t * P:(t + 1) * P], xl[:, k, t * P:(t + 1) * P],
                                              wh[:, s, kk * 512:(kk + 1) * 512], wl[:, s, kk * 512:(kk + 1) * 512],
                                              k == 0, k == KT - 1)
                        ins.then_inc(chunk_used, 1)
                        if j == 0 and between is not None:
                            between()

                def turn_hid(e):
                    pe.wait_ge(m_hid, e * 2 + 2)
                    for k in range(2):
                        for t in range(NT):
                            at = k * S + t * P
                            ins = nc.tensor.transpose(B[6][:, at:at + P], hid[:, t, k * P:(k + 1) * P], ident)
                    ins.then_inc(m_tr, 1)

                def turn(i, c, off):
                    up(i + (e0 + 1), c, off, lambda: turn_hid(i + e0))
                    pe.wait_ge(m_low, i + (e0 + 1))
                    down(c + 2, off, 0, False)

                clear()
                up(None, c0, 0)
                with pe.Fori(0, NE - 2) as i:
                    turn(i, c0 + 2, i)
                turn(NE - 2, c0 + 2 + 3 * (NE - 2), 0)
                turn_hid(e0 + NE - 1)
                pe.wait_ge(m_low, e0 + NE)
                down(c0 + 3 * NE - 1, 0, 0, True)

            pe.wait_ge(const_in, 16)
            pe.wait_ge(zero_ready, 1)
            toks = [0]

            def tokens_ready():
                toks[0] += 2
                return toks[0]

            transposes(T_L0, tok, tokens_ready())
            ready(T_L0)
            run(group(C_FB, 1, [B[5][:, 0:8], B[5][:, 8:16]], 8, kt=KT))
            mm(B[5][:, 16:24], zero[:, 0:P], zero[:, 0:8], start=True, stop=True).then_inc(f_done, 1)

            def forget_transposes():
                pe.wait_ge(f_tok_ready, 1)
                for t in range(NT):
                    ins = nc.tensor.transpose(B[4][0:8, t * P:(t + 1) * P], f_tok[:, t, :], ident)
                ins.then_inc(f_trans, 1)

            forget_transposes()
            projections(C_HYB, 0)

            def head_rows(a):
                r = (a % 2) * HD
                return qT[r:r + HD, a // 2, :], kT[r:r + HD, a // 2, :]

            pe.wait_ge(qkT_ready, 8)
            pe.wait_ge(negc_ready, 1)
            pe.wait_ge(v_ready, 4)
            attention(0, 16, head_rows, lambda a, t: v[:, t, a * HD:(a + 1) * HD], HD,
                      lambda a: con[0:8, CONST["sel"][0] + (a - 8) * P:CONST["sel"][0] + (a - 7) * P] if a >= 8 else None)
            transposes(T_L0O, tok, tokens_ready())
            ready(T_L0O)
            out_projection(C_HYB_OUT)
            transposes(T_F0, tok, tokens_ready())
            ready(T_F0)
            glu(0)

            transposes(T_L1, tok, tokens_ready())
            ready(T_L1)
            projections(C_DIFF, 4)
            pe.wait_ge(qkT_ready, 16)
            pe.wait_ge(v_ready, 8)
            attention(16, 16, head_rows, lambda a, t: v[:, t, (a // 2) * P:(a // 2 + 1) * P], P)
            transposes(T_L1O, tok, tokens_ready())
            ready(T_L1O)
            out_projection(C_DIFF_OUT)
            transposes(T_F1, tok, tokens_ready())
            ready(T_F1)
            glu(1)

            for l in range(LAYERS):
                c0 = C_LAYER[l]
                n = 8 + 5 * l
                vr = 8 + 6 * l
                transposes(t_layer(l, 0), tok, tokens_ready())
                ready(t_layer(l, 0))
                run(group(c0, 2, [B[0][:, 0:G0W], B[1][:, 0:G0W]], G0W))
                run(group(c0 + 2, 2, [B[2][:, :], B[3][:, :]], G1W))
                pe.wait_ge(c_tok_ready, 2 * l + 2)
                for j in group(c0 + 4, 2, [B[0][:, :], B[1][:, :]], G2W):
                    if j == 0:
                        transposes(t_layer(l, 1), c_tok, 2 * l + 2, 3, c_tok_ready)
                        qk_transposes(n)
                ready(t_layer(l, 1))
                u = (c0 + C_UQ) % RING
                pe.wait_ge(w_low, c0 + C_UQ + 1)
                pe.wait_ge(v_ready, vr + 2)
                pe.wait_ge(qk_tok_ready, 2 * n + 2)
                for g in range(2):
                    for t in range(NT):
                        for k in range(2):
                            lo = k * 768 + g * 384
                            ins = product(B[2 * g + t][:, 0:384], ch[:, k, t * P:(t + 1) * P], cl[:, k, t * P:(t + 1) * P],
                                          wh[:, u, lo:lo + 384], wl[:, u, lo:lo + 384], k == 0, k == 1)
                    ins.then_inc(chunk_used if g else mla_group, 1)
                qk_transposes(n + 1, MLA_QK)
                u = (c0 + C_UKV) % RING
                pe.wait_ge(w_low, c0 + C_UKV + 1)
                for g in range(2):
                    pe.wait_ge(qk_tok_ready, 2 * (n + 1 + g) + 2)
                    for t in range(NT):
                        lo = g * 512
                        ins = product(B[2 * g + t][:, :], ch[:, 2, t * P:(t + 1) * P], cl[:, 2, t * P:(t + 1) * P],
                                      wh[:, u, lo:lo + 512], wl[:, u, lo:lo + 512], True, True)
                    ins.then_inc(chunk_used if g else mla_group, 1)
                    if g == 0:
                        qk_transposes(n + 2, MLA_QK)
                qk_transposes(n + 3, MLA_QK)
                qk_transposes(n + 4, MLA_QK)
                pe.wait_ge(qkT_ready, 2 * (n + 5))
                pe.wait_ge(v_ready, vr + 6)
                attention(32 + 8 * l, 8, lambda a: (qT[0:MLA_QK, a, :], kT[0:MLA_QK, a, :]),
                          lambda a, t: v[:, t, a * HD:(a + 1) * HD], HD)
                for s in range(4):
                    i = 4 * l + s
                    b = s % 2
                    r = (s % 2) * HD
                    q, k = sT[r:r + HD, s // 2, :], sT[r:r + HD, 2 + s // 2, :]
                    mm(B[b][:, 0:S], k[:, 0:P], q, start=True, stop=True)
                    mm(B[b][:, S:384], k[:, P:S], q[:, P:S], start=True, stop=True).then_inc(z_done, 1)
                    pe.wait_ge(sp_ready, i + 1)
                    o = B[2 + b]
                    mm(o[:, 0:S], cs("upper"), sp[:, b, 0:S], start=True, stop=False, skip_group_check=True)
                    mm(o[:, P:S], cs("ones"), sp[:, b, S:384], start=False, stop=True, skip_group_check=True)
                    mm(o[:, S:384], cs("upper"), sp[:, b, S:384], start=True, stop=True, skip_group_check=True)\
                        .then_inc(cum_done, 1)
                    pe.wait_ge(a_ready, i + 1)
                    z = B[4 + b]
                    col = 512 + s * HD
                    mm(z[:, 0:HD], sd[:, b, 0:P], v[:, 0, col:col + HD], start=True, stop=True)
                    mm(z[:, HD:2 * HD], sd[:, b, P:S], v[:, 0, col:col + HD], start=True, stop=False)
                    mm(z[:, HD:2 * HD], sd[:, b, S:384], v[:, 1, col:col + HD], start=False, stop=True).then_inc(spv_done, 1)
                for g in range(4):
                    o = B[6][(g % 2) * HD:(g % 2 + 1) * HD, :]
                    at, col = (g // 2) * S, 768 + g * HD
                    mm(o[:, at:at + S], v[:, 0, col:col + HD], cs("pool", g * 384, g * 384 + S), start=True, stop=False,
                       skip_group_check=True)
                    ins = mm(o[:, at + P:at + S], v[:, 1, col:col + HD], cs("pool", g * 384 + S, (g + 1) * 384),
                             start=False, stop=True, skip_group_check=True)
                ins.then_inc(pool_d, 1)
                pe.wait_ge(pool_dT, l + 1)
                pe.wait_ge(so_done, 4 * l + 4)
                for g in range(4):
                    r = slice((g % 2) * HD, (g % 2 + 1) * HD)
                    lo = SMALL["pool_w"][0] + l * 2 * HD + (g // 2) * HD
                    for t in range(NT):
                        at = t * P + (g // 2) * HD
                        ins = mm(B[5 if g % 2 else 7][:, at:at + HD], dT[r, g // 2, t * P:(t + 1) * P],
                                 sml[r, lo:lo + HD], start=True, stop=True)
                ins.then_inc(pool_y, 1)
                transposes(t_layer(l, 2), tok, tokens_ready())
                ready(t_layer(l, 2))
                out_projection(c0 + C_OUT2)
                transposes(t_layer(l, 3), tok, tokens_ready())
                ready(t_layer(l, 3))
                w = NG + NE
                run(group(c0 + C_ROUTER, 1, [B[7][:, 0:w], B[7][:, w:2 * w]], w, kt=KT))
                mm(B[7][:, 100:108], zero[:, 0:P], zero[:, 0:8], start=True, stop=True).then_inc(r_done, 1)
                moe(l)

        @block.sync
        def _(sync):
            sync.wait_ge(h_ready, 10)
            sync.dma_start(fg[:, :], fgain[1]).then_inc(fg_in, 16)
            sync.wait_ge(h_ready, 20)
            sync.dma_start(out.rearrange("(t p) d -> p t d", p=P), h[:, :, :]).then_inc(out_done, 16)
            sync.wait_ge(out_done, 16)




def _constants():
    f = np.float32
    con = np.zeros((P, CONST_N), f)

    def put(name, a):
        lo, hi = CONST[name]
        con[0:a.shape[0], lo:hi] = a.reshape(a.shape[0], hi - lo)

    i = np.arange(P)
    put("ident", np.eye(P, dtype=f))
    put("upper", (i[:, None] >= i[None, :]).astype(f))
    put("ones", np.ones((P, P), f))
    t, s = np.arange(S)[:, None], np.arange(S)[None, :]
    lag = t - s

    def packed(m):
        return np.concatenate([m[0:P, 0:P], m[P:S, 0:S]], axis=1)

    count = sum(((lag >= 0) & (lag % d == 0) & (lag <= w)).astype(np.int64) for w, d in ((128, 1), (512, 4), (2048, 16)))
    put("dilated", packed(np.where(count > 0, np.log(np.maximum(count, 1)), NEG).astype(f)))
    put("causal", packed(np.where(lag >= 0, 0.0, NEG).astype(f)))
    put("chunked", packed(np.where(s // 64 <= t // 64, 0.0, NEG).astype(f)))
    strict = np.where(lag > 0, 0.0, NEG).astype(f).T
    put("strict", np.concatenate([strict[0:P, 0:S], strict[P:S, P:S]], axis=1))

    def tokens(a):
        return a.reshape(NT, P, -1).transpose(1, 0, 2)

    inv = (f(1.0) / (f(10000.0) ** (np.arange(0, HD, 2, dtype=f) / f(HD)))).astype(f)
    ang = np.arange(S, dtype=f)[:, None] * inv[None, :]
    cos, sin = np.cos(ang).astype(f), np.sin(ang).astype(f)
    cos, sin = np.concatenate([cos, cos], 1), np.concatenate([-sin, sin], 1)
    put("cos_q", tokens(cos * f(HD ** -0.5)))
    put("sin_q", tokens(sin * f(HD ** -0.5)))
    put("cos_k", tokens(cos))
    put("sin_k", tokens(sin))
    inv = (f(10000.0) ** (-np.arange(0, 32, 2, dtype=f) / f(32))).astype(f)
    ang = np.arange(S, dtype=f)[:, None] * inv[None, :]
    cos, sin = np.cos(ang).astype(f), np.sin(ang).astype(f)
    put("cos_m", tokens(np.concatenate([cos, cos], 1)))
    put("sin_m", tokens(np.concatenate([-sin, sin], 1)))
    pools = []
    for w in (2, 4, 8, 16):
        m = np.where((lag >= 0) & (lag < w), 1.0 / np.minimum(t + 1, w), 0.0) - np.eye(S)
        m = m.T.astype(f)
        pools.append(np.concatenate([m[0:P, 0:S], m[P:S, P:S]], axis=1))
    put("pool", np.stack(pools, axis=1))
    put("sel", np.repeat(np.eye(8, dtype=f), P, axis=1))
    put("iota", np.tile(np.arange(8, dtype=f), (P, 1)))
    put("iota64", np.tile(np.arange(8, dtype=f) - 64, (P, 1)))
    put("minus_half", np.full((P, 16), -0.5, f))
    put("inv_c", np.tile(np.array([1 / 256, 1 / 128] * 2, f), (P, 1)))
    return con


def _stream(a):
    out = np.zeros((NCHUNK, P, CH), np.float32)

    def tiles(w):
        return w.reshape(-1, P, w.shape[1]).transpose(1, 0, 2)

    def put(c, part):
        part = part.reshape(P, -1)
        out[c, :, 0:part.shape[1]] = part

    def columns(c, w, groups):
        for lo, hi in groups:
            k = tiles(w[:, lo:hi])
            put(c, k[:, 0:4])
            put(c + 1, k[:, 4:8])
            c += 2

    halves = [(0, 512), (512, 1024)]
    w = a["hyb_w_in"][0]
    put(C_FB, tiles(w[:, 3072:3080]))
    columns(C_HYB, w, [(lo, lo + 512) for lo in (0, 512, 1536, 2048, 1024, 2560)])
    columns(C_HYB_OUT, a["hyb_w_out"][0], halves)
    columns(C_DIFF, a["diff_w_qkv"][0], [(lo, lo + 512) for lo in (0, 1024, 512, 1536, 2048, 2560)])
    columns(C_DIFF_OUT, a["diff_w_out"][0], halves)

    def up_at(c0, j):
        return c0 if j == 0 else c0 + 3 * j - 1

    def down_at(c0, j, n):
        return c0 + 3 * j + 4 if j < n - 1 else c0 + 3 * n - 1

    for l in range(LAYERS):
        up, down = a["ffn_w_up"][l], a["ffn_w_down"][l]
        for j in range(NFB):
            for u in range(2):
                f = (2 * j + u) * P
                put(up_at(C_FFN[l], j) + u, np.stack([tiles(up[:, f:f + P]), tiles(up[:, DFF + f:DFF + f + P])], axis=2))
            put(down_at(C_FFN[l], j, NFB), tiles(down[2 * j * P:(2 * j + 2) * P]))
        c0 = C_LAYER[l]
        columns(c0 + C_IN2, a["w_in_2"][l], [(0, 416), (416, 928), (928, 1440)])
        put(c0 + C_UQ, tiles(a["w_uq_2"][l]))
        put(c0 + C_UKV, tiles(a["w_ukv_2"][l]))
        columns(c0 + C_OUT2, a["w_out_2"][l], halves)
        put(c0 + C_ROUTER, tiles(np.concatenate([a["w_group_2"][l], a["w_expert_2"][l]], axis=1)))
        for e in range(NE):
            gate, up, down = (a[k][l, e // EG, e % EG] for k in ("w_gate_2", "w_up_2", "w_down_2"))
            both = np.concatenate([tiles(gate), tiles(up)], axis=2)
            c = up_at(c0 + C_MOE, e)
            put(c, both[:, 0:4])
            put(c + 1, both[:, 4:8])
            put(down_at(c0 + C_MOE, e, NE), tiles(down))
    return out


def _small(a):
    small = np.zeros((P, SMALL_N), np.float32)

    def put(name, part):
        lo, hi = SMALL[name]
        small[0:part.shape[0], lo:hi] = part.reshape(part.shape[0], hi - lo)

    def columns(w):
        return w.reshape(-1, P).T

    def rows(w):
        return np.broadcast_to(w.reshape(1, -1), (P, w.size))

    put("attn_g", columns(a["attn_norm"]))
    put("ffn_g", columns(a["ffn_norm"]))
    put("norm1_g", columns(a["norm1_g_2"]))
    put("norm2_g", columns(a["norm2_g_2"]))
    put("c_g", columns(np.concatenate([a["q_norm_g_2"], a["kv_norm_g_2"]], axis=1)))
    put("subln", columns(a["diff_subln"]))
    put("conv_b", columns(a["ffn_conv_b"]))
    put("conv_w", columns(a["ffn_conv_w"]))
    put("b_f", a["hyb_b_f"].reshape(-1, 1))
    put("router_b", rows(np.concatenate([a["b_group_2"], a["b_expert_2"]], axis=1)))
    put("pool_scale", rows(a["pool_scale_2"]))
    put("lam", rows(a["diff_lambda"]))
    put("pool_w", a["pool_w_2"].reshape(2, 2, 2, HD, HD).transpose(2, 3, 0, 1, 4).reshape(P, -1))
    return small


def kernel(**inputs):
    import concourse.bacc as _bacc
    from concourse.bass_utils import run_bass_kernel_spmd as _run

    a = {k: np.asarray(v) for k, v in inputs.items()}
    gains = np.stack([np.broadcast_to(a[k].reshape(1, D), (P, D)) for k in ("final_norm", "final_g_2")])
    arrays = {
        "x": np.ascontiguousarray(a["x"].reshape(S, D)), "stream": _stream(a), "small": _small(a),
        "const": _constants(), "fgain": np.ascontiguousarray(gains),
    }
    nc = _bacc.Bacc("TRN2", target_bir_lowering=False, num_devices=1)
    args = [nc.dram_tensor(n, v.shape, F32, kind="ExternalInput").ap() for n, v in arrays.items()]
    args.append(nc.dram_tensor("out", (S, D), F32, kind="ExternalOutput").ap())
    build(nc, *args)
    r = _run(nc, [arrays], core_ids=[0])
    return r.results[0]["out"].reshape(1, S, D)
```

```python
import math

import numpy as np
import concourse.bass as bass
from concourse import mybir
from contextlib import ExitStack

F32 = mybir.dt.float32
F32R = mybir.dt.float32r
ALU = mybir.AluOpType
ACT = mybir.ActivationFunctionType
AX = mybir.AxisListType

P = 128
S = 256
NT = S // P
D = 1024
KT = D // P
HD = 64
DFF = 2816
FT = DFF // P
NFB = FT // 2
NE = 32
NG = 4
EG = NE // NG
DE = 256
LAYERS = 2
CH = 2048
RING = 3
AHEAD = 2
NEG = -1e30
EPS = 1e-6
SUB_EPS = 1e-5
LAM_INIT = 0.8 - 0.6 * math.exp(-0.3 * 1)
MLA_QK = 96
MLA_SCALE = float(MLA_QK) ** -0.5
G0W, G1W, G2W = 416, 512, 512

C_FB = 0
C_HYB = 1
C_HYB_OUT = C_HYB + 12
C_FFN = [C_HYB_OUT + 4, 0]
C_DIFF = C_FFN[0] + 3 * NFB
C_DIFF_OUT = C_DIFF + 12
C_FFN[1] = C_DIFF_OUT + 4
C_LAYER = [C_FFN[1] + 3 * NFB, 0]
C_IN2, C_UQ, C_UKV, C_OUT2, C_ROUTER, C_MOE = 0, 6, 7, 8, 12, 13
C_PER_LAYER = C_MOE + 3 * NE
C_LAYER[1] = C_LAYER[0] + C_PER_LAYER
NCHUNK = C_LAYER[1] + C_PER_LAYER



def _columns(fields):
    at, out = 0, {}
    for name, n in fields:
        out[name] = (at, at + n)
        at += n
    return out, at


SMALL, SMALL_N = _columns([
    ("attn_g", 2 * KT), ("ffn_g", 2 * KT), ("norm1_g", 2 * KT), ("norm2_g", 2 * KT), ("c_g", 2 * 3),
    ("subln", 1), ("conv_b", 2 * FT), ("conv_w", 2 * 3 * FT), ("b_f", 1), ("router_b", 2 * (NG + NE)),
    ("pool_scale", 2 * 256), ("lam", 4 * HD), ("pool_w", 2 * 2 * HD)])
CONST, CONST_N = _columns([
    ("ident", P), ("upper", P), ("ones", P), ("dilated", 384), ("causal", 384), ("chunked", 384),
    ("strict", 384), ("cos_q", NT * HD), ("sin_q", NT * HD), ("cos_k", NT * HD), ("sin_k", NT * HD),
    ("cos_m", NT * 32), ("sin_m", NT * 32), ("pool", 4 * 384), ("sel", 8 * P), ("iota", 8), ("iota64", 8),
    ("minus_half", 16), ("inv_c", 4),
    ("before", P), ("slot", P), ("chunk_of", 24)])

T_BANKS = [4, 4, 4, 4, 4, 4] + [4, 2, 4, 4] * LAYERS
T_BASE = [sum(T_BANKS[:q]) for q in range(len(T_BANKS) + 1)]
T_L0, T_L0O, T_F0, T_L1, T_L1O, T_F1 = range(6)


def t_layer(l, j):
    return 6 + 4 * l + j


def build(nc, x, stream, small, const, fgain, out):
    es = ExitStack()
    with es:
        def sb(name, shape, dt=F32):
            return es.enter_context(nc.sbuf_tensor(name, shape, dt))

        def sem(name):
            return es.enter_context(nc.semaphore(name))

        raw = sb("raw", [P, RING, CH])
        wh = sb("w_high", [P, RING, CH], F32R)
        wl = sb("w_low", [P, RING, CH], F32R)
        h = sb("residual", [P, NT, D])
        tok = sb("tok", [P, NT, D])
        xh = sb("x_high", [P, KT, S], F32R)
        xl = sb("x_low", [P, KT, S], F32R)
        ch = sb("c_high", [P, 3, S], F32R)
        cl = sb("c_low", [P, 3, S], F32R)
        qT = sb("qT", [P, 8, S])
        kT = sb("kT", [P, 8, S])
        sT = sb("stick_qkT", [P, 4, S])
        v = sb("v", [P, NT, D])
        qk_tok = sb("qk_tok", [P, NT, 512])
        rope_a = sb("rope_a", [P, NT, 512])
        rope_b = sb("rope_b", [P, NT, 512])
        c_tok = sb("c_tok", [P, NT, 384])
        kr_tok = sb("kr_tok", [P, NT, 32])
        sm = sb("scores_masked", [P, 2, 384])
        pr = sb("probs", [P, 2, 384])
        prT = sb("probsT", [P, 2, 384])
        nmax = sb("neg_max", [P, 16, NT])
        den = sb("den", [P, 16, NT])
        rden = sb("rden", [P, 16, NT])
        zm, sw, sp = sm, pr, prT
        sd = sb("stick_d", [P, 2, 384])
        conv, gate = rope_a[:, :, 0:S], rope_a[:, :, S:2 * S]
        hid, dT = rope_b[:, :, 0:S], rope_b[:, :, S:2 * S]
        gh = sb("hid_high", [P, 2, 2, S], F32R)
        gl = sb("hid_low", [P, 2, 2, S], F32R)
        sml = sb("small_sb", [P, SMALL_N])
        con = sb("const_sb", [P, CONST_N])
        fg = sb("final_gain", [P, D])
        ssq = sb("ssq", [P, NT])
        rstd = sb("rstd", [P, NT])
        msq = sb("msq", [P, 16])
        cssq = sb("c_ssq", [P, 4])
        crs = sb("c_rstd", [P, 4])
        hss = sb("head_ssq", [P, 16])
        hrs = sb("head_rstd", [P, 16])
        gain_sub = sb("gain_sub", [P, 1])
        lamb = sb("lam", [P, 8])
        lamw = sb("lam_work", [P, HD])
        f_tok = sb("forget_tok", [P, NT, 8])
        spare_c, spare_s = (a[0:8, :, :].rearrange("p t d -> p (t d)") for a in (c_tok, sm))
        f_w = [s[:, i * S:(i + 1) * S] for s, i in ((spare_c, 1), (spare_c, 2), (spare_s, 0), (spare_s, 1),
                                                    (spare_c, 0), (spare_s, 2))]
        spare_q = qk_tok[:, :, :].rearrange("p t d -> p (t d)")
        rw = spare_q[:, 0:384].rearrange("p (j n) -> p j n", j=24)
        rl = spare_q[:, 384:384 + NT * (NG + NE)].rearrange("p (t n) -> p t n", t=NT)
        rbig = spare_q[:, 512:512 + NT * NE].rearrange("p (t n) -> p t n", t=NT)
        comb = sb("combine", [P, NG, EG])
        spare_v = v[:, :, :].rearrange("p t d -> p (t d)")
        pick = spare_v[:, 0:NT * NG * P].rearrange("p (t g j) -> p t g j", t=NT, g=NG)
        spread = spare_v[:, NT * NG * P:].rearrange("p (g t) -> p g t", g=NG)
        ys = kT[:, 0:4, :].rearrange("p a s -> p (a s)")
        x_over, hid_over = qT[:, 0:4, :].rearrange("p a s -> p (a s)").rearrange("p (k j) -> p k j", k=KT), qT[:, 4, :]
        chunk_over = tok[:, :, :].rearrange("p t d -> p (t d)")
        route_f = sb("route_values", [P, 32])
        route_i = sb("route_integers", [P, 32], mybir.dt.int32)
        zero = sb("zero", [P, 512], F32R)

        B = [es.enter_context(nc.psum_tensor(f"bank{i}", [P, 512], F32)) for i in range(8)]

        x_in, const_in, small_in, fg_in, out_done = map(sem, ("x_in", "const_in", "small_in", "fg_in", "out_done"))
        chunk_in = [sem(f"chunk_in{i}") for i in range(RING)]
        w_high, w_low, chunk_used = map(sem, ("w_high_ready", "w_low_ready", "chunk_used"))
        ssq_ready, rstd_ready, tok_ready = map(sem, ("ssq_ready", "rstd_ready", "tok_ready"))
        pool_step = sem("pool_step")
        t_done, t_high, t_low = map(sem, ("t_done", "t_high_ready", "t_low_ready"))
        h_ready = sem("h_ready")
        dve_step, act_step = sem("dve_step"), sem("act_step")
        qk_tok_ready, qk_tr, qkT_ready, v_ready = map(sem, ("qk_tok_ready", "qk_transposed", "qkT_ready", "v_ready"))
        rope_ready = sem("rope_ready")
        f_done, f_tok_ready, f_trans, f_z, f_neg, f_ln, negc_ready = map(sem, (
            "forget_done", "forget_tok_ready", "forget_transposed", "forget_z_ready", "forget_neg_ready",
            "forget_ln_ready", "neg_c_ready"))
        s_done, nm_ready, p_ready, p_tr, pT_ready, pv_done, o_done = map(sem, (
            "scores_done", "neg_max_ready", "probs_ready", "probs_transposed", "probsT_ready", "pv_done", "o_done"))
        hss_ready, hrs_ready, lam_sum, lam_exp = map(sem, ("head_ssq_ready", "head_rstd_ready", "lam_sum", "lam_exp"))
        conv_init, conv_ready, silu_ready, hid_ready, g_high, g_low = map(sem, (
            "conv_init", "conv_ready", "silu_ready", "hid_ready", "hid_high_ready", "hid_low_ready"))
        m_silu, m_hid, m_tr, m_high, m_low = map(sem, (
            "expert_silu_ready", "expert_hid_ready", "expert_hid_transposed", "expert_high_ready", "expert_low_ready"))
        zero_ready = sem("zero_ready")
        goh_ready, place_done, pick_ready, spread_done, spread_ready, share_ready, comb_done, route_ready = map(sem, (
            "group_one_hot_ready", "places_done", "pick_ready", "spread_done", "spread_ready", "share_ready",
            "combine_done", "route_ready"))
        gx_done, gx_high, gx_low, ys_ready, sc_done, sc_read = map(sem, (
            "slots_gathered", "slots_high_ready", "slots_low_ready", "group_result_ready", "scatter_done", "scatter_added"))
        over_turn = [sem(f"overflow_turn{l}") for l in range(LAYERS)]
        over_in = [sem(f"overflow_chunk_in{l}") for l in range(LAYERS)]
        c_ssq_ready, c_rstd_ready, c_tok_ready, mla_group, mla_q_copied = map(sem, (
            "c_ssq_ready", "c_rstd_ready", "c_tok_ready", "mla_group_done", "mla_q_copied"))
        z_done, na_ready, ln_ready, sp_ready, cum_done, d_ready, a_ready, spv_done, so_done = map(sem, (
            "stick_z_done", "stick_na_ready", "stick_ln_ready", "stick_sp_ready", "stick_cum_done",
            "stick_d_ready", "stick_a_ready", "stick_pv_done", "stick_o_done"))
        pool_d, pool_dT, pool_y = map(sem, ("pool_d_done", "pool_dT_ready", "pool_y_done"))
        r_done, r_sub, r_exp, r_dif, r_exp2, comb_ready = map(sem, (
            "router_done", "router_sub_ready", "router_exp_ready", "router_dif_ready", "router_exp2_ready", "combine_ready"))
        block = es.enter_context(nc.Block())

        def cs(name, a=0, b=None):
            lo, hi = CONST[name]
            return con[:, lo + a:hi if b is None else lo + b]

        def ps(name, a=0, b=None):
            lo, hi = SMALL[name]
            return sml[:, lo + a:hi if b is None else lo + b]

        ident = cs("ident")

        @block.sync
        def _(sync):
            sync.dma_start(h[:, :, :], x.rearrange("(t p) d -> p t d", p=P)).then_inc(x_in, 16)
            sync.dma_start(con[:, :], const).then_inc(const_in, 16)
            sync.dma_start(sml[:, :], small).then_inc(small_in, 16)
            for c in range(RING):
                sync.dma_start(raw[:, c, :], stream[c]).then_inc(chunk_in[c], 16)
            sync.dma_start(fg[:, :], fgain[0]).then_inc(fg_in, 16)

            def load(c, u):
                sync.wait_ge(w_low, c - RING + 1)
                sync.dma_start(raw[:, u, :], stream[bass.ds(c, 1)].squeeze(0) if not isinstance(c, int) else stream[c])\
                    .then_inc(chunk_in[u], 16)

            whole = NCHUNK // RING
            with sync.Fori(1, whole) as i:
                for u in range(RING):
                    load(i * RING + u, u)
            for c in range(whole * RING, NCHUNK):
                load(c, c % RING)

        @block.gpsimd
        def _(pool):
            step = [0]

            def link(ins):
                step[0] += 1
                ins.then_inc(pool_step, 1)
                pool.wait_ge(pool_step, step[0])

            def power(dst, src, n, scale, eps, ready):
                link(nc.gpsimd.tensor_scalar(msq[:, 0:n], src, scale, eps, ALU.mult, ALU.add))
                nc.gpsimd.tensor_tensor(dst, msq[:, 0:n], cs("minus_half", 0, n), ALU.pow).then_inc(ready, 1)

            pool.wait_ge(const_in, 16)
            norm = [0]

            def rms():
                pool.wait_ge(ssq_ready, 2 * norm[0] + 2)
                norm[0] += 1
                power(rstd[:, :], ssq[:, :], NT, 1.0 / D, EPS, rstd_ready)

            rms()
            rms()
            rms()
            pool.wait_ge(hss_ready, 1)
            power(hrs[:, :], hss[:, :], 16, 1.0 / P, SUB_EPS, hrs_ready)
            rms()
            rms()
            for l in range(LAYERS):
                rms()
                pool.wait_ge(c_ssq_ready, l + 1)
                link(nc.gpsimd.tensor_tensor(msq[:, 0:4], cssq[:, :], cs("inv_c"), ALU.mult))
                link(nc.gpsimd.tensor_scalar(msq[:, 4:8], msq[:, 0:4], 1.0, EPS, ALU.mult, ALU.add))
                nc.gpsimd.tensor_tensor(crs[:, :], msq[:, 4:8], cs("minus_half", 0, 4), ALU.pow).then_inc(c_rstd_ready, 1)
                rms()
                pool.wait_ge(route_ready, l + 1)
                with pool.If(pool.value_load(route_i[0:1, 0:1], min_val=0, max_val=1)):
                    for e in range(EG):
                        for j in range(3):
                            pool.wait_ge(over_turn[l], 3 + 7 * e + (0, 1, 2)[j] if e or j else 3)
                            c = pool.value_load(route_i[0:1, 1 + j * EG + e:2 + j * EG + e], min_val=0, max_val=NCHUNK - 1)
                            pool.dma_start(chunk_over, stream[bass.ds(c, 1)].squeeze(0)).then_inc(over_in[l], 16)
            rms()

        @block.scalar
        def _(act):
            step = [0]
            norm = [0]

            def link(ins):
                step[0] += 1
                ins.then_inc(act_step, 1)
                act.wait_ge(act_step, step[0])

            def split(c, off=0):
                if isinstance(off, int) and c + RING * off >= NCHUNK:
                    return
                u = c % RING
                act.wait_ge(chunk_in[u], (off + c // RING) * 16 + 16)
                if c >= RING or not isinstance(off, int):
                    act.wait_ge(chunk_used, off * RING + (c - RING + 1))
                nc.scalar.activation(wh[:, u, :], raw[:, u, :], ACT.Copy).then_inc(w_high, 1)

            def rms(residual):
                for t in range(NT):
                    if residual:
                        act.wait_ge(h_ready, 2 * (residual - 1) + t + 1)
                    elif t == 0:
                        act.wait_ge(x_in, 16)
                    nc.scalar.activation(tok[:, t, :], h[:, t, :], ACT.Square,
                                         accum_out=ssq[:, t:t + 1]).then_inc(ssq_ready, 1)
                norm[0] += 1

            def high(q, dst, gain, free):
                act.wait_ge(chunk_used, free) if free else None
                nk = dst.shape[1]
                for b in range(T_BANKS[q]):
                    act.wait_ge(t_done, T_BASE[q] + b + 1)
                    for k in range(2 * b, min(2 * b + 2, nk)):
                        ins = nc.scalar.activation(dst[:, k, :], B[4 + b][:, (k % 2) * S:(k % 2) * S + S], ACT.Copy,
                                                   scale=gain(k))
                    ins.then_inc(t_high, 1)

            def one(k):
                return cs("ones", 0, 1)

            def qkT_copy(n, dst, tile, rows=P):
                for t in range(NT):
                    act.wait_ge(qk_tr, 2 * n + t + 1)
                    nc.scalar.activation(dst[0:rows, tile:tile + 4, t * P:(t + 1) * P],
                                         B[6 + t][0:rows, :].rearrange("p (a s) -> p a s", a=4), ACT.Copy)\
                        .then_inc(qkT_ready, 1)

            def copy_v(c, banks, at, src=None):
                act.wait_ge(chunk_used, c + 1)
                for t in range(NT):
                    nc.scalar.activation(v[:, t, at:at + 512], B[banks + t][:, :], ACT.Copy).then_inc(v_ready, 1)

            def softmaxes(first, n, scale):
                for a in range(n):
                    act.wait_ge(nm_ready, first + a + 1)
                    if a >= 2:
                        act.wait_ge(p_tr, first + a - 1)
                    for t, lo, hi in ((0, 0, 128), (1, 128, 384)):
                        ins = nc.scalar.activation(pr[:, a % 2, lo:hi], sm[:, a % 2, lo:hi], ACT.Exp,
                                                   bias=nmax[:, a, t:t + 1], scale=-1.0,
                                                   accum_out=den[:, a, t:t + 1])
                    ins.then_inc(p_ready, 1)

            def projections(c0, qk_first, attention):
                for g in range(6):
                    c = c0 + 2 * g
                    split(c + AHEAD)
                    if 1 <= g <= 4:
                        n = qk_first + g - 1
                        qkT_copy(n, (qT, kT)[(g - 1) % 2], 4 * ((g - 1) // 2))
                    split(c + 1 + AHEAD)
                    if g >= 4:
                        copy_v(c + 1, 2 * (g % 2), 512 * (g - 4))

            def plain(c0, n):
                for c in range(c0, c0 + n):
                    split(c + AHEAD)

            def glu(l):
                c0 = C_FFN[l]
                nc_b, nc_w = SMALL["conv_b"][0] + l * FT, SMALL["conv_w"][0] + l * 3 * FT

                def tile(f, fi, u, c, off, lookahead):
                    act.wait_ge(chunk_used, off * RING + (c + 1))
                    if not isinstance(f, int) or f >= 2 or l:
                        act.wait_ge(hid_ready, fi - 1)
                    wcol = sml[:, bass.ds(f + (nc_w + 2 * FT), 1)]
                    bcol = sml[:, bass.ds(f + nc_b, 1)]
                    nc.scalar.activation(conv[:, u, :], B[4 + u][:, 0:S], ACT.Identity, bias=bcol,
                                         scale=wcol).then_inc(conv_init, 1)
                    if lookahead is not None:
                        split(lookahead, off)
                    act.wait_ge(conv_ready, fi * 2 + 2)
                    nc.scalar.activation(gate[:, u, :], conv[:, u, :], ACT.Silu).then_inc(silu_ready, 1)

                def high_part(fi, u, buf, free):
                    act.wait_ge(hid_ready, fi + 1)
                    if free is not None:
                        act.wait_ge(chunk_used, free)
                    nc.scalar.activation(gh[:, buf, u, :], hid[:, u, :], ACT.Copy).then_inc(g_high, 1)

                f0 = l * FT
                plain(c0, 1)
                tile(0, f0, 0, c0, 0, c0 + 1 + AHEAD)
                high_part(f0, 0, 0, c0)
                tile(1, f0 + 1, 1, c0 + 1, 0, None)
                high_part(f0 + 1, 1, 0, c0)
                with act.Fori(0, (NFB - 1) // 2) as i:
                    for j in range(2):
                        c = c0 + 2 + 3 * j
                        for u in range(2):
                            fi = i * 4 + (f0 + 2 + 2 * j + u)
                            f = i * 4 + (2 + 2 * j + u)
                            if u == 0:
                                split(c + AHEAD, i * 2)
                            tile(f, fi, u, c + u, i * 2, c + 1 + AHEAD if u == 0 else None)
                            high_part(fi, u, (1 + j) % 2, i * 6 + (c - 3))
                        split(c + 2 + AHEAD, i * 2)
                plain(c0 + 3 * NFB - 1, 1)

            def moe(l):
                c0 = C_LAYER[l] + C_MOE
                e0, g0 = l * NE, l * NG

                def gathered(g):
                    for b in range(2):
                        act.wait_ge(gx_done, 2 * (g0 + g) + b + 1)
                        for k in range(4 * b, 4 * b + 4):
                            ins = nc.scalar.activation(xh[:, k, (g % 2) * P:(g % 2 + 1) * P],
                                                       B[2 + b][:, (k % 4) * P:(k % 4 + 1) * P], ACT.Copy,
                                                       scale=ps("norm2_g", l * KT + k, l * KT + k + 1))
                        ins.then_inc(gx_high, 1)

                def silu(e, c, off):
                    act.wait_ge(chunk_used, off * RING + (c + 1))
                    if not isinstance(e, int) or e > 0:
                        act.wait_ge(m_hid, e)
                    nc.scalar.activation(gate[:, 0, :], B[4][:, 0:DE], ACT.Silu).then_inc(m_silu, 1)

                def high_part(e):
                    act.wait_ge(m_tr, e + 1)
                    nc.scalar.activation(gh[:, 0, :, 0:P], B[6][:, 0:2 * P].rearrange("p (k s) -> p k s", k=2), ACT.Copy)\
                        .then_inc(m_high, 1)

                def turn(i, c, off):
                    split(c + AHEAD, off)
                    high_part(i + e0)
                    split(c + 1 + AHEAD, off)
                    silu(i + (e0 + 1), c + 1, off)
                    split(c + 2 + AHEAD, off)

                def result(g, c):
                    act.wait_ge(chunk_used, c + 1)
                    if g0 + g:
                        act.wait_ge(sc_done, 2 * (g0 + g))
                    for half in range(2):
                        ins = nc.scalar.activation(ys[:, half * 512:(half + 1) * 512], B[half][:, :], ACT.Copy)
                    ins.then_inc(ys_ready, 1)

                split(c0 + AHEAD)
                act.wait_ge(spread_done, l + 1)
                for b in range(2):
                    ins = nc.scalar.activation(spread[:, 2 * b:2 * b + 2, :], B[2 + b][:, :].rearrange("p (g t) -> p g t", g=2),
                                               ACT.Copy)
                ins.then_inc(spread_ready, 1)
                act.wait_ge(comb_done, l + 1)
                nc.scalar.activation(comb[:, :, :], B[7][:, 0:NE].rearrange("p (g e) -> p g e", g=NG), ACT.Copy)\
                    .then_inc(comb_ready, 1)
                gathered(0)
                split(c0 + 1 + AHEAD)
                silu(e0, c0 + 1, 0)
                gathered(1)
                for g in range(NG):
                    c = c0 + 2 + 3 * EG * g
                    end = l == LAYERS - 1 and g == NG - 1
                    with act.Fori(0, EG - 1 - end) as i:
                        turn(i + EG * g, c, i)
                    if end:
                        turn(EG * (g + 1) - 2, c + 3 * (EG - 2), 0)
                    c += 3 * (EG - 1)
                    if g < NG - 1:
                        turn(EG * (g + 1) - 1, c, 0)
                        result(g, c + 2)
                        if g + 2 < NG:
                            gathered(g + 2)
                split(c0 + 3 * NE - 1 + AHEAD)
                high_part(e0 + NE - 1)
                result(NG - 1, c0 + 3 * NE - 1)

                with act.If(act.value_load(route_i[0:1, 0:1], min_val=0, max_val=1)):
                    turn_is = over_turn[l]
                    act.wait_ge(turn_is, 2)
                    for k in range(KT):
                        nc.scalar.activation(x_over[:, k, :], B[2 + k // 4][:, (k % 4) * P:(k % 4 + 1) * P], ACT.Copy,
                                             scale=ps("norm2_g", l * KT + k, l * KT + k + 1))
                    nc.scalar.activation(spread[:, 0, :], B[6][:, 0:S], ACT.Copy)
                    nc.scalar.activation(comb[:, 0, :], B[7][:, 0:EG], ACT.Copy).then_inc(turn_is, 1)
                    with act.Fori(0, EG) as e:
                        act.wait_ge(turn_is, e * 7 + 5)
                        nc.scalar.activation(gate[:, 0, :], B[4][:, 0:DE], ACT.Silu).then_inc(turn_is, 1)
                        act.wait_ge(turn_is, e * 7 + 8)
                        nc.scalar.activation(hid_over, B[6][:, 0:2 * P], ACT.Copy).then_inc(turn_is, 1)
                    act.wait_ge(turn_is, 3 + 7 * EG)
                    for half in range(2):
                        ins = nc.scalar.activation(ys[:, half * 512:(half + 1) * 512], B[half][:, :], ACT.Copy)
                    ins.then_inc(turn_is, 1)

            split(0)
            split(1)
            rms(0)
            act.wait_ge(const_in, 16)
            act.wait_ge(small_in, 16)
            high(T_L0, xh, lambda k: ps("attn_g", k, k + 1), 0)

            split(AHEAD)
            act.wait_ge(f_trans, 1)
            nc.scalar.activation(f_w[0], B[4][0:8, 0:S], ACT.Identity,
                                 bias=sml[0:8, SMALL["b_f"][0]:SMALL["b_f"][1]]).then_inc(f_z, 1)
            act.wait_ge(f_neg, 1)
            link(nc.scalar.activation(f_w[2], f_w[1], ACT.Exp))
            nc.scalar.activation(f_w[3], f_w[2], ACT.Ln, bias=1.0).then_inc(f_ln, 1)

            projections(C_HYB, 0, 0)
            softmaxes(0, 16, 1.0)
            high(T_L0O, xh, one, C_HYB_OUT)
            plain(C_HYB_OUT, 4)
            rms(1)
            high(T_F0, xh, lambda k: ps("ffn_g", k, k + 1), C_FFN[0])
            glu(0)

            rms(2)
            high(T_L1, xh, lambda k: ps("attn_g", KT + k, KT + k + 1), C_DIFF)
            act.wait_ge(lam_sum, 1)
            nc.scalar.activation(lamb[:, 2:4], lamb[:, 0:2], ACT.Exp).then_inc(lam_exp, 1)
            projections(C_DIFF, 4, 0)
            softmaxes(16, 16, 1.0)
            high(T_L1O, xh, lambda k: gain_sub[:, 0:1], C_DIFF_OUT)
            plain(C_DIFF_OUT, 4)
            rms(3)
            high(T_F1, xh, lambda k: ps("ffn_g", KT + k, KT + k + 1), C_FFN[1])
            glu(1)
            rms(4)

            for l in range(LAYERS):
                c0 = C_LAYER[l]
                rms(5 + 2 * l)
                high(t_layer(l, 0), xh, lambda k: ps("norm1_g", l * KT + k, l * KT + k + 1), c0)
                plain(c0, 2)
                act.wait_ge(chunk_used, c0 + 2)
                for t in range(NT):
                    for j, (a, b) in enumerate(((0, 256), (256, 384))):
                        ins = nc.scalar.activation(c_tok[:, t, a:b], B[t][:, a:b], ACT.Square,
                                                   accum_out=cssq[:, 2 * t + j:2 * t + j + 1])
                ins.then_inc(c_ssq_ready, 1)
                plain(c0 + 2, 2)
                high(t_layer(l, 1), ch, lambda k: ps("c_g", l * 3 + k, l * 3 + k + 1), c0)
                n = 8 + 5 * l
                qkT_copy(n, sT, 0)
                plain(c0 + 4, 2)
                copy_v(c0 + 5, 0, 512)
                split(c0 + C_UQ + AHEAD)
                for g in range(2):
                    act.wait_ge(*((mla_group, 2 * l + 1) if g == 0 else (chunk_used, c0 + C_UQ + 1)))
                    act.wait_ge(qk_tr, 2 * (n + g) + 2)
                    for t in range(NT):
                        nc.scalar.activation(
                            qk_tok[:, t, 0:384].rearrange("p (a d) -> p a d", a=4)[:, :, 0:HD],
                            B[2 * g + t][:, 0:384].rearrange("p (a d) -> p a d", a=4)[:, :, 0:HD],
                            ACT.Copy).then_inc(mla_q_copied, 1)
                    qkT_copy(n + 1 + g, qT, 4 * g, MLA_QK)
                split(c0 + C_UKV + AHEAD)
                for g in range(2):
                    act.wait_ge(*((mla_group, 2 * l + 2) if g == 0 else (chunk_used, c0 + C_UKV + 1)))
                    act.wait_ge(qk_tr, 2 * (n + 2 + g) + 2)
                    for t in range(NT):
                        kv = B[2 * g + t][:, :].rearrange("p (a d) -> p a d", a=4)
                        nc.scalar.activation(v[:, t, 256 * g:256 * g + 256].rearrange("p (a d) -> p a d", a=4),
                                             kv[:, :, HD:2 * HD], ACT.Copy).then_inc(v_ready, 1)
                        nc.scalar.activation(
                            qk_tok[:, t, 0:384].rearrange("p (a d) -> p a d", a=4)[:, :, 0:HD],
                            kv[:, :, 0:HD], ACT.Copy).then_inc(mla_q_copied, 1)
                    qkT_copy(n + 3 + g, kT, 4 * g, MLA_QK)
                softmaxes(32 + 8 * l, 8, MLA_SCALE)
                for s in range(4):
                    k = 4 * l + s
                    act.wait_ge(na_ready, k + 1)
                    link(nc.scalar.activation(sw[:, s % 2, :], sw[:, s % 2, :], ACT.Exp))
                    nc.scalar.activation(sw[:, s % 2, :], sw[:, s % 2, :], ACT.Ln, bias=1.0).then_inc(ln_ready, 1)
                    act.wait_ge(d_ready, k + 1)
                    nc.scalar.activation(sd[:, s % 2, :], sd[:, s % 2, :], ACT.Exp).then_inc(a_ready, 1)
                act.wait_ge(pool_d, l + 1)
                nc.scalar.activation(dT[:, :, :], B[6][:, :].rearrange("p (a s) -> p a s", a=2), ACT.Copy)\
                    .then_inc(pool_dT, 1)
                high(t_layer(l, 2), xh, one, c0 + C_OUT2)
                plain(c0 + C_OUT2, 4)
                rms(6 + 2 * l)
                high(t_layer(l, 3), xh, lambda k: ps("norm2_g", l * KT + k, l * KT + k + 1), c0 + C_ROUTER)
                plain(c0 + C_ROUTER, 1)
                act.wait_ge(r_sub, l + 1)
                nc.scalar.activation(rw[:, 2, 0:8], rw[:, 1, 0:8], ACT.Exp).then_inc(r_exp, 1)
                act.wait_ge(r_dif, l + 1)
                nc.scalar.activation(rw[:, 13, 0:2], rw[:, 12, 0:2], ACT.Exp).then_inc(r_exp2, 1)
                moe(l)
            rms(9)

        @block.vector
        def _(dve):
            step = [0]
            tt, ts, stt = nc.vector.tensor_tensor, nc.vector.tensor_scalar, nc.vector.scalar_tensor_tensor

            def link(ins):
                step[0] += 1
                ins.then_inc(dve_step, 1)
                dve.wait_ge(dve_step, step[0])

            def split(c, off=0):
                if isinstance(off, int) and c + RING * off >= NCHUNK:
                    return
                u = c % RING
                dve.wait_ge(w_high, off * RING + (c + 1))
                tt(wl[:, u, :], raw[:, u, :], wh[:, u, :].bitcast(F32), ALU.subtract).then_inc(w_low, 1)

            def plain(c0, n):
                for c in range(c0, c0 + n):
                    split(c + AHEAD)

            def normed(n):
                dve.wait_ge(rstd_ready, n + 1)
                for t in range(NT):
                    ts(tok[:, t, :], h[:, t, :], rstd[:, t:t + 1], None, ALU.mult).then_inc(tok_ready, 1)

            def low(q, dst, hi, gain):
                nk = dst.shape[1]
                for b in range(T_BANKS[q]):
                    dve.wait_ge(t_high, T_BASE[q] + b + 1)
                    for k in range(2 * b, min(2 * b + 2, nk)):
                        ins = stt(dst[:, k, :], B[4 + b][:, (k % 2) * S:(k % 2) * S + S], gain(k),
                                  hi[:, k, :].bitcast(F32), ALU.mult, ALU.subtract)
                    ins.then_inc(t_low, 1)

            def one(k):
                return cs("ones", 0, 1)

            def rope(n, c, banks, cos, sin):
                dve.wait_ge(chunk_used, c + 1)
                for t in range(NT):
                    src = B[banks + t][:, :].rearrange("p (a d) -> p a d", a=8)
                    co = cs(cos, t * HD, (t + 1) * HD).unsqueeze(1).broadcast_to([P, 8, HD])
                    si = cs(sin, t * HD, (t + 1) * HD).unsqueeze(1).broadcast_to([P, 8, HD])
                    a = rope_a[:, t, :].rearrange("p (a d) -> p a d", a=8)
                    b = rope_b[:, t, :].rearrange("p (a d) -> p a d", a=8)
                    tt(a, src, co, ALU.mult)
                    tt(b[:, :, 0:32], src[:, :, 32:64], si[:, :, 0:32], ALU.mult)
                    link(tt(b[:, :, 32:64], src[:, :, 0:32], si[:, :, 32:64], ALU.mult))
                    if n:
                        dve.wait_ge(qk_tr, 2 * (n - 1) + t + 1)
                    tt(qk_tok[:, t, :], rope_a[:, t, :], rope_b[:, t, :], ALU.add).then_inc(qk_tok_ready, 1)

            def scaled(n, c, banks, parts):
                dve.wait_ge(chunk_used, c + 1)
                for t in range(NT):
                    dve.wait_ge(qk_tr, 2 * (n - 1) + t + 1)
                    for a, b, f in parts:
                        ins = ts(qk_tok[:, t, a:b], B[banks + t][:, a:b], f, None, ALU.mult)
                    ins.then_inc(qk_tok_ready, 1)

            def attention(first, n, masks, scale, dv, diff, last):
                def scores(a):
                    dve.wait_ge(s_done, first + a + 1)
                    if a >= 2:
                        dve.wait_ge(p_ready, first + a - 1)
                    for t, lo, hi in ((0, 0, 128), (1, 128, 384)):
                        ins = nc.vector.tensor_tensor_reduce(
                            sm[:, a % 2, lo:hi], B[a % 2][:, lo:hi], cs(masks(a), lo, hi), -scale, 3e38,
                            ALU.add, ALU.min, nmax[:, a, t:t + 1])
                    ins.then_inc(nm_ready, 1)

                def probs(a):
                    dve.wait_ge(p_tr, first + a + 1)
                    if a >= 2:
                        dve.wait_ge(pv_done, first + a - 1)
                    nc.vector.tensor_copy(prT[:, a % 2, :], B[2 + a % 2][:, 0:384]).then_inc(pT_ready, 1)

                def outputs(a):
                    link(nc.vector.reciprocal(rden[:, a, :], den[:, a, :]))
                    if diff and a % 2:
                        link(ts(rden[:, a, :], rden[:, a, :], lamb[:, 6:7], None, ALU.mult))
                    dve.wait_ge(pv_done, first + a + 1)
                    for t in range(NT):
                        z = B[4 + a % 2][:, t * dv:(t + 1) * dv]
                        col = (a // 2 if diff else a) * dv
                        o = tok[:, t, col:col + dv]
                        if diff and a % 2:
                            ins = stt(o, z, rden[:, a, t:t + 1], o, ALU.mult, ALU.add)
                        else:
                            ins = ts(o, z, rden[:, a, t:t + 1], None, ALU.mult)
                    ins.then_inc(o_done, 1)
                    dve.wait_ge(o_done, first + a + 1)

                scores(0)
                scores(1)
                probs(0)
                for a in range(n):
                    if a + 2 < n:
                        scores(a + 2)
                    if a + 1 < n:
                        probs(a + 1)
                    outputs(a)

            def residual(c_of_half):
                for half in range(2):
                    dve.wait_ge(chunk_used, c_of_half[half] + 1)
                    for t in range(NT):
                        cols = slice(half * 512, half * 512 + 512)
                        ins = tt(h[:, t, cols], h[:, t, cols], B[2 * half + t][:, :], ALU.add)
                        if half:
                            ins.then_inc(h_ready, 1)

            def glu(l):
                c0 = C_FFN[l]
                cw = SMALL["conv_w"][0] + l * 3 * FT

                def tile(f, fi, u, buf):
                    w0 = sml[:, bass.ds(f + cw, 1)]
                    w1 = sml[:, bass.ds(f + (cw + FT), 1)]
                    dve.wait_ge(conv_init, fi + 1)
                    stt(conv[:, u, 1:S], B[4 + u][:, 0:S - 1], w1, conv[:, u, 1:S], ALU.mult, ALU.add)\
                        .then_inc(conv_ready, 1)
                    dve.wait_ge(conv_ready, fi * 2 + 1)
                    stt(conv[:, u, 2:S], B[4 + u][:, 0:S - 2], w0, conv[:, u, 2:S], ALU.mult, ALU.add)\
                        .then_inc(conv_ready, 1)
                    dve.wait_ge(silu_ready, fi + 1)
                    tt(hid[:, u, :], gate[:, u, :], B[4 + u][:, S:2 * S], ALU.mult).then_inc(hid_ready, 1)
                    dve.wait_ge(g_high, fi + 1)
                    tt(gl[:, buf, u, :], hid[:, u, :], gh[:, buf, u, :].bitcast(F32), ALU.subtract).then_inc(g_low, 1)

                f0 = l * FT
                plain(c0, 1)
                split(c0 + 1 + AHEAD)
                tile(0, f0, 0, 0)
                tile(1, f0 + 1, 1, 0)
                with dve.Fori(0, (NFB - 1) // 2) as i:
                    for j in range(2):
                        c = c0 + 2 + 3 * j
                        split(c + AHEAD, i * 2)
                        split(c + 1 + AHEAD, i * 2)
                        for u in range(2):
                            tile(i * 4 + (2 + 2 * j + u), i * 4 + (f0 + 2 + 2 * j + u), u, (1 + j) % 2)
                        split(c + 2 + AHEAD, i * 2)
                plain(c0 + 3 * NFB - 1, 1)
                residual([c0 + 3 * NFB - 1] * 2)

            def route(l):
                A3 = lambda j, n: rw[:, j, 0:NT * n].rearrange("p (t e) -> p t e", t=NT)
                col = lambda j: rw[:, j, 0:NT]
                wide = lambda j, n: col(j).unsqueeze(2).broadcast_to([P, NT, n])
                io = lambda name, n: cs(name, 0, n).unsqueeze(1).broadcast_to([P, NT, n])

                def one_hot(src, best, eq, at, dst, n):
                    link(tt(A3(eq, n), src, wide(best, n), ALU.is_equal))
                    link(stt(A3(eq, n), A3(eq, n), -64.0, io("iota", n), ALU.mult, ALU.add))
                    link(nc.vector.tensor_reduce(col(at), A3(eq, n), AX.X, ALU.min))
                    return tt(A3(dst, n), io("iota64", n), wide(at, n), ALU.is_equal)

                dve.wait_ge(r_done, l + 1)
                n = NG + NE
                for t in range(NT):
                    ins = tt(rl[:, t, :], B[7][:, t * n:(t + 1) * n], ps("router_b", l * n, l * n + n), ALU.add)
                link(ins)
                g_log = rl[:, :, 0:NG]
                link(nc.vector.tensor_reduce(col(0), g_log, AX.X, ALU.max))
                one_hot(g_log, 0, 3, 4, 5, NG).then_inc(goh_ready, 1)
                tt(A3(1, NG), g_log, wide(0, NG), ALU.subtract).then_inc(r_sub, 1)
                dve.wait_ge(place_done, l + 1)
                dve.wait_ge(goh_ready, l + 1)
                at = B[7][:, 128:140]
                link(tt(A3(6, NG), at[:, 0:8].rearrange("p (t g) -> p t g", t=NT), A3(5, NG), ALU.mult))
                link(nc.vector.tensor_reduce(col(7), A3(6, NG), AX.X, ALU.add))
                for g in range(NG):
                    for t in range(NT):
                        ins = ts(pick[:, t, g, :], cs("slot"), rw[:, 7, t:t + 1], rw[:, 5, t * NG + g:t * NG + g + 1],
                                 ALU.is_equal, ALU.mult)
                ins.then_inc(pick_ready, 1)
                big = rbig[:, :, :].rearrange("p t (g e) -> p t g e", g=NG)
                link(tt(big, rl[:, :, NG:].rearrange("p t (g e) -> p t g e", g=NG),
                        A3(5, NG).unsqueeze(3).broadcast_to([P, NT, NG, EG]), ALU.mult))
                link(nc.vector.tensor_reduce(A3(8, EG), rbig[:, :, :].rearrange("p t (g e) -> p t e g", g=NG), AX.X, ALU.add))
                link(nc.vector.tensor_reduce(col(9), A3(8, EG), AX.X, ALU.max))
                link(one_hot(A3(8, EG), 9, 3, 4, 10, EG))
                link(stt(A3(11, EG), A3(10, EG), NEG, A3(8, EG), ALU.mult, ALU.add))
                link(nc.vector.tensor_reduce(col(14), A3(11, EG), AX.X, ALU.max))
                tt(col(12), col(14), col(9), ALU.subtract).then_inc(r_dif, 1)
                link(one_hot(A3(11, EG), 14, 15, 16, 17, EG))
                dve.wait_ge(r_exp, l + 1)
                link(nc.vector.tensor_reduce(col(18), A3(2, NG), AX.X, ALU.add))
                link(nc.vector.reciprocal(col(18), col(18)))
                dve.wait_ge(r_exp2, l + 1)
                link(ts(col(19), col(13), 1.0, None, ALU.add))
                link(nc.vector.reciprocal(col(19), col(19)))
                link(tt(col(20), col(19), col(18), ALU.mult))
                link(tt(col(21), col(20), col(13), ALU.mult))
                tt(A3(22, EG), A3(10, EG), wide(20, EG), ALU.mult)
                link(tt(A3(23, EG), A3(17, EG), wide(21, EG), ALU.mult))
                tt(A3(22, EG), A3(22, EG), A3(23, EG), ALU.add).then_inc(share_ready, 1)
                f = route_f
                link(ts(f[:, 28:32], at[:, 8:12], float(P), None, ALU.is_gt))
                nc.vector.tensor_reduce(f[:, 0:1], f[:, 28:32], AX.X, ALU.max)
                link(tt(f[:, 28:32], f[:, 28:32], cs("iota", 0, NG), ALU.mult))
                link(nc.vector.tensor_reduce(f[:, 25:26], f[:, 28:32], AX.X, ALU.add))
                link(ts(f[:, 25:26], f[:, 25:26], float(3 * EG), None, ALU.mult))
                link(ts(f[:, 1:25], cs("chunk_of"), f[:, 25:26], None, ALU.add))
                c0 = C_LAYER[l] + C_MOE
                ts(f[:, 1:9], f[:, 1:9], 0.0, float(c0), ALU.max, ALU.add)
                ts(f[:, 9:17], f[:, 9:17], 1.0, float(c0), ALU.max, ALU.add)
                link(ts(f[:, 17:25], f[:, 17:25], float(3 * NE - 1), float(c0), ALU.min, ALU.add))
                nc.vector.tensor_copy(route_i[:, 0:25], f[:, 0:25]).then_inc(route_ready, 1)

            def moe(l):
                c0 = C_LAYER[l] + C_MOE
                e0, g0 = l * NE, l * NG

                def gathered(g):
                    for b in range(2):
                        dve.wait_ge(gx_high, 2 * (g0 + g) + b + 1)
                        for k in range(4 * b, 4 * b + 4):
                            half = slice((g % 2) * P, (g % 2 + 1) * P)
                            ins = stt(xl[:, k, half], B[2 + b][:, (k % 4) * P:(k % 4 + 1) * P],
                                      ps("norm2_g", l * KT + k, l * KT + k + 1), xh[:, k, half].bitcast(F32),
                                      ALU.mult, ALU.subtract)
                        ins.then_inc(gx_low, 1)

                def hidden(e, weight):
                    dve.wait_ge(m_silu, e + 1)
                    stt(hid[:, 0, :], gate[:, 0, :], weight, B[4][:, DE:2 * DE], ALU.mult, ALU.mult).then_inc(m_hid, 1)

                def low_part(e):
                    dve.wait_ge(m_high, e + 1)
                    tt(gl[:, 0, :, 0:P], B[6][:, 0:2 * P].rearrange("p (k s) -> p k s", k=2),
                       gh[:, 0, :, 0:P].bitcast(F32), ALU.subtract).then_inc(m_low, 1)

                def turn(e, c, off, weight):
                    split(c + AHEAD, off)
                    low_part(e)
                    split(c + 1 + AHEAD, off)
                    hidden(e + 1, weight)
                    split(c + 2 + AHEAD, off)

                def add(g):
                    for half in range(2):
                        dve.wait_ge(sc_done, 2 * (g0 + g) + half + 1)
                        for t in range(NT):
                            cols = slice(half * 512, half * 512 + 512)
                            ins = tt(h[:, t, cols], h[:, t, cols], B[((5, 7), (2, 3))[half][t]][:, :], ALU.add)
                        ins.then_inc(sc_read, 1)
                        dve.wait_ge(sc_read, 2 * (g0 + g) + half + 1)

                split(c0 + AHEAD)
                gathered(0)
                split(c0 + 1 + AHEAD)
                dve.wait_ge(comb_ready, l + 1)
                hidden(e0, comb[:, 0, 0:1])
                gathered(1)
                for g in range(NG):
                    c = c0 + 2 + 3 * EG * g
                    end = l == LAYERS - 1 and g == NG - 1
                    with dve.Fori(0, EG - 1 - end) as i:
                        turn(i + (e0 + EG * g), c, i, comb[:, g, bass.ds(i + 1, 1)])
                    if end:
                        turn(e0 + NE - 2, c + 3 * (EG - 2), 0, comb[:, g, EG - 1:EG])
                    c += 3 * (EG - 1)
                    if g < NG - 1:
                        turn(e0 + EG * (g + 1) - 1, c, 0, comb[:, g + 1, 0:1])
                        if g + 2 < NG:
                            gathered(g + 2)
                        add(g)
                split(c0 + 3 * NE - 1 + AHEAD)
                low_part(e0 + NE - 1)
                add(NG - 1)

                with dve.If(dve.value_load(route_i[0:1, 0:1], min_val=0, max_val=1)):
                    turn_is = over_turn[l]
                    for t in range(NT):
                        ins = ts(pick[:, t, 0, :], cs("slot"), rw[:, 7, t:t + 1], -float(P), ALU.subtract, ALU.is_equal)
                    ins.then_inc(turn_is, 1)
                    with dve.Fori(0, EG) as e:
                        dve.wait_ge(turn_is, e * 7 + 6)
                        stt(hid[:, 0, :], gate[:, 0, :], comb[:, 0, bass.ds(e, 1)], B[4][:, DE:2 * DE], ALU.mult, ALU.mult)\
                            .then_inc(turn_is, 1)
                    dve.wait_ge(turn_is, 5 + 7 * EG)
                    for half in range(2):
                        for t in range(NT):
                            cols = slice(half * 512, half * 512 + 512)
                            ins = tt(h[:, t, cols], h[:, t, cols], B[((5, 7), (2, 3))[half][t]][:, :], ALU.add)
                    ins.then_inc(turn_is, 1)
                    dve.wait_ge(turn_is, 6 + 7 * EG)
                nc.vector.engine_nop().then_inc(h_ready, 2)

            def gained(n, ready):
                dve.wait_ge(rstd_ready, n + 1)
                dve.wait_ge(fg_in, 16 * ready)
                for t in range(NT):
                    stt(h[:, t, :], h[:, t, :], rstd[:, t:t + 1], fg[:, :], ALU.mult, ALU.mult).then_inc(h_ready, 1)

            nc.vector.memset(zero[:, :].bitcast(F32), 0.0).then_inc(zero_ready, 1)
            split(0)
            split(1)
            dve.wait_ge(const_in, 16)
            dve.wait_ge(small_in, 16)
            dve.wait_ge(x_in, 16)
            for j in range(2):
                lo = SMALL["lam"][0] + 2 * j * HD
                link(nc.vector.tensor_tensor_reduce(lamw[:, :], sml[:, lo:lo + HD], sml[:, lo + HD:lo + 2 * HD], 1.0, 0.0,
                                                    ALU.mult, ALU.add, lamb[:, j:j + 1]))
            ts(gain_sub[:, :], ps("subln"), 1.0 - LAM_INIT, None, ALU.mult).then_inc(lam_sum, 1)

            normed(0)
            low(T_L0, xl, xh, lambda k: ps("attn_g", k, k + 1))
            split(AHEAD)
            dve.wait_ge(f_done, 1)
            nc.vector.tensor_copy(f_tok[:, :, :], B[5][:, 0:16].rearrange("p (t e) -> p t e", t=NT)).then_inc(f_tok_ready, 1)
            dve.wait_ge(f_z, 1)
            stt(f_w[1], f_w[0], -1.0, f_w[0], ALU.mult, ALU.min).then_inc(f_neg, 1)
            link(ts(f_w[4], f_w[0], -1.0, 0.0, ALU.mult, ALU.max))
            dve.wait_ge(f_ln, 1)
            dve.wait_ge(f_neg, 1)
            link(tt(f_w[5], f_w[4], f_w[3], ALU.add))
            link(nc.vector.memset(f_w[2], 1.0))
            nc.vector.tensor_tensor_scan(f_w[4], f_w[2], f_w[5], 0.0, ALU.mult, ALU.add)\
                .then_inc(negc_ready, 1)

            def projections(c0, qk_first, kinds):
                for g in range(6):
                    c = c0 + 2 * g
                    plain(c, 2)
                    if g < 4:
                        kinds(g, qk_first + g, c + 1, 2 * (g % 2))

            def kinds0(g, n, c, banks):
                if g < 2:
                    rope(n, c, banks, *(("cos_q", "sin_q"), ("cos_k", "sin_k"))[g])
                else:
                    scaled(n, c, banks, [(0, 512, HD ** -0.5 if g == 2 else 1.0)])

            def kinds1(g, n, c, banks):
                rope(n, c, banks, *(("cos_q", "sin_q"), ("cos_k", "sin_k"))[g % 2])

            projections(C_HYB, 0, kinds0)
            attention(0, 16, lambda a: "dilated" if a < 8 else "causal", 1.0, HD, False, 0)
            nc.vector.engine_nop().then_inc(tok_ready, 2)
            low(T_L0O, xl, xh, one)
            plain(C_HYB_OUT, 4)
            residual([C_HYB_OUT + 1, C_HYB_OUT + 3])
            normed(1)
            low(T_F0, xl, xh, lambda k: ps("ffn_g", k, k + 1))
            glu(0)

            normed(2)
            low(T_L1, xl, xh, lambda k: ps("attn_g", KT + k, KT + k + 1))
            dve.wait_ge(lam_exp, 1)
            link(tt(lamb[:, 5:6], lamb[:, 3:4], lamb[:, 2:3], ALU.subtract))
            link(ts(lamb[:, 6:7], lamb[:, 5:6], -LAM_INIT, None, ALU.add))
            projections(C_DIFF, 4, kinds1)
            attention(16, 16, lambda a: "causal", 1.0, P, True, 0)
            for t in range(NT):
                sq = rope_a[:, :, :].rearrange("p a b -> p (a b)")
                link(tt(sq, tok[:, t, :], tok[:, t, :], ALU.mult))
                ins = nc.vector.tensor_reduce(hss[:, 8 * t:8 * t + 8], sq.rearrange("p (a d) -> p a d", a=8), AX.X, ALU.add)
                link(ins) if t == 0 else ins.then_inc(hss_ready, 1)
            dve.wait_ge(hrs_ready, 1)
            for t in range(NT):
                o = tok[:, t, :].rearrange("p (a d) -> p a d", a=8)
                tt(o, o, hrs[:, 8 * t:8 * t + 8].unsqueeze(2).broadcast_to([P, 8, P]), ALU.mult).then_inc(tok_ready, 1)
            low(T_L1O, xl, xh, lambda k: gain_sub[:, 0:1])
            plain(C_DIFF_OUT, 4)
            residual([C_DIFF_OUT + 1, C_DIFF_OUT + 3])
            normed(3)
            low(T_F1, xl, xh, lambda k: ps("ffn_g", KT + k, KT + k + 1))
            glu(1)
            gained(4, 1)

            for l in range(LAYERS):
                c0 = C_LAYER[l]
                n = 8 + 5 * l
                normed(5 + 2 * l)
                low(t_layer(l, 0), xl, xh, lambda k: ps("norm1_g", l * KT + k, l * KT + k + 1))
                plain(c0, 4)
                dve.wait_ge(c_rstd_ready, l + 1)
                for t in range(NT):
                    ts(c_tok[:, t, 0:256], B[t][:, 0:256], crs[:, 2 * t:2 * t + 1], None, ALU.mult)
                    ts(c_tok[:, t, 256:384], B[t][:, 256:384], crs[:, 2 * t + 1:2 * t + 2], None, ALU.mult)
                    kr = B[t][:, 384:416]
                    tt(rope_a[:, t, 0:32], kr, cs("cos_m", 32 * t, 32 * t + 32), ALU.mult)
                    tt(rope_b[:, t, 0:16], kr[:, 16:32], cs("sin_m", 32 * t, 32 * t + 16), ALU.mult)
                    link(tt(rope_b[:, t, 16:32], kr[:, 0:16], cs("sin_m", 32 * t + 16, 32 * t + 32), ALU.mult))
                    tt(kr_tok[:, t, :], rope_a[:, t, 0:32], rope_b[:, t, 0:32], ALU.add).then_inc(c_tok_ready, 1)
                scaled(n, c0 + 3, 2, [(0, 256, HD ** -0.5), (256, 512, 1.0)])
                low(t_layer(l, 1), cl, ch, lambda k: ps("c_g", l * 3 + k, l * 3 + k + 1))
                plain(c0 + 4, 3)
                for g in range(2):
                    dve.wait_ge(*((mla_group, 2 * l + 1) if g == 0 else (chunk_used, c0 + C_UQ + 1)))
                    for t in range(NT):
                        dve.wait_ge(mla_q_copied, 8 * l + 2 * g + t + 1)
                        src = B[2 * g + t][:, 0:384].rearrange("p (a d) -> p a d", a=4)
                        a = rope_a[:, t, 0:128].rearrange("p (a d) -> p a d", a=4)
                        b = rope_b[:, t, 0:128].rearrange("p (a d) -> p a d", a=4)
                        co = cs("cos_m", 32 * t, 32 * t + 32).unsqueeze(1).broadcast_to([P, 4, 32])
                        si = cs("sin_m", 32 * t, 32 * t + 32).unsqueeze(1).broadcast_to([P, 4, 32])
                        tt(a, src[:, :, 64:96], co, ALU.mult)
                        tt(b[:, :, 0:16], src[:, :, 80:96], si[:, :, 0:16], ALU.mult)
                        link(tt(b[:, :, 16:32], src[:, :, 64:80], si[:, :, 16:32], ALU.mult))
                        tt(qk_tok[:, t, 0:384].rearrange("p (a d) -> p a d", a=4)[:, :, 64:96], a, b, ALU.add)\
                            .then_inc(qk_tok_ready, 1)
                split(c0 + C_UKV + AHEAD)
                for g in range(2):
                    for t in range(NT):
                        dve.wait_ge(mla_q_copied, 8 * l + 4 + 2 * g + t + 1)
                        nc.vector.tensor_copy(qk_tok[:, t, 0:384].rearrange("p (a d) -> p a d", a=4)[:, :, 64:96],
                                              kr_tok[:, t, :].unsqueeze(1).broadcast_to([P, 4, 32]))\
                            .then_inc(qk_tok_ready, 1)
                attention(32 + 8 * l, 8, lambda a: "chunked", MLA_SCALE, HD, False, 0)
                for s in range(4):
                    k = 4 * l + s
                    b = s % 2
                    dve.wait_ge(z_done, k + 1)
                    link(tt(zm[:, b, :], B[b][:, 0:384], cs("strict"), ALU.add))
                    stt(sw[:, b, :], zm[:, b, :], -1.0, zm[:, b, :], ALU.mult, ALU.min).then_inc(na_ready, 1)
                    dve.wait_ge(ln_ready, k + 1)
                    stt(sp[:, b, :], zm[:, b, :], 0.0, sw[:, b, :], ALU.max, ALU.add).then_inc(sp_ready, 1)
                    dve.wait_ge(cum_done, k + 1)
                    tt(sd[:, b, :], zm[:, b, :], B[2 + b][:, 0:384], ALU.subtract).then_inc(d_ready, 1)
                    dve.wait_ge(spv_done, k + 1)
                    col = 512 + s * HD
                    nc.vector.tensor_copy(tok[:, :, col:col + HD], B[4 + b][:, 0:128].rearrange("p (t d) -> p t d", t=NT))\
                        .then_inc(so_done, 1)
                dve.wait_ge(pool_y, l + 1)
                for t in range(NT):
                    for r in range(2):
                        o, f = (w.rearrange("p (j r d) -> p j r d", j=2, r=2)[:, :, r, :]
                                for w in (tok[:, t, 768:1024], ps("pool_scale", l * 256, l * 256 + 256)))
                        ins = tt(o, B[5 if r else 7][:, t * P:(t + 1) * P].rearrange("p (j d) -> p j d", j=2), f, ALU.mult)
                    ins.then_inc(tok_ready, 1)
                low(t_layer(l, 2), xl, xh, one)
                plain(c0 + C_OUT2, 4)
                residual([c0 + C_OUT2 + 1, c0 + C_OUT2 + 3])
                normed(6 + 2 * l)
                low(t_layer(l, 3), xl, xh, lambda k: ps("norm2_g", l * KT + k, l * KT + k + 1))
                plain(c0 + C_ROUTER, 1)
                route(l)
                moe(l)
            gained(9, 2)

        @block.tensor
        def _(pe):
            mm = nc.tensor.matmul

            def product(o, ah, al, bh, bl, start, stop, **kw):
                mm(o, ah, bh, start=start, stop=False, **kw)
                mm(o, ah, bl, start=False, stop=False, **kw)
                return mm(o, al, bh, start=False, stop=stop, **kw)

            def group(c0, n, banks, width, kt=4, k_all=KT, a=(xh, xl), at=0, off=0):
                for j in range(n):
                    u = (c0 + j) % RING
                    pe.wait_ge(w_low, off * RING + (c0 + j + 1))
                    for t in range(NT):
                        for kk in range(kt):
                            k = j * kt + kk
                            ins = product(banks[t], a[0][:, k, t * P:(t + 1) * P], a[1][:, k, t * P:(t + 1) * P],
                                          wh[:, u, kk * width:(kk + 1) * width], wl[:, u, kk * width:(kk + 1) * width],
                                          k == 0, k == n * kt - 1)
                    ins.then_inc(chunk_used, 1)
                    yield j

            def run(steps):
                for _ in steps:
                    pass

            def transposes(q, src, need, nk=KT, sem=None):
                pe.wait_ge(tok_ready if sem is None else sem, need)
                for b in range(T_BANKS[q]):
                    for k in range(2 * b, min(2 * b + 2, nk)):
                        for t in range(NT):
                            at = (k % 2) * S + t * P
                            ins = nc.tensor.transpose(B[4 + b][:, at:at + P], src[:, t, k * P:(k + 1) * P], ident)
                    ins.then_inc(t_done, 1)

            def ready(q):
                pe.wait_ge(t_low, T_BASE[q + 1])

            def qk_transposes(n, width=P):
                for t in range(NT):
                    pe.wait_ge(qk_tok_ready, 2 * n + t + 1)
                    if n:
                        pe.wait_ge(qkT_ready, 2 * (n - 1) + t + 1)
                    for j in range(4):
                        ins = nc.tensor.transpose(B[6 + t][0:width, j * P:(j + 1) * P],
                                                  qk_tok[:, t, j * width:(j + 1) * width], ident)
                    ins.then_inc(qk_tr, 1)

            def projections(c0, n0):
                for g in range(6):
                    if g in (2, 3):
                        pe.wait_ge(qk_tok_ready, 2 * (n0 + g - 2) + 2)
                    if g in (4, 5):
                        pe.wait_ge(qk_tok_ready, 2 * (n0 + g - 2) + 2)
                    b = 2 * (g % 2)
                    for j in group(c0 + 2 * g, 2, [B[b][:, :], B[b + 1][:, :]], 512):
                        if j == 0 and 1 <= g <= 4:
                            qk_transposes(n0 + g - 1)

            def attention(first, n, operands, v_of, dv, forget=None):
                def scores(a):
                    if a >= 2:
                        pe.wait_ge(nm_ready, first + a - 1)
                    o = B[a % 2]
                    q, k = operands(a)
                    f = forget(a) if forget else None
                    for lo, hi, t in ((0, 128, 0), (128, 384, 1)):
                        ins = mm(o[:, lo:hi], q[:, t * P:(t + 1) * P], k[:, 0:hi - lo], start=True, stop=f is None)
                        if f is not None:
                            ins = mm(o[:, lo:hi], f, f_w[4][:, 0:hi - lo], start=False, stop=True)
                    ins.then_inc(s_done, 1)

                def turn(a):
                    pe.wait_ge(p_ready, first + a + 1)
                    if a >= 2:
                        pe.wait_ge(pT_ready, first + a - 1)
                    for j in range(3):
                        ins = nc.tensor.transpose(B[2 + a % 2][:, j * P:(j + 1) * P], pr[:, a % 2, j * P:(j + 1) * P], ident)
                    ins.then_inc(p_tr, 1)

                def values(a):
                    pe.wait_ge(pT_ready, first + a + 1)
                    if a >= 2:
                        pe.wait_ge(o_done, first + a - 1)
                    z = B[4 + a % 2]
                    pt = prT[:, a % 2, :]
                    mm(z[:, 0:dv], pt[:, 0:P], v_of(a, 0), start=True, stop=True)
                    mm(z[:, dv:2 * dv], pt[:, P:2 * P], v_of(a, 0), start=True, stop=False)
                    mm(z[:, dv:2 * dv], pt[:, 2 * P:3 * P], v_of(a, 1), start=False, stop=True).then_inc(pv_done, 1)

                scores(0)
                scores(1)
                turn(0)
                for a in range(n):
                    if a + 2 < n:
                        scores(a + 2)
                    if a + 1 < n:
                        turn(a + 1)
                    values(a)

            def out_projection(c0):
                for half in range(2):
                    run(group(c0 + 2 * half, 2, [B[2 * half][:, :], B[2 * half + 1][:, :]], 512))

            def clear():
                for i in range(4):
                    mm(B[i][:, :], zero[:, 0:P], zero[:, :], start=True, stop=False, skip_group_check=True)

            def down(c, off, buf, last):
                u = c % RING
                pe.wait_ge(w_low, off * RING + (c + 1))
                for half in range(2):
                    for t in range(NT):
                        for k in range(2):
                            lo = k * D + half * 512
                            ins = product(B[2 * half + t][:, :], gh[:, buf, k, t * P:(t + 1) * P],
                                          gl[:, buf, k, t * P:(t + 1) * P], wh[:, u, lo:lo + 512], wl[:, u, lo:lo + 512],
                                          False, last and k == 1, skip_group_check=True)
                ins.then_inc(chunk_used, 1)

            def glu(l):
                c0 = C_FFN[l]
                f0 = l * FT

                def up(fi, u, c, off):
                    if u is not None and (not isinstance(off, int) or c >= c0 + 2):
                        pe.wait_ge(hid_ready, fi - 1)
                    s = c % RING
                    pe.wait_ge(w_low, off * RING + (c + 1))
                    for g in range(2):
                        for k in range(KT):
                            lo = k * 2 * P + g * P
                            ins = product(B[4 + u][:, g * S:(g + 1) * S], wh[:, s, lo:lo + P], wl[:, s, lo:lo + P],
                                          xh[:, k, :], xl[:, k, :], k == 0, k == KT - 1)
                    ins.then_inc(chunk_used, 1)

                clear()
                up(f0, 0, c0, 0)
                up(f0 + 1, 1, c0 + 1, 0)
                with pe.Fori(0, (NFB - 1) // 2) as i:
                    for j in range(2):
                        c = c0 + 2 + 3 * j
                        for u in range(2):
                            up(i * 4 + (f0 + 2 + 2 * j + u), u, c + u, i * 2)
                        pe.wait_ge(g_low, i * 4 + (f0 + 2 * j + 2))
                        down(c + 2, i * 2, j, False)
                pe.wait_ge(g_low, f0 + FT)
                down(c0 + 3 * NFB - 1, 0, 0, True)

            def moe(l):
                c0 = C_LAYER[l] + C_MOE
                e0, g0 = l * NE, l * NG

                def gather(g):
                    if g >= 1:
                        pe.wait_ge(gx_low, 2 * (g0 + g))
                    for b in range(2):
                        for k in range(4 * b, 4 * b + 4):
                            for t in range(NT):
                                ins = mm(B[2 + b][:, (k % 4) * P:(k % 4 + 1) * P], tok[:, t, k * P:(k + 1) * P],
                                         pick[:, t, g, :], start=t == 0, stop=t == NT - 1)
                        ins.then_inc(gx_done, 1)

                def scatter(g):
                    pe.wait_ge(ys_ready, g0 + g + 1)
                    for half in range(2):
                        if half:
                            pe.wait_ge(gx_low, 2 * min(g0 + NG, g0 + g + 3))
                        for t in range(NT):
                            ins = mm(B[((5, 7), (2, 3))[half][t]][:, :], spread[:, g, t * P:(t + 1) * P],
                                     ys[:, half * 512:(half + 1) * 512], start=True, stop=True)
                        ins.then_inc(sc_done, 1)

                def clear_sums():
                    for half in range(2):
                        mm(B[half][:, :], zero[:, 0:P], zero[:, :], start=True, stop=False, skip_group_check=True)

                def up(e, c, off, g, between=None):
                    for j in range(2):
                        s = (c + j) % RING
                        pe.wait_ge(w_low, off * RING + (c + j + 1))
                        if j == 0 and e is not None:
                            pe.wait_ge(m_hid, e)
                        for kk in range(4):
                            k = 4 * j + kk
                            x_of = slice((g % 2) * P, (g % 2 + 1) * P)
                            ins = product(B[4][:, :], xh[:, k, x_of], xl[:, k, x_of],
                                          wh[:, s, kk * 512:(kk + 1) * 512], wl[:, s, kk * 512:(kk + 1) * 512],
                                          k == 0, k == KT - 1)
                        ins.then_inc(chunk_used, 1)
                        if j == 0 and between is not None:
                            between()

                def turn_hid(e):
                    pe.wait_ge(m_hid, e + 1)
                    for k in range(2):
                        ins = nc.tensor.transpose(B[6][:, k * P:(k + 1) * P], hid[:, 0, k * P:(k + 1) * P], ident)
                    ins.then_inc(m_tr, 1)

                def down_sums(e, c, off, last):
                    u = c % RING
                    pe.wait_ge(m_low, e + 1)
                    pe.wait_ge(w_low, off * RING + (c + 1))
                    for half in range(2):
                        for k in range(2):
                            lo = k * D + half * 512
                            ins = product(B[half][:, :], gh[:, 0, k, 0:P], gl[:, 0, k, 0:P], wh[:, u, lo:lo + 512],
                                          wl[:, u, lo:lo + 512], False, last and k == 1, skip_group_check=True)
                    ins.then_inc(chunk_used, 1)

                def turn(e, c, off, g, last):
                    up(e + 1, c, off, g, lambda: turn_hid(e))
                    down_sums(e, c + 2, off, last)

                pe.wait_ge(goh_ready, l + 1)
                hot = [rw[:, 5, t * NG:(t + 1) * NG] for t in range(NT)]
                o = B[7]
                mm(o[:, 128:132], cs("before"), hot[0], start=True, stop=True)
                mm(o[:, 132:136], cs("ones"), hot[0], start=True, stop=False)
                mm(o[:, 132:136], cs("before"), hot[1], start=False, stop=True)
                mm(o[:, 136:140], cs("ones"), hot[0], start=True, stop=False)
                mm(o[:, 136:140], cs("ones"), hot[1], start=False, stop=True).then_inc(place_done, 1)
                pe.wait_ge(pick_ready, l + 1)
                for g in range(NG):
                    for t in range(NT):
                        at = (g % 2) * S + t * P
                        ins = nc.tensor.transpose(B[2 + g // 2][:, at:at + P], pick[:, t, g, :], ident)
                ins.then_inc(spread_done, 1)
                pe.wait_ge(spread_ready, l + 1)
                gather(0)
                pe.wait_ge(share_ready, l + 1)
                pe.wait_ge(route_ready, l + 1)
                for g in range(NG):
                    for t in range(NT):
                        ins = mm(o[:, g * EG:(g + 1) * EG], pick[:, t, g, :], rw[:, 22, t * EG:(t + 1) * EG],
                                 start=t == 0, stop=t == NT - 1)
                ins.then_inc(comb_done, 1)
                pe.wait_ge(gx_low, 2 * g0 + 2)
                up(None, c0, 0, 0)
                gather(1)
                for g in range(NG):
                    c = c0 + 2 + 3 * EG * g
                    if g:
                        pe.wait_ge(ys_ready, g0 + g)
                    clear_sums()
                    if g:
                        scatter(g - 1)
                    with pe.Fori(0, EG - 1) as i:
                        turn(i + (e0 + EG * g), c, i, g, False)
                    c += 3 * (EG - 1)
                    if g < NG - 1:
                        pe.wait_ge(gx_low, 2 * (g0 + g + 2))
                        turn(e0 + EG * (g + 1) - 1, c, 0, g + 1, True)
                        if g + 2 < NG:
                            gather(g + 2)
                turn_hid(e0 + NE - 1)
                down_sums(e0 + NE - 1, c0 + 3 * NE - 1, 0, True)
                scatter(NG - 1)

                with pe.If(pe.value_load(route_i[0:1, 0:1], min_val=0, max_val=1)):
                    turn_is = over_turn[l]
                    pe.wait_ge(turn_is, 1)
                    clear_sums()
                    for k in range(KT):
                        for t in range(NT):
                            mm(B[2 + k // 4][:, (k % 4) * P:(k % 4 + 1) * P], tok[:, t, k * P:(k + 1) * P],
                               pick[:, t, 0, :], start=t == 0, stop=t == NT - 1)
                    for t in range(NT):
                        nc.tensor.transpose(B[6][:, t * P:(t + 1) * P], pick[:, t, 0, :], ident)
                    for t in range(NT):
                        ins = mm(B[7][:, 0:EG], pick[:, t, 0, :], rw[:, 22, t * EG:(t + 1) * EG], start=t == 0, stop=t == NT - 1)
                    ins.then_inc(turn_is, 1)
                    pe.wait_ge(turn_is, 3)
                    with pe.Fori(0, EG) as e:
                        for j in range(2):
                            pe.wait_ge(over_in[l], e * 48 + 16 * (j + 1))
                            for kk in range(4):
                                k = 4 * j + kk
                                ins = mm(B[4][:, :], x_over[:, k, :], chunk_over[:, kk * 512:(kk + 1) * 512],
                                         start=k == 0, stop=k == KT - 1)
                            ins.then_inc(turn_is, 1)
                        pe.wait_ge(turn_is, e * 7 + 7)
                        for k in range(2):
                            ins = nc.tensor.transpose(B[6][:, k * P:(k + 1) * P], hid[:, 0, k * P:(k + 1) * P], ident)
                        ins.then_inc(turn_is, 1)
                        pe.wait_ge(turn_is, e * 7 + 9)
                        pe.wait_ge(over_in[l], e * 48 + 48)
                        for half in range(2):
                            for k in range(2):
                                lo = k * D + half * 512
                                ins = mm(B[half][:, :], hid_over[:, k * P:(k + 1) * P], chunk_over[:, lo:lo + 512],
                                         start=False, stop=k == 1, skip_group_check=True)
                        ins.then_inc(turn_is, 1)
                    pe.wait_ge(turn_is, 4 + 7 * EG)
                    for half in range(2):
                        for t in range(NT):
                            ins = mm(B[((5, 7), (2, 3))[half][t]][:, :], spread[:, 0, t * P:(t + 1) * P],
                                     ys[:, half * 512:(half + 1) * 512], start=True, stop=True)
                    ins.then_inc(turn_is, 1)

            pe.wait_ge(const_in, 16)
            pe.wait_ge(zero_ready, 1)
            toks = [0]

            def tokens_ready():
                toks[0] += 2
                return toks[0]

            transposes(T_L0, tok, tokens_ready())
            ready(T_L0)
            run(group(C_FB, 1, [B[5][:, 0:8], B[5][:, 8:16]], 8, kt=KT))
            mm(B[5][:, 16:24], zero[:, 0:P], zero[:, 0:8], start=True, stop=True).then_inc(f_done, 1)

            def forget_transposes():
                pe.wait_ge(f_tok_ready, 1)
                for t in range(NT):
                    ins = nc.tensor.transpose(B[4][0:8, t * P:(t + 1) * P], f_tok[:, t, :], ident)
                ins.then_inc(f_trans, 1)

            forget_transposes()
            projections(C_HYB, 0)

            def head_rows(a):
                r = (a % 2) * HD
                return qT[r:r + HD, a // 2, :], kT[r:r + HD, a // 2, :]

            pe.wait_ge(qkT_ready, 8)
            pe.wait_ge(negc_ready, 1)
            pe.wait_ge(v_ready, 4)
            attention(0, 16, head_rows, lambda a, t: v[:, t, a * HD:(a + 1) * HD], HD,
                      lambda a: con[0:8, CONST["sel"][0] + (a - 8) * P:CONST["sel"][0] + (a - 7) * P] if a >= 8 else None)
            transposes(T_L0O, tok, tokens_ready())
            ready(T_L0O)
            out_projection(C_HYB_OUT)
            transposes(T_F0, tok, tokens_ready())
            ready(T_F0)
            glu(0)

            transposes(T_L1, tok, tokens_ready())
            ready(T_L1)
            projections(C_DIFF, 4)
            pe.wait_ge(qkT_ready, 16)
            pe.wait_ge(v_ready, 8)
            attention(16, 16, head_rows, lambda a, t: v[:, t, (a // 2) * P:(a // 2 + 1) * P], P)
            transposes(T_L1O, tok, tokens_ready())
            ready(T_L1O)
            out_projection(C_DIFF_OUT)
            transposes(T_F1, tok, tokens_ready())
            ready(T_F1)
            glu(1)

            for l in range(LAYERS):
                c0 = C_LAYER[l]
                n = 8 + 5 * l
                vr = 8 + 6 * l
                transposes(t_layer(l, 0), tok, tokens_ready())
                ready(t_layer(l, 0))
                run(group(c0, 2, [B[0][:, 0:G0W], B[1][:, 0:G0W]], G0W))
                run(group(c0 + 2, 2, [B[2][:, :], B[3][:, :]], G1W))
                pe.wait_ge(c_tok_ready, 2 * l + 2)
                for j in group(c0 + 4, 2, [B[0][:, :], B[1][:, :]], G2W):
                    if j == 0:
                        transposes(t_layer(l, 1), c_tok, 2 * l + 2, 3, c_tok_ready)
                        qk_transposes(n)
                ready(t_layer(l, 1))
                u = (c0 + C_UQ) % RING
                pe.wait_ge(w_low, c0 + C_UQ + 1)
                pe.wait_ge(v_ready, vr + 2)
                pe.wait_ge(qk_tok_ready, 2 * n + 2)
                for g in range(2):
                    for t in range(NT):
                        for k in range(2):
                            lo = k * 768 + g * 384
                            ins = product(B[2 * g + t][:, 0:384], ch[:, k, t * P:(t + 1) * P], cl[:, k, t * P:(t + 1) * P],
                                          wh[:, u, lo:lo + 384], wl[:, u, lo:lo + 384], k == 0, k == 1)
                    ins.then_inc(chunk_used if g else mla_group, 1)
                qk_transposes(n + 1, MLA_QK)
                u = (c0 + C_UKV) % RING
                pe.wait_ge(w_low, c0 + C_UKV + 1)
                for g in range(2):
                    pe.wait_ge(qk_tok_ready, 2 * (n + 1 + g) + 2)
                    for t in range(NT):
                        lo = g * 512
                        ins = product(B[2 * g + t][:, :], ch[:, 2, t * P:(t + 1) * P], cl[:, 2, t * P:(t + 1) * P],
                                      wh[:, u, lo:lo + 512], wl[:, u, lo:lo + 512], True, True)
                    ins.then_inc(chunk_used if g else mla_group, 1)
                    if g == 0:
                        qk_transposes(n + 2, MLA_QK)
                qk_transposes(n + 3, MLA_QK)
                qk_transposes(n + 4, MLA_QK)
                pe.wait_ge(qkT_ready, 2 * (n + 5))
                pe.wait_ge(v_ready, vr + 6)
                attention(32 + 8 * l, 8, lambda a: (qT[0:MLA_QK, a, :], kT[0:MLA_QK, a, :]),
                          lambda a, t: v[:, t, a * HD:(a + 1) * HD], HD)
                for s in range(4):
                    i = 4 * l + s
                    b = s % 2
                    r = (s % 2) * HD
                    q, k = sT[r:r + HD, s // 2, :], sT[r:r + HD, 2 + s // 2, :]
                    mm(B[b][:, 0:S], k[:, 0:P], q, start=True, stop=True)
                    mm(B[b][:, S:384], k[:, P:S], q[:, P:S], start=True, stop=True).then_inc(z_done, 1)
                    pe.wait_ge(sp_ready, i + 1)
                    o = B[2 + b]
                    mm(o[:, 0:S], cs("upper"), sp[:, b, 0:S], start=True, stop=False, skip_group_check=True)
                    mm(o[:, P:S], cs("ones"), sp[:, b, S:384], start=False, stop=True, skip_group_check=True)
                    mm(o[:, S:384], cs("upper"), sp[:, b, S:384], start=True, stop=True, skip_group_check=True)\
                        .then_inc(cum_done, 1)
                    pe.wait_ge(a_ready, i + 1)
                    z = B[4 + b]
                    col = 512 + s * HD
                    mm(z[:, 0:HD], sd[:, b, 0:P], v[:, 0, col:col + HD], start=True, stop=True)
                    mm(z[:, HD:2 * HD], sd[:, b, P:S], v[:, 0, col:col + HD], start=True, stop=False)
                    mm(z[:, HD:2 * HD], sd[:, b, S:384], v[:, 1, col:col + HD], start=False, stop=True).then_inc(spv_done, 1)
                for g in range(4):
                    o = B[6][(g % 2) * HD:(g % 2 + 1) * HD, :]
                    at, col = (g // 2) * S, 768 + g * HD
                    mm(o[:, at:at + S], v[:, 0, col:col + HD], cs("pool", g * 384, g * 384 + S), start=True, stop=False,
                       skip_group_check=True)
                    ins = mm(o[:, at + P:at + S], v[:, 1, col:col + HD], cs("pool", g * 384 + S, (g + 1) * 384),
                             start=False, stop=True, skip_group_check=True)
                ins.then_inc(pool_d, 1)
                pe.wait_ge(pool_dT, l + 1)
                pe.wait_ge(so_done, 4 * l + 4)
                for g in range(4):
                    r = slice((g % 2) * HD, (g % 2 + 1) * HD)
                    lo = SMALL["pool_w"][0] + l * 2 * HD + (g // 2) * HD
                    for t in range(NT):
                        at = t * P + (g // 2) * HD
                        ins = mm(B[5 if g % 2 else 7][:, at:at + HD], dT[r, g // 2, t * P:(t + 1) * P],
                                 sml[r, lo:lo + HD], start=True, stop=True)
                ins.then_inc(pool_y, 1)
                transposes(t_layer(l, 2), tok, tokens_ready())
                ready(t_layer(l, 2))
                out_projection(c0 + C_OUT2)
                transposes(t_layer(l, 3), tok, tokens_ready())
                ready(t_layer(l, 3))
                w = NG + NE
                run(group(c0 + C_ROUTER, 1, [B[7][:, 0:w], B[7][:, w:2 * w]], w, kt=KT))
                mm(B[7][:, 100:108], zero[:, 0:P], zero[:, 0:8], start=True, stop=True).then_inc(r_done, 1)
                moe(l)

        @block.sync
        def _(sync):
            sync.wait_ge(h_ready, 10)
            sync.dma_start(fg[:, :], fgain[1]).then_inc(fg_in, 16)
            sync.wait_ge(h_ready, 20)
            sync.dma_start(out.rearrange("(t p) d -> p t d", p=P), h[:, :, :]).then_inc(out_done, 16)
            sync.wait_ge(out_done, 16)




def _constants():
    f = np.float32
    con = np.zeros((P, CONST_N), f)

    def put(name, a):
        lo, hi = CONST[name]
        con[0:a.shape[0], lo:hi] = a.reshape(a.shape[0], hi - lo)

    i = np.arange(P)
    put("ident", np.eye(P, dtype=f))
    put("upper", (i[:, None] >= i[None, :]).astype(f))
    put("ones", np.ones((P, P), f))
    t, s = np.arange(S)[:, None], np.arange(S)[None, :]
    lag = t - s

    def packed(m):
        return np.concatenate([m[0:P, 0:P], m[P:S, 0:S]], axis=1)

    count = sum(((lag >= 0) & (lag % d == 0) & (lag <= w)).astype(np.int64) for w, d in ((128, 1), (512, 4), (2048, 16)))
    put("dilated", packed(np.where(count > 0, np.log(np.maximum(count, 1)), NEG).astype(f)))
    put("causal", packed(np.where(lag >= 0, 0.0, NEG).astype(f)))
    put("chunked", packed(np.where(s // 64 <= t // 64, 0.0, NEG).astype(f)))
    strict = np.where(lag > 0, 0.0, NEG).astype(f).T
    put("strict", np.concatenate([strict[0:P, 0:S], strict[P:S, P:S]], axis=1))

    def tokens(a):
        return a.reshape(NT, P, -1).transpose(1, 0, 2)

    inv = (f(1.0) / (f(10000.0) ** (np.arange(0, HD, 2, dtype=f) / f(HD)))).astype(f)
    ang = np.arange(S, dtype=f)[:, None] * inv[None, :]
    cos, sin = np.cos(ang).astype(f), np.sin(ang).astype(f)
    cos, sin = np.concatenate([cos, cos], 1), np.concatenate([-sin, sin], 1)
    put("cos_q", tokens(cos * f(HD ** -0.5)))
    put("sin_q", tokens(sin * f(HD ** -0.5)))
    put("cos_k", tokens(cos))
    put("sin_k", tokens(sin))
    inv = (f(10000.0) ** (-np.arange(0, 32, 2, dtype=f) / f(32))).astype(f)
    ang = np.arange(S, dtype=f)[:, None] * inv[None, :]
    cos, sin = np.cos(ang).astype(f), np.sin(ang).astype(f)
    put("cos_m", tokens(np.concatenate([cos, cos], 1)))
    put("sin_m", tokens(np.concatenate([-sin, sin], 1)))
    pools = []
    for w in (2, 4, 8, 16):
        m = np.where((lag >= 0) & (lag < w), 1.0 / np.minimum(t + 1, w), 0.0) - np.eye(S)
        m = m.T.astype(f)
        pools.append(np.concatenate([m[0:P, 0:S], m[P:S, P:S]], axis=1))
    put("pool", np.stack(pools, axis=1))
    put("sel", np.repeat(np.eye(8, dtype=f), P, axis=1))
    put("iota", np.tile(np.arange(8, dtype=f), (P, 1)))
    put("iota64", np.tile(np.arange(8, dtype=f) - 64, (P, 1)))
    put("minus_half", np.full((P, 16), -0.5, f))
    put("before", (i[:, None] < i[None, :]).astype(f))
    put("slot", np.tile(np.arange(P, dtype=f), (P, 1)))
    e = np.arange(EG, dtype=f)
    put("chunk_of", np.tile(np.concatenate([3 * e - 1, 3 * e, 3 * e + 4]), (P, 1)))
    put("inv_c", np.tile(np.array([1 / 256, 1 / 128] * 2, f), (P, 1)))
    return con


def _stream(a):
    out = np.zeros((NCHUNK, P, CH), np.float32)

    def tiles(w):
        return w.reshape(-1, P, w.shape[1]).transpose(1, 0, 2)

    def put(c, part):
        part = part.reshape(P, -1)
        out[c, :, 0:part.shape[1]] = part

    def columns(c, w, groups):
        for lo, hi in groups:
            k = tiles(w[:, lo:hi])
            put(c, k[:, 0:4])
            put(c + 1, k[:, 4:8])
            c += 2

    halves = [(0, 512), (512, 1024)]
    w = a["hyb_w_in"][0]
    put(C_FB, tiles(w[:, 3072:3080]))
    columns(C_HYB, w, [(lo, lo + 512) for lo in (0, 512, 1536, 2048, 1024, 2560)])
    columns(C_HYB_OUT, a["hyb_w_out"][0], halves)
    columns(C_DIFF, a["diff_w_qkv"][0], [(lo, lo + 512) for lo in (0, 1024, 512, 1536, 2048, 2560)])
    columns(C_DIFF_OUT, a["diff_w_out"][0], halves)

    def up_at(c0, j):
        return c0 if j == 0 else c0 + 3 * j - 1

    def down_at(c0, j, n):
        return c0 + 3 * j + 4 if j < n - 1 else c0 + 3 * n - 1

    for l in range(LAYERS):
        up, down = a["ffn_w_up"][l], a["ffn_w_down"][l]
        for j in range(NFB):
            for u in range(2):
                f = (2 * j + u) * P
                put(up_at(C_FFN[l], j) + u, np.stack([tiles(up[:, f:f + P]), tiles(up[:, DFF + f:DFF + f + P])], axis=2))
            put(down_at(C_FFN[l], j, NFB), tiles(down[2 * j * P:(2 * j + 2) * P]))
        c0 = C_LAYER[l]
        columns(c0 + C_IN2, a["w_in_2"][l], [(0, 416), (416, 928), (928, 1440)])
        put(c0 + C_UQ, tiles(a["w_uq_2"][l]))
        put(c0 + C_UKV, tiles(a["w_ukv_2"][l]))
        columns(c0 + C_OUT2, a["w_out_2"][l], halves)
        put(c0 + C_ROUTER, tiles(np.concatenate([a["w_group_2"][l], a["w_expert_2"][l]], axis=1)))
        for e in range(NE):
            gate, up, down = (a[k][l, e // EG, e % EG] for k in ("w_gate_2", "w_up_2", "w_down_2"))
            both = np.concatenate([tiles(gate), tiles(up)], axis=2)
            c = up_at(c0 + C_MOE, e)
            put(c, both[:, 0:4])
            put(c + 1, both[:, 4:8])
            put(down_at(c0 + C_MOE, e, NE), tiles(down))
    return out


def _small(a):
    small = np.zeros((P, SMALL_N), np.float32)

    def put(name, part):
        lo, hi = SMALL[name]
        small[0:part.shape[0], lo:hi] = part.reshape(part.shape[0], hi - lo)

    def columns(w):
        return w.reshape(-1, P).T

    def rows(w):
        return np.broadcast_to(w.reshape(1, -1), (P, w.size))

    put("attn_g", columns(a["attn_norm"]))
    put("ffn_g", columns(a["ffn_norm"]))
    put("norm1_g", columns(a["norm1_g_2"]))
    put("norm2_g", columns(a["norm2_g_2"]))
    put("c_g", columns(np.concatenate([a["q_norm_g_2"], a["kv_norm_g_2"]], axis=1)))
    put("subln", columns(a["diff_subln"]))
    put("conv_b", columns(a["ffn_conv_b"]))
    put("conv_w", columns(a["ffn_conv_w"]))
    put("b_f", a["hyb_b_f"].reshape(-1, 1))
    put("router_b", rows(np.concatenate([a["b_group_2"], a["b_expert_2"]], axis=1)))
    put("pool_scale", rows(a["pool_scale_2"]))
    put("lam", rows(a["diff_lambda"]))
    put("pool_w", a["pool_w_2"].reshape(2, 2, 2, HD, HD).transpose(2, 3, 0, 1, 4).reshape(P, -1))
    return small


def kernel(**inputs):
    import concourse.bacc as _bacc
    from concourse.bass_utils import run_bass_kernel_spmd as _run

    a = {k: np.asarray(v) for k, v in inputs.items()}
    gains = np.stack([np.broadcast_to(a[k].reshape(1, D), (P, D)) for k in ("final_norm", "final_g_2")])
    arrays = {
        "x": np.ascontiguousarray(a["x"].reshape(S, D)), "stream": _stream(a), "small": _small(a),
        "const": _constants(), "fgain": np.ascontiguousarray(gains),
    }
    nc = _bacc.Bacc("TRN2", target_bir_lowering=False, num_devices=1)
    args = [nc.dram_tensor(n, v.shape, F32, kind="ExternalInput").ap() for n, v in arrays.items()]
    args.append(nc.dram_tensor("out", (S, D), F32, kind="ExternalOutput").ap())
    build(nc, *args)
    r = _run(nc, [arrays], core_ids=[0])
    return r.results[0]["out"].reshape(1, S, D)
```

```python
import math

import numpy as np
import concourse.bass as bass
from concourse import mybir
from contextlib import ExitStack

F32 = mybir.dt.float32
F32R = mybir.dt.float32r
ALU = mybir.AluOpType
ACT = mybir.ActivationFunctionType
AX = mybir.AxisListType

P = 128
S = 256
NT = S // P
D = 1024
KT = D // P
HD = 64
DFF = 2816
FT = DFF // P
NFB = FT // 2
NE = 32
NG = 4
EG = NE // NG
DE = 256
LAYERS = 2
CH = 2048
RING = 3
AHEAD = 2
NEG = -1e30
EPS = 1e-6
SUB_EPS = 1e-5
LAM_INIT = 0.8 - 0.6 * math.exp(-0.3 * 1)
MLA_QK = 96
MLA_SCALE = float(MLA_QK) ** -0.5
G0W, G1W, G2W = 416, 512, 512

C_FB = 0
C_HYB = 1
C_HYB_OUT = C_HYB + 12
C_FFN = [C_HYB_OUT + 4, 0]
C_DIFF = C_FFN[0] + 3 * NFB
C_DIFF_OUT = C_DIFF + 12
C_FFN[1] = C_DIFF_OUT + 4
C_LAYER = [C_FFN[1] + 3 * NFB, 0]
C_IN2, C_UQ, C_UKV, C_OUT2, C_MOE = 0, 6, 7, 8, 12
C_PER_LAYER = C_MOE + 3 * NE
C_LAYER[1] = C_LAYER[0] + C_PER_LAYER
NCHUNK = C_LAYER[1] + C_PER_LAYER
WIDTH = {C_FB: KT * 8}
for _c in C_LAYER:
    WIDTH.update({_c + C_UQ: 2 * 768, _c + C_UKV: 1024})



def _columns(fields):
    at, out = 0, {}
    for name, n in fields:
        out[name] = (at, at + n)
        at += n
    return out, at


SMALL, SMALL_N = _columns([
    ("attn_g", 2 * KT), ("ffn_g", 2 * KT), ("norm1_g", 2 * KT), ("norm2_g", 2 * KT), ("c_g", 2 * 3),
    ("subln", 1), ("conv_b", 2 * FT), ("conv_w", 2 * 3 * FT), ("b_f", 1), ("router_b", 2),
    ("pool_scale", 2 * 256), ("lam", 4 * HD), ("pool_w", 2 * 4 * HD)])
CONST, CONST_N = _columns([
    ("ident", P), ("ones", P), ("minus_half", 16), ("upper", P), ("dilated", 384), ("causal", 384), ("chunked", 384),
    ("strict", 384), ("cos_q", NT * HD), ("sin_q", NT * HD), ("cos_k", NT * HD), ("sin_k", NT * HD),
    ("cos_m", NT * 32), ("sin_m", NT * 32), ("pool", 4 * 384), ("iota", 8), ("iota64", 8),
    ("inv_c", 4),
    ("before", P), ("slot", P), ("chunk_of", 24)])

MLA_BANKS = (2, 0)
CONST_HEAD = CONST["minus_half"][1]

T_TILES = [8, 8, 8, 8, 8, 8] + [8, 3, 8, 8] * LAYERS
T_BASE = [sum(T_TILES[:q]) for q in range(len(T_TILES) + 1)]
T_BANKS = [2 * (n // 3) for n in T_TILES]
T_BANK_BASE = [sum(T_BANKS[:q]) for q in range(len(T_BANKS) + 1)]
HALVES = {False: [(0, 0), (0, 1), (1, 0), (1, 1)], True: [(0, 0), (1, 0), (0, 1), (1, 1)]}


def t_place(k):
    return 2 * (k // 4) + k % 2, k % 4 // 2

T_L0, T_L0O, T_F0, T_L1, T_L1O, T_F1 = range(6)


def t_layer(l, j):
    return 6 + 4 * l + j


def build(nc, x, stream, router, small, const, fgain, out):
    es = ExitStack()
    with es:
        def sb(name, shape, dt=F32):
            return es.enter_context(nc.sbuf_tensor(name, shape, dt))

        def sem(name):
            return es.enter_context(nc.semaphore(name))

        raw = sb("raw", [P, RING, CH])
        wh = sb("w_high", [P, RING, CH], F32R)
        wl = sb("w_low", [P, RING, CH], F32R)
        h = sb("residual", [P, NT, D])
        tok = sb("tok", [P, NT, D])
        xh = sb("x_high", [P, KT, S], F32R)
        xl = sb("x_low", [P, KT, S], F32R)
        ch = sb("c_high", [P, 3, S], F32R)
        cl = sb("c_low", [P, 3, S], F32R)
        qT = sb("qT", [P, 8, S])
        kT = sb("kT", [P, 8, S])
        sT = sb("stick_qkT", [P, 4, S])
        v = sb("v", [P, NT, D])
        qk_tok = sb("qk_tok", [P, NT, 512])
        rope_a = sb("rope_a", [P, NT, 512])
        rope_b = sb("rope_b", [P, NT, 512])
        c_tok = sb("c_tok", [P, NT, 384])
        kr_tok = sb("kr_tok", [P, NT, 32])
        sm = sb("scores_masked", [P, 2, 384])
        probs = sb("probs", [P, 4, 384])
        pr, prT = probs[:, 0:2, :], probs[:, 2:4, :]
        nmax = sb("neg_max", [P, 16, NT])
        den = sb("den", [P, 16, NT])
        rden = sb("rden", [P, 16, NT])
        zm, sw = sb("stick_z", [P, 4, 384]), probs
        mla_tok = (qk_tok[:, :, 0:384], c_tok)
        conv, gate = rope_a[:, :, 0:S], rope_a[:, :, S:2 * S]
        hid = rope_b[:, :, 0:S]
        dT = rope_b[0:HD, :, :].rearrange("p t d -> p (t d)").rearrange("p (g s) -> p g s", g=4)
        gh = sb("hid_high", [P, 2, 2, S], F32R)
        gl = sb("hid_low", [P, 2, 2, S], F32R)
        sml = sb("small_sb", [P, SMALL_N])
        con = sb("const_sb", [P, CONST_N])
        fg = sb("final_gain", [P, D])
        ssq = sb("ssq", [P, NT, 2])
        rstd = sb("rstd", [P, NT])
        msq = sb("msq", [P, 16])
        cssq = sb("c_ssq", [P, 4])
        crs = sb("c_rstd", [P, 4])
        hss = sb("head_ssq", [P, 16])
        hrs = sb("head_rstd", [P, 16])
        gain_sub = sb("gain_sub", [P, 1])
        lamb = sb("lam", [P, 8])
        lamw = rope_a[:, 0, 0:HD]
        spare_c, spare_s = (a[0:8, :, :].rearrange("p t d -> p (t d)") for a in (c_tok, sm))
        f_w = [s[:, i * S:(i + 1) * S] for s, i in ((spare_c, 1), (spare_c, 2), (spare_s, 0), (spare_s, 1),
                                                    (spare_c, 0), (spare_s, 2))]
        spare_q = qk_tok[:, :, :].rearrange("p t d -> p (t d)")
        rw = spare_q[:, 0:384].rearrange("p (j n) -> p j n", j=24)
        rbig = spare_q[:, 512:512 + NT * NE].rearrange("p (t n) -> p t n", t=NT)
        rl = spare_q[:, 384:384 + NT * (NG + NE)].rearrange("p (t n) -> p t n", t=NT)
        rT = spare_q[0:NG + NE, 640:640 + S]
        comb = sb("combine", [P, NG, EG])
        spare_v = v[:, :, :].rearrange("p t d -> p (t d)")
        pick = spare_v[:, 0:NT * NG * P].rearrange("p (t g j) -> p t g j", t=NT, g=NG)
        spread = spare_v[:, NT * NG * P:].rearrange("p (g t) -> p g t", g=NG)
        router_raw = rope_a[:, 1, P:P + KT * (NG + NE)]
        router_wh, router_wl = (sb(f"router_{n}", [P, KT * (NG + NE)], F32R) for n in ("high", "low"))
        ys = kT[:, 0:4, :].rearrange("p a s -> p (a s)")
        x_over, hid_over = qT[:, 0:4, :].rearrange("p a s -> p (a s)").rearrange("p (k j) -> p k j", k=KT), qT[:, 4, :]
        chunk_over = tok[:, :, :].rearrange("p t d -> p (t d)")
        route_f = sb("route_values", [P, 32])
        route_i = sb("route_integers", [P, 32], mybir.dt.int32)
        zero = sb("zero", [P, P], F32R)

        B = [es.enter_context(nc.psum_tensor(f"bank{i}", [P, 512], F32)) for i in range(8)]

        x_in = [sem(f"x_in{t}") for t in range(NT)]
        head_in, const_in, small_in, fg_in, out_done = map(sem, (
            "const_head_in", "const_in", "small_in", "fg_in", "out_done"))
        chunk_in = [sem(f"chunk_in{i}") for i in range(RING)]
        w_high, w_low, chunk_used = map(sem, ("w_high_ready", "w_low_ready", "chunk_used"))
        ssq_ready, rstd_ready, tok_ready = map(sem, ("ssq_ready", "rstd_ready", "tok_ready"))
        pool_step = sem("pool_step")
        t_done, t_high, t_low = map(sem, ("t_done", "t_high_ready", "t_low_ready"))
        h_ready, bank_done = sem("h_ready"), sem("bank_done")
        dve_step, act_step = sem("dve_step"), sem("act_step")
        qk_tok_ready, qk_tr, qkT_ready, v_ready = map(sem, ("qk_tok_ready", "qk_transposed", "qkT_ready", "v_ready"))
        rope_ready = sem("rope_ready")
        f_z, f_neg, f_ln, negc_ready = map(sem, ("forget_z_ready", "forget_neg_ready", "forget_ln_ready", "neg_c_ready"))
        s_done, nm_ready, p_ready, p_tr, pT_ready, pv_done, o_done = map(sem, (
            "scores_done", "neg_max_ready", "probs_ready", "probs_transposed", "probsT_ready", "pv_done", "o_done"))
        hss_ready, hrs_ready, lam_sum, lam_exp = map(sem, ("head_ssq_ready", "head_rstd_ready", "lam_sum", "lam_exp"))
        conv_init, conv_ready, silu_ready, hid_ready, g_high, g_low = map(sem, (
            "conv_init", "conv_ready", "silu_ready", "hid_ready", "hid_high_ready", "hid_low_ready"))
        m_silu, m_hid, m_tr, m_high, m_low = map(sem, (
            "expert_silu_ready", "expert_hid_ready", "expert_hid_transposed", "expert_high_ready", "expert_low_ready"))
        zero_ready = sem("zero_ready")
        goh_ready, place_done, pick_ready, spread_done, spread_ready, share_ready, comb_done, route_ready = map(sem, (
            "group_one_hot_ready", "places_done", "pick_ready", "spread_done", "spread_ready", "share_ready",
            "combine_done", "route_ready"))
        sums_half = sem("group_sums_first_half_done")
        gx_done, gx_high, gx_low, ys_ready, sc_done, sc_read = map(sem, (
            "slots_gathered", "slots_high_ready", "slots_low_ready", "group_result_ready", "scatter_done", "scatter_added"))
        over_turn = [sem(f"overflow_turn{l}") for l in range(LAYERS)]
        over_in = [sem(f"overflow_chunk_in{l}") for l in range(LAYERS)]
        c_ssq_ready, c_rstd_ready, c_tok_ready, mla_group, mla_q_copied = map(sem, (
            "c_ssq_ready", "c_rstd_ready", "c_tok_ready", "mla_group_done", "mla_q_copied"))
        z_done, na_ready, nexp_ready, ln_ready, sp_ready, cum_done, d_ready, a_ready, spv_done = map(sem, (
            "stick_z_done", "stick_na_ready", "stick_exp_ready", "stick_ln_ready", "stick_sp_ready", "stick_cum_done",
            "stick_d_ready", "stick_a_ready", "stick_pv_done"))
        pool_d, pool_dT, pool_y = map(sem, ("pool_d_done", "pool_dT_ready", "pool_y_done"))
        router_in, router_high, router_low = map(sem, ("router_in", "router_high_ready", "router_low_ready"))
        r_products = sem("router_products_done")
        r_biased, r_done, r_sub, r_exp, r_dif, r_exp2, comb_ready = map(sem, (
            "router_biased", "router_done", "router_sub_ready", "router_exp_ready", "router_dif_ready", "router_exp2_ready", "combine_ready"))
        block = es.enter_context(nc.Block())

        def cs(name, a=0, b=None):
            lo, hi = CONST[name]
            return con[:, lo + a:hi if b is None else lo + b]

        def ps(name, a=0, b=None):
            lo, hi = SMALL[name]
            return sml[:, lo + a:hi if b is None else lo + b]

        ident = cs("ident")

        @block.sync
        def _(sync):
            for t in range(NT):
                sync.dma_start(h[:, t, :], x[t * P:(t + 1) * P, :]).then_inc(x_in[t], 16)
            sync.dma_start(con[:, 0:CONST_HEAD], const[:, 0:CONST_HEAD]).then_inc(head_in, 16)
            sync.dma_start(raw[:, C_FB, 0:WIDTH[C_FB]], stream[C_FB][:, 0:WIDTH[C_FB]]).then_inc(chunk_in[C_FB], 16)
            sync.dma_start(sml[:, :], small).then_inc(small_in, 16)
            for c in range(1, RING):
                sync.dma_start(raw[:, c, :], stream[c]).then_inc(chunk_in[c], 16)
            sync.dma_start(con[:, CONST_HEAD:], const[:, CONST_HEAD:]).then_inc(const_in, 16)
            sync.dma_start(fg[:, :], fgain[0]).then_inc(fg_in, 16)

            def load(c, u):
                sync.wait_ge(w_low, c - RING + 1)
                sync.dma_start(raw[:, u, :], stream[bass.ds(c, 1)].squeeze(0) if not isinstance(c, int) else stream[c])\
                    .then_inc(chunk_in[u], 16)

            whole = NCHUNK // RING
            with sync.Fori(1, whole) as i:
                for u in range(RING):
                    load(i * RING + u, u)
            for c in range(whole * RING, NCHUNK):
                load(c, c % RING)

        @block.gpsimd
        def _(pool):
            step = [0]

            def link(ins):
                step[0] += 1
                ins.then_inc(pool_step, 1)
                pool.wait_ge(pool_step, step[0])

            pool.wait_ge(head_in, 16)
            norm = [0]

            def rms(by_half=False):
                order = HALVES[by_half]
                norm[0] += 1
                for t in range(NT):
                    pool.wait_ge(ssq_ready, 4 * norm[0] - 3 + order.index((t, 1)))
                    link(nc.gpsimd.tensor_scalar(msq[:, t:t + 1], ssq[:, t, 0:1], ssq[:, t, 1:2], EPS, ALU.add, ALU.add))
                    nc.gpsimd.tensor_tensor(rstd[:, t:t + 1], msq[:, t:t + 1], cs("minus_half", 0, 1), ALU.pow)\
                        .then_inc(rstd_ready, 1)

            rms()
            rms(True)
            rms()
            pool.wait_ge(const_in, 16)
            for j in range(8):
                pool.wait_ge(hss_ready, j + 1)
                cols = slice(2 * j, 2 * j + 2)
                link(nc.gpsimd.tensor_scalar(msq[:, cols], hss[:, cols], 1.0 / P, SUB_EPS, ALU.mult, ALU.add))
                nc.gpsimd.tensor_tensor(hrs[:, cols], msq[:, cols], cs("minus_half", 0, 2), ALU.pow).then_inc(hrs_ready, 1)
            rms(True)
            rms()
            for l in range(LAYERS):
                if l:
                    pool.wait_ge(router_low, l)
                pool.dma_start(router_raw, router[l]).then_inc(router_in, 16)
                rms()
                pool.wait_ge(c_ssq_ready, l + 1)
                link(nc.gpsimd.tensor_tensor(msq[:, 0:4], cssq[:, :], cs("inv_c"), ALU.mult))
                link(nc.gpsimd.tensor_scalar(msq[:, 4:8], msq[:, 0:4], 1.0, EPS, ALU.mult, ALU.add))
                nc.gpsimd.tensor_tensor(crs[:, :], msq[:, 4:8], cs("minus_half", 0, 4), ALU.pow).then_inc(c_rstd_ready, 1)
                rms(True)
                pool.wait_ge(route_ready, l + 1)
                with pool.If(pool.value_load(route_i[0:1, 0:1], min_val=0, max_val=1)):
                    for e in range(EG):
                        for j in range(3):
                            pool.wait_ge(over_turn[l], 3 + 7 * e + (0, 1, 2)[j] if e or j else 3)
                            c = pool.value_load(route_i[0:1, 1 + j * EG + e:2 + j * EG + e], min_val=0, max_val=NCHUNK - 1)
                            pool.dma_start(chunk_over, stream[bass.ds(c, 1)].squeeze(0)).then_inc(over_in[l], 16)
            rms()

        @block.scalar
        def _(act):
            step = [0]
            norm = [0]

            def link(ins):
                step[0] += 1
                ins.then_inc(act_step, 1)
                act.wait_ge(act_step, step[0])

            def split(c, off=0):
                if isinstance(off, int) and c + RING * off >= NCHUNK:
                    return
                u = c % RING
                act.wait_ge(chunk_in[u], (off + c // RING) * 16 + 16)
                if c >= RING or not isinstance(off, int):
                    act.wait_ge(chunk_used, off * RING + (c - RING + 1))
                n = WIDTH.get(c, CH) // 2
                for half in range(2):
                    cols = slice(half * n, half * n + n)
                    nc.scalar.activation(wh[:, u, cols], raw[:, u, cols], ACT.Copy).then_inc(w_high, 1)

            def rms(additions, by_half=False):
                for i, (t, half) in enumerate(HALVES[by_half]):
                    if additions:
                        act.wait_ge(h_ready, 4 * (additions - 1) + i + 1)
                    elif half == 0:
                        act.wait_ge(x_in[t], 16)
                    cols = slice(half * 512, half * 512 + 512)
                    nc.scalar.activation(tok[:, t, cols], h[:, t, cols], ACT.Square, scale=float(D) ** -0.5,
                                         accum_out=ssq[:, t, half:half + 1]).then_inc(ssq_ready, 1)

            def high(q, dst, gain, free):
                act.wait_ge(chunk_used, free) if free else None
                for k in range(T_TILES[q]):
                    b, at = t_place(k)
                    act.wait_ge(t_done, T_BANK_BASE[q] + b + 1)
                    if at:
                        act.wait_ge(t_low, T_BASE[q] + k - 1)
                    nc.scalar.activation(dst[:, k, :], B[4 + b][:, at * S:at * S + S], ACT.Copy, scale=gain(k)).then_inc(t_high, 1)

            def one(k):
                return cs("ones", 0, 1)

            def qkT_copy(n, dst, tile, rows=P):
                for t in range(NT):
                    act.wait_ge(qk_tr, 2 * n + t + 1)
                    nc.scalar.activation(dst[0:rows, tile:tile + 4, t * P:(t + 1) * P],
                                         B[6 + t][0:rows, :].rearrange("p (a s) -> p a s", a=4), ACT.Copy)\
                        .then_inc(qkT_ready, 1)

            def copy_v(c, banks, at, src=None):
                act.wait_ge(chunk_used, c + 1)
                for t in range(NT):
                    nc.scalar.activation(v[:, t, at:at + 512], B[banks + t][:, :], ACT.Copy).then_inc(v_ready, 1)

            def softmaxes(first, heads, between=None):
                for a in heads:
                    act.wait_ge(nm_ready, first + a + 1)
                    if a >= 2:
                        act.wait_ge(p_tr, first + a - 1)
                    for t, lo, hi in ((0, 0, 128), (1, 128, 384)):
                        ins = nc.scalar.activation(pr[:, a % 2, lo:hi], sm[:, a % 2, lo:hi], ACT.Exp,
                                                   bias=nmax[:, a, t:t + 1], scale=-1.0,
                                                   accum_out=den[:, a, t:t + 1])
                    ins.then_inc(p_ready, 1)
                    if between is not None:
                        between(a)

            def head_squares(a):
                if a % 2 and a >= 3:
                    j = (a - 3) // 2
                    act.wait_ge(o_done, 16 + 2 * j + 2)
                    for t in range(NT):
                        ins = nc.scalar.activation((rope_a, rope_b)[j // 4][:, t, (j % 4) * P:(j % 4 + 1) * P],
                                                   tok[:, t, j * P:(j + 1) * P], ACT.Square,
                                                   accum_out=hss[:, 2 * j + t:2 * j + t + 1])
                    ins.then_inc(hss_ready, 1)

            def projections(c0, qk_first, first):
                for g in range(6):
                    c = c0 + 2 * g
                    split(c + AHEAD)
                    if 1 <= g <= 4:
                        n = qk_first + g - 1
                        qkT_copy(n, (qT, kT)[(g - 1) % 2], 4 * ((g - 1) // 2))
                    if g == 5:
                        softmaxes(first, (0, 1))
                    split(c + 1 + AHEAD)
                    if g >= 4:
                        copy_v(c + 1, 2 * (g % 2), 512 * (g - 4))

            def plain(c0, n):
                for c in range(c0, c0 + n):
                    split(c + AHEAD)

            def glu(l):
                c0 = C_FFN[l]
                nc_b, nc_w = SMALL["conv_b"][0] + l * FT, SMALL["conv_w"][0] + l * 3 * FT

                def tile(f, fi, u, c, off, lookahead):
                    act.wait_ge(chunk_used, off * RING + (c + 1))
                    if not isinstance(f, int) or f >= 2 or l:
                        act.wait_ge(hid_ready, fi - 1)
                    wcol = sml[:, bass.ds(f + (nc_w + 2 * FT), 1)]
                    bcol = sml[:, bass.ds(f + nc_b, 1)]
                    nc.scalar.activation(conv[:, u, :], B[4 + u][:, 0:S], ACT.Identity, bias=bcol,
                                         scale=wcol).then_inc(conv_init, 1)
                    if lookahead is not None:
                        split(lookahead, off)
                    act.wait_ge(conv_ready, fi * 2 + 2)
                    nc.scalar.activation(gate[:, u, :], conv[:, u, :], ACT.Silu).then_inc(silu_ready, 1)

                def high_part(fi, u, buf, free):
                    act.wait_ge(hid_ready, fi + 1)
                    if free is not None:
                        act.wait_ge(chunk_used, free)
                    nc.scalar.activation(gh[:, buf, u, :], hid[:, u, :], ACT.Copy).then_inc(g_high, 1)

                f0 = l * FT
                plain(c0, 1)
                tile(0, f0, 0, c0, 0, c0 + 1 + AHEAD)
                high_part(f0, 0, 0, c0)
                tile(1, f0 + 1, 1, c0 + 1, 0, None)
                high_part(f0 + 1, 1, 0, c0)
                with act.Fori(0, (NFB - 1) // 2) as i:
                    for j in range(2):
                        c = c0 + 2 + 3 * j
                        for u in range(2):
                            fi = i * 4 + (f0 + 2 + 2 * j + u)
                            f = i * 4 + (2 + 2 * j + u)
                            if u == 0:
                                split(c + AHEAD, i * 2)
                            tile(f, fi, u, c + u, i * 2, c + 1 + AHEAD if u == 0 else None)
                            high_part(fi, u, (1 + j) % 2, i * 6 + (c - 3))
                        split(c + 2 + AHEAD, i * 2)
                plain(c0 + 3 * NFB - 1, 1)

            def moe(l):
                c0 = C_LAYER[l] + C_MOE
                e0, g0 = l * NE, l * NG

                def gathered(g, halves=(0, 1)):
                    for b in halves:
                        act.wait_ge(gx_done, 2 * (g0 + g) + b + 1)
                        for k in range(4 * b, 4 * b + 4):
                            ins = nc.scalar.activation(xh[:, k, (g % 2) * P:(g % 2 + 1) * P],
                                                       B[2 + b][:, (k % 4) * P:(k % 4 + 1) * P], ACT.Copy,
                                                       scale=ps("norm2_g", l * KT + k, l * KT + k + 1))
                        ins.then_inc(gx_high, 1)

                def silu(e, c, off):
                    act.wait_ge(chunk_used, off * RING + (c + 1))
                    if not isinstance(e, int) or e > 0:
                        act.wait_ge(m_hid, e)
                    nc.scalar.activation(gate[:, 0, :], B[4][:, 0:DE], ACT.Silu).then_inc(m_silu, 1)

                def high_part(e):
                    act.wait_ge(m_tr, e + 1)
                    nc.scalar.activation(gh[:, 0, :, 0:P], B[6][:, 0:2 * P].rearrange("p (k s) -> p k s", k=2), ACT.Copy)\
                        .then_inc(m_high, 1)

                def turn(i, c, off, end=False, extra=None):
                    split(c + AHEAD, off)
                    if extra is not None:
                        extra()
                    high_part(i + e0)
                    split(c + 1 + AHEAD, off)
                    silu(i + (e0 + 1), c + 1, off)
                    if not end:
                        split(c + 2 + AHEAD, off)

                def result(g, c):
                    if g0 + g:
                        act.wait_ge(sc_done, 2 * (g0 + g))
                    for half in range(2):
                        act.wait_ge(*((chunk_used, c + 1) if half else (sums_half, g0 + g + 1)))
                        nc.scalar.activation(ys[:, half * 512:(half + 1) * 512], B[half][:, :], ACT.Copy).then_inc(ys_ready, 1)

                gathered(0)
                act.wait_ge(r_dif, l + 1)
                nc.scalar.activation(rw[:, 13, 0:2], rw[:, 12, 0:2], ACT.Exp).then_inc(r_exp2, 1)
                act.wait_ge(spread_done, l + 1)
                for b in range(2):
                    ins = nc.scalar.activation(spread[:, 2 * b:2 * b + 2, :], B[5 + b][:, :].rearrange("p (g t) -> p g t", g=2),
                                               ACT.Copy)
                ins.then_inc(spread_ready, 1)
                act.wait_ge(comb_done, l + 1)
                nc.scalar.activation(comb[:, :, :], B[0][:, 0:NE].rearrange("p (g e) -> p g e", g=NG), ACT.Copy)\
                    .then_inc(comb_ready, 1)
                split(c0 + 1 + AHEAD)
                silu(e0, c0 + 1, 0)
                for g in range(NG):
                    c = c0 + 2 + 3 * EG * g
                    end = g == NG - 1
                    turn(EG * g, c, 0, False, (lambda: result(g - 1, c - 1)) if g else None)
                    turn(EG * g + 1, c + 3, 0)
                    for b in range(2):
                        turn(EG * g + 2 + b, c + 6 + 3 * b, 0, False, None if end else lambda: gathered(g + 1, (b,)))
                    with act.Fori(4, EG - 1 - end) as i:
                        turn(i + EG * g, c, i)
                    turn(EG * (g + 1) - 1 - end, c + 3 * (EG - 1 - end), 0, end)
                overflow = act.value_load(route_i[0:1, 0:1], min_val=0, max_val=1)
                high_part(e0 + NE - 1)
                split(c0 + 3 * NE - 2 + AHEAD)
                split(c0 + 3 * NE - 1 + AHEAD)
                result(NG - 1, c0 + 3 * NE - 1)

                with act.If(overflow):
                    turn_is = over_turn[l]
                    act.wait_ge(turn_is, 2)
                    for k in range(KT):
                        nc.scalar.activation(x_over[:, k, :], B[2 + k // 4][:, (k % 4) * P:(k % 4 + 1) * P], ACT.Copy,
                                             scale=ps("norm2_g", l * KT + k, l * KT + k + 1))
                    nc.scalar.activation(spread[:, 0, :], B[6][:, 0:S], ACT.Copy)
                    nc.scalar.activation(comb[:, 0, :], B[7][:, 0:EG], ACT.Copy).then_inc(turn_is, 1)
                    with act.Fori(0, EG) as e:
                        act.wait_ge(turn_is, e * 7 + 5)
                        nc.scalar.activation(gate[:, 0, :], B[4][:, 0:DE], ACT.Silu).then_inc(turn_is, 1)
                        act.wait_ge(turn_is, e * 7 + 8)
                        nc.scalar.activation(hid_over, B[6][:, 0:2 * P], ACT.Copy).then_inc(turn_is, 1)
                    act.wait_ge(turn_is, 3 + 7 * EG)
                    for half in range(2):
                        ins = nc.scalar.activation(ys[:, half * 512:(half + 1) * 512], B[half][:, :], ACT.Copy)
                    ins.then_inc(turn_is, 1)

            rms(0)
            split(C_FB)
            act.wait_ge(small_in, 16)
            high(T_L0, xh, lambda k: ps("attn_g", k, k + 1), 0)
            split(1)

            split(AHEAD)
            act.wait_ge(chunk_used, C_FB + 1)
            nc.scalar.activation(f_w[0], B[2][0:8, 0:S], ACT.Identity,
                                 bias=sml[0:8, SMALL["b_f"][0]:SMALL["b_f"][1]]).then_inc(f_z, 1)
            act.wait_ge(f_neg, 1)
            link(nc.scalar.activation(f_w[2], f_w[1], ACT.Exp))
            nc.scalar.activation(f_w[3], f_w[2], ACT.Ln, bias=1.0).then_inc(f_ln, 1)

            projections(C_HYB, 0, 0)
            softmaxes(0, range(2, 16))
            high(T_L0O, xh, one, C_HYB_OUT)
            plain(C_HYB_OUT, 3)
            rms(1, True)
            high(T_F0, xh, lambda k: ps("ffn_g", k, k + 1), C_FFN[0])
            split(C_FFN[0] - 1 + AHEAD)
            glu(0)

            rms(2)
            high(T_L1, xh, lambda k: ps("attn_g", KT + k, KT + k + 1), C_DIFF)
            act.wait_ge(lam_sum, 1)
            nc.scalar.activation(lamb[:, 2:4], lamb[:, 0:2], ACT.Exp).then_inc(lam_exp, 1)
            projections(C_DIFF, 4, 16)
            softmaxes(16, range(2, 16), head_squares)
            head_squares(17)
            high(T_L1O, xh, lambda k: gain_sub[:, 0:1], C_DIFF_OUT)
            plain(C_DIFF_OUT, 3)
            rms(3, True)
            high(T_F1, xh, lambda k: ps("ffn_g", KT + k, KT + k + 1), C_FFN[1])
            split(C_FFN[1] - 1 + AHEAD)
            glu(1)
            rms(4)

            for l in range(LAYERS):
                c0 = C_LAYER[l]
                rms(5 + 2 * l)
                high(t_layer(l, 0), xh, lambda k: ps("norm1_g", l * KT + k, l * KT + k + 1), c0)
                plain(c0, 2)
                act.wait_ge(chunk_used, c0 + 2)
                for t in range(NT):
                    for j, (a, b) in enumerate(((0, 256), (256, 384))):
                        ins = nc.scalar.activation(c_tok[:, t, a:b], B[t][:, a:b], ACT.Square,
                                                   accum_out=cssq[:, 2 * t + j:2 * t + j + 1])
                ins.then_inc(c_ssq_ready, 1)
                plain(c0 + 2, 2)
                high(t_layer(l, 1), ch, lambda k: ps("c_g", l * 3 + k, l * 3 + k + 1), c0)
                n = 8 + 5 * l
                qkT_copy(n, sT, 0)
                plain(c0 + 4, 2)
                copy_v(c0 + 5, 0, 512)

                def stick(function, first, n, ready, done, x, **kw):
                    for i in range(first, first + n):
                        act.wait_ge(ready, 4 * l + i + 1)
                        nc.scalar.activation(x[:, i, :], x[:, i, :], function, **kw).then_inc(done, 1)

                def mla_plain(i, at, with_v):
                    first = MLA_BANKS[i % 2]
                    act.wait_ge(*((mla_group, 2 * l + i // 2 + 1) if i % 2 == 0 else (chunk_used, c0 + C_UQ + i // 2 + 1)))
                    act.wait_ge(qk_tr, 2 * (n + at) + 2)
                    for t in range(NT):
                        src = B[first + t][:, 0:512 if with_v else 384].rearrange("p (a d) -> p a d", a=4)
                        if with_v:
                            nc.scalar.activation(v[:, t, 256 * (i % 2):256 * (i % 2) + 256].rearrange("p (a d) -> p a d", a=4),
                                                 src[:, :, HD:2 * HD], ACT.Copy).then_inc(v_ready, 1)
                        nc.scalar.activation(mla_tok[i % 2][:, t, :].rearrange("p (a d) -> p a d", a=4)[:, :, 0:HD],
                                             src[:, :, 0:HD], ACT.Copy).then_inc(mla_q_copied, 1)

                stick(ACT.Exp, 0, 2, na_ready, nexp_ready, sw)
                mla_plain(0, 0, False)
                mla_plain(1, 0, False)
                stick(ACT.Exp, 2, 2, na_ready, nexp_ready, sw)
                qkT_copy(n + 1, qT, 0, MLA_QK)
                stick(ACT.Ln, 0, 4, nexp_ready, ln_ready, sw, bias=1.0)
                mla_plain(2, 1, True)
                qkT_copy(n + 2, qT, 4, MLA_QK)
                mla_plain(3, 2, True)
                qkT_copy(n + 3, kT, 0, MLA_QK)
                softmaxes(32 + 8 * l, (0, 1))
                qkT_copy(n + 4, kT, 4, MLA_QK)
                stick(ACT.Exp, 0, 4, d_ready, a_ready, zm)

                def other_mixers(a):
                    if a == 2:
                        act.wait_ge(pool_d, l + 1)
                        for j in range(2):
                            ins = nc.scalar.activation(dT[:, 2 * j:2 * j + 2, :],
                                                       B[6 + j][0:HD, :].rearrange("p (g s) -> p g s", g=2), ACT.Copy)
                        ins.then_inc(pool_dT, 1)

                softmaxes(32 + 8 * l, range(2, 8), other_mixers)
                split(c0 + C_OUT2)
                split(c0 + C_OUT2 + 1)
                high(t_layer(l, 2), xh, one, c0 + C_OUT2)
                act.wait_ge(router_in, 16 * (l + 1))
                if l:
                    act.wait_ge(r_done, l)
                nc.scalar.activation(router_wh[:, :], router_raw, ACT.Copy).then_inc(router_high, 1)
                plain(c0 + C_OUT2, 3)
                rms(6 + 2 * l, True)
                high(t_layer(l, 3), xh, lambda k: ps("norm2_g", l * KT + k, l * KT + k + 1), c0 + C_MOE)
                plain(c0 + C_MOE - 1, 2)
                act.wait_ge(r_sub, l + 1)
                nc.scalar.activation(rw[:, 2, 0:8], rw[:, 1, 0:8], ACT.Exp).then_inc(r_exp, 1)
                moe(l)
            rms(9)

        @block.vector
        def _(dve):
            step = [0]
            tt, ts, stt = nc.vector.tensor_tensor, nc.vector.tensor_scalar, nc.vector.scalar_tensor_tensor

            def link(ins):
                step[0] += 1
                ins.then_inc(dve_step, 1)
                dve.wait_ge(dve_step, step[0])

            def split(c, off=0):
                if isinstance(off, int) and c + RING * off >= NCHUNK:
                    return
                u = c % RING
                n = WIDTH.get(c, CH) // 2
                for half in range(2):
                    cols = slice(half * n, half * n + n)
                    dve.wait_ge(w_high, off * (2 * RING) + (2 * c + half + 1))
                    ins = tt(wl[:, u, cols], raw[:, u, cols], wh[:, u, cols].bitcast(F32), ALU.subtract)
                ins.then_inc(w_low, 1)

            def plain(c0, n):
                for c in range(c0, c0 + n):
                    split(c + AHEAD)

            def normed(n):
                dve.wait_ge(rstd_ready, 2 * n + 1)
                ts(tok[:, 0, :], h[:, 0, :], rstd[:, 0:1], None, ALU.mult).then_inc(tok_ready, 1)
                dve.wait_ge(rstd_ready, 2 * n + 2)
                for half in range(2):
                    cols = slice(half * 512, half * 512 + 512)
                    ts(tok[:, 1, cols], h[:, 1, cols], rstd[:, 1:2], None, ALU.mult).then_inc(tok_ready, 1)

            def low(q, dst, hi, gain):
                for k in range(T_TILES[q]):
                    b, at = t_place(k)
                    dve.wait_ge(t_high, T_BASE[q] + k + 1)
                    stt(dst[:, k, :], B[4 + b][:, at * S:at * S + S], gain(k), hi[:, k, :].bitcast(F32),
                        ALU.mult, ALU.subtract).then_inc(t_low, 1)

            def one(k):
                return cs("ones", 0, 1)

            def rope(n, c, banks, cos, sin):
                dve.wait_ge(chunk_used, c + 1)
                for t in range(NT):
                    src = B[banks + t][:, :].rearrange("p (a d) -> p a d", a=8)
                    co = cs(cos, t * HD, (t + 1) * HD).unsqueeze(1).broadcast_to([P, 8, HD])
                    si = cs(sin, t * HD, (t + 1) * HD).unsqueeze(1).broadcast_to([P, 8, HD])
                    a = rope_a[:, t, :].rearrange("p (a d) -> p a d", a=8)
                    b = rope_b[:, t, :].rearrange("p (a d) -> p a d", a=8)
                    tt(a, src, co, ALU.mult)
                    tt(b[:, :, 0:32], src[:, :, 32:64], si[:, :, 0:32], ALU.mult)
                    link(tt(b[:, :, 32:64], src[:, :, 0:32], si[:, :, 32:64], ALU.mult))
                    if n:
                        dve.wait_ge(qk_tr, 2 * (n - 1) + t + 1)
                    tt(qk_tok[:, t, :], rope_a[:, t, :], rope_b[:, t, :], ALU.add).then_inc(qk_tok_ready, 1)

            def scaled(n, c, banks, parts):
                dve.wait_ge(chunk_used, c + 1)
                for t in range(NT):
                    dve.wait_ge(qk_tr, 2 * (n - 1) + t + 1)
                    for a, b, f in parts:
                        ins = ts(qk_tok[:, t, a:b], B[banks + t][:, a:b], f, None, ALU.mult)
                    ins.then_inc(qk_tok_ready, 1)

            def attention(first, n, masks, scale, dv, diff, between=None, score_bank=0, turned_bank=6):
                def scores(a):
                    dve.wait_ge(s_done, first + a + 1)
                    if a >= 2:
                        dve.wait_ge(p_ready, first + a - 1)
                    for t, lo, hi in ((0, 0, 128), (1, 128, 384)):
                        ins = nc.vector.tensor_tensor_reduce(
                            sm[:, a % 2, lo:hi], B[score_bank + a % 2][:, lo:hi], cs(masks(a), lo, hi), -scale, 3e38,
                            ALU.add, ALU.min, nmax[:, a, t:t + 1])
                    ins.then_inc(nm_ready, 1)

                def probs(a):
                    dve.wait_ge(p_tr, first + a + 1)
                    step[0] += 1
                    nc.vector.reciprocal(rden[:, a, :], den[:, a, :]).then_inc(dve_step, 1)
                    if a >= 2:
                        dve.wait_ge(pv_done, first + a - 1)
                    nc.vector.tensor_copy(prT[:, a % 2, :], B[turned_bank + a % 2][:, 0:384]).then_inc(pT_ready, 1)

                    if diff and a % 2:
                        dve.wait_ge(dve_step, step[0])
                        step[0] += 1
                        ts(rden[:, a, :], rden[:, a, :], lamb[:, 6:7], None, ALU.mult).then_inc(dve_step, 1)
                    scale_step[a] = step[0]

                def outputs(a):
                    dve.wait_ge(dve_step, scale_step[a])
                    dve.wait_ge(pv_done, first + a + 1)
                    if diff and a % 2:
                        dve.wait_ge(o_done, first + a)
                    for t in range(NT):
                        z = B[4 + a % 2][:, t * dv:(t + 1) * dv]
                        col = (a // 2 if diff else a) * dv
                        o = tok[:, t, col:col + dv]
                        if diff and a % 2:
                            ins = stt(o, z, rden[:, a, t:t + 1], o, ALU.mult, ALU.add)
                        else:
                            ins = ts(o, z, rden[:, a, t:t + 1], None, ALU.mult)
                    ins.then_inc(o_done, 1)

                scale_step = {}

                def start():
                    scores(0)
                    scores(1)

                def rest():
                    probs(0)
                    for a in range(n):
                        if a + 2 < n:
                            scores(a + 2)
                        if a + 1 < n:
                            probs(a + 1)
                        outputs(a)
                        if between is not None:
                            between(a)
                    dve.wait_ge(o_done, first + n)

                return start, rest

            def head_norms(a):
                if a % 2 and a >= 3:
                    j = (a - 3) // 2
                    dve.wait_ge(hrs_ready, j + 1)
                    for t in range(NT):
                        o = tok[:, t, j * P:(j + 1) * P]
                        ins = ts(o, o, hrs[:, 2 * j + t:2 * j + t + 1], None, ALU.mult)
                    if j == 7:
                        ins.then_inc(tok_ready, 2)

            banks_read = [0]

            def add_bank(t, half, c):
                if c is None:
                    banks_read[0] += 1
                    dve.wait_ge(bank_done, banks_read[0])
                else:
                    dve.wait_ge(chunk_used, c + 1)
                cols = slice(half * 512, half * 512 + 512)
                tt(h[:, t, cols], h[:, t, cols], B[2 * half + t][:, :], ALU.add).then_inc(h_ready, 1)

            def out_projection(c0):
                split(c0 + AHEAD)
                split(c0 + 1 + AHEAD)
                for half in range(2):
                    add_bank(0, half, None)
                    add_bank(1, half, c0 + 2 * half + 1)
                    if half == 0:
                        split(c0 + 2 + AHEAD)

            def glu(l):
                c0 = C_FFN[l]
                cw = SMALL["conv_w"][0] + l * 3 * FT

                def tile(f, fi, u, buf):
                    w0 = sml[:, bass.ds(f + cw, 1)]
                    w1 = sml[:, bass.ds(f + (cw + FT), 1)]
                    dve.wait_ge(conv_init, fi + 1)
                    stt(conv[:, u, 1:S], B[4 + u][:, 0:S - 1], w1, conv[:, u, 1:S], ALU.mult, ALU.add)\
                        .then_inc(conv_ready, 1)
                    dve.wait_ge(conv_ready, fi * 2 + 1)
                    stt(conv[:, u, 2:S], B[4 + u][:, 0:S - 2], w0, conv[:, u, 2:S], ALU.mult, ALU.add)\
                        .then_inc(conv_ready, 1)
                    dve.wait_ge(silu_ready, fi + 1)
                    tt(hid[:, u, :], gate[:, u, :], B[4 + u][:, S:2 * S], ALU.mult).then_inc(hid_ready, 1)
                    dve.wait_ge(g_high, fi + 1)
                    tt(gl[:, buf, u, :], hid[:, u, :], gh[:, buf, u, :].bitcast(F32), ALU.subtract).then_inc(g_low, 1)

                f0 = l * FT
                plain(c0, 1)
                split(c0 + 1 + AHEAD)
                tile(0, f0, 0, 0)
                tile(1, f0 + 1, 1, 0)
                with dve.Fori(0, (NFB - 1) // 2) as i:
                    for j in range(2):
                        c = c0 + 2 + 3 * j
                        split(c + AHEAD, i * 2)
                        split(c + 1 + AHEAD, i * 2)
                        for u in range(2):
                            tile(i * 4 + (2 + 2 * j + u), i * 4 + (f0 + 2 + 2 * j + u), u, (1 + j) % 2)
                        split(c + 2 + AHEAD, i * 2)
                plain(c0 + 3 * NFB - 1, 1)
                c = c0 + 3 * NFB - 1
                for t, half in ((0, 0), (0, 1), (1, 0), (1, 1)):
                    add_bank(t, half, c if t and half else None)

            def route(l, meanwhile):
                A3 = lambda j, n: rw[:, j, 0:NT * n].rearrange("p (t e) -> p t e", t=NT)
                col = lambda j: rw[:, j, 0:NT]
                wide = lambda j, n: col(j).unsqueeze(2).broadcast_to([P, NT, n])
                io = lambda name, n: cs(name, 0, n).unsqueeze(1).broadcast_to([P, NT, n])

                def one_hot(src, best, eq, at, dst, n):
                    link(tt(A3(eq, n), src, wide(best, n), ALU.is_equal))
                    link(stt(A3(eq, n), A3(eq, n), -64.0, io("iota", n), ALU.mult, ALU.add))
                    link(nc.vector.tensor_reduce(col(at), A3(eq, n), AX.X, ALU.min))
                    return tt(A3(dst, n), io("iota64", n), wide(at, n), ALU.is_equal)

                dve.wait_ge(r_products, l + 1)
                n = NG + NE
                bias = sml[0:n, SMALL["router_b"][0] + l:SMALL["router_b"][0] + l + 1]
                ts(rT, B[0][0:n, 0:S], bias, None, ALU.add).then_inc(r_biased, 1)
                dve.wait_ge(r_done, l + 1)
                link(nc.vector.tensor_copy(rl, B[0][:, S:S + NT * n].rearrange("p (t n) -> p t n", t=NT)))
                g_log = rl[:, :, 0:NG]
                link(nc.vector.tensor_reduce(col(0), g_log, AX.X, ALU.max))
                one_hot(g_log, 0, 3, 4, 5, NG).then_inc(goh_ready, 1)
                tt(A3(1, NG), g_log, wide(0, NG), ALU.subtract).then_inc(r_sub, 1)
                dve.wait_ge(place_done, l + 1)
                dve.wait_ge(goh_ready, l + 1)
                at = B[0][:, 128:140]
                link(tt(A3(6, NG), at[:, 0:8].rearrange("p (t g) -> p t g", t=NT), A3(5, NG), ALU.mult))
                link(nc.vector.tensor_reduce(col(7), A3(6, NG), AX.X, ALU.add))
                for g in range(NG):
                    for t in range(NT):
                        ins = ts(pick[:, t, g, :], cs("slot"), rw[:, 7, t:t + 1], rw[:, 5, t * NG + g:t * NG + g + 1],
                                 ALU.is_equal, ALU.mult)
                    ins.then_inc(pick_ready, 1)
                f = route_f
                ts(f[:, 28:32], at[:, 8:12], float(P), None, ALU.is_gt)
                big = rbig[:, :, :].rearrange("p t (g e) -> p t g e", g=NG)
                link(tt(big, rl[:, :, NG:].rearrange("p t (g e) -> p t g e", g=NG),
                        A3(5, NG).unsqueeze(3).broadcast_to([P, NT, NG, EG]), ALU.mult))
                link(nc.vector.tensor_reduce(A3(8, EG), rbig[:, :, :].rearrange("p t (g e) -> p t e g", g=NG), AX.X, ALU.add))
                link(nc.vector.tensor_reduce(col(9), A3(8, EG), AX.X, ALU.max))
                link(one_hot(A3(8, EG), 9, 3, 4, 10, EG))
                link(stt(A3(11, EG), A3(10, EG), NEG, A3(8, EG), ALU.mult, ALU.add))
                link(nc.vector.tensor_reduce(col(14), A3(11, EG), AX.X, ALU.max))
                tt(col(12), col(14), col(9), ALU.subtract).then_inc(r_dif, 1)
                meanwhile()
                link(one_hot(A3(11, EG), 14, 15, 16, 17, EG))
                dve.wait_ge(r_exp, l + 1)
                link(nc.vector.tensor_reduce(col(18), A3(2, NG), AX.X, ALU.add))
                link(nc.vector.reciprocal(col(18), col(18)))
                dve.wait_ge(r_exp2, l + 1)
                link(ts(col(19), col(13), 1.0, None, ALU.add))
                link(nc.vector.reciprocal(col(19), col(19)))
                link(tt(col(20), col(19), col(18), ALU.mult))
                link(tt(col(21), col(20), col(13), ALU.mult))
                tt(A3(22, EG), A3(10, EG), wide(20, EG), ALU.mult)
                link(tt(A3(23, EG), A3(17, EG), wide(21, EG), ALU.mult))
                tt(A3(22, EG), A3(22, EG), A3(23, EG), ALU.add).then_inc(share_ready, 1)
                nc.vector.tensor_reduce(f[:, 0:1], f[:, 28:32], AX.X, ALU.max)
                link(tt(f[:, 28:32], f[:, 28:32], cs("iota", 0, NG), ALU.mult))
                link(nc.vector.tensor_reduce(f[:, 25:26], f[:, 28:32], AX.X, ALU.add))
                link(ts(f[:, 25:26], f[:, 25:26], float(3 * EG), None, ALU.mult))
                link(ts(f[:, 1:25], cs("chunk_of"), f[:, 25:26], None, ALU.add))
                c0 = C_LAYER[l] + C_MOE
                ts(f[:, 1:9], f[:, 1:9], 0.0, float(c0), ALU.max, ALU.add)
                ts(f[:, 9:17], f[:, 9:17], 1.0, float(c0), ALU.max, ALU.add)
                link(ts(f[:, 17:25], f[:, 17:25], float(3 * NE - 1), float(c0), ALU.min, ALU.add))
                nc.vector.tensor_copy(route_i[:, 0:25], f[:, 0:25]).then_inc(route_ready, 1)

            def moe(l):
                c0 = C_LAYER[l] + C_MOE
                e0, g0 = l * NE, l * NG

                def gathered(g, halves=(0, 1)):
                    for b in halves:
                        dve.wait_ge(gx_high, 2 * (g0 + g) + b + 1)
                        for k in range(4 * b, 4 * b + 4):
                            half = slice((g % 2) * P, (g % 2 + 1) * P)
                            ins = stt(xl[:, k, half], B[2 + b][:, (k % 4) * P:(k % 4 + 1) * P],
                                      ps("norm2_g", l * KT + k, l * KT + k + 1), xh[:, k, half].bitcast(F32),
                                      ALU.mult, ALU.subtract)
                        ins.then_inc(gx_low, 1)

                def hidden(e, weight):
                    dve.wait_ge(m_silu, e + 1)
                    stt(hid[:, 0, :], gate[:, 0, :], weight, B[4][:, DE:2 * DE], ALU.mult, ALU.mult).then_inc(m_hid, 1)

                def low_part(e):
                    dve.wait_ge(m_high, e + 1)
                    tt(gl[:, 0, :, 0:P], B[6][:, 0:2 * P].rearrange("p (k s) -> p k s", k=2),
                       gh[:, 0, :, 0:P].bitcast(F32), ALU.subtract).then_inc(m_low, 1)

                def turn(e, c, off, weight, end=False, extra=None):
                    split(c + AHEAD, off)
                    if extra is not None:
                        extra()
                    low_part(e)
                    split(c + 1 + AHEAD, off)
                    hidden(e + 1, weight)
                    if not end:
                        split(c + 2 + AHEAD, off)

                def add(g):
                    for half in range(2):
                        dve.wait_ge(sc_done, 2 * (g0 + g) + half + 1)
                        for t in range(NT):
                            cols = slice(half * 512, half * 512 + 512)
                            ins = tt(h[:, t, cols], h[:, t, cols], B[((5, 7), (2, 3))[half][t]][:, :], ALU.add)
                        ins.then_inc(sc_read, 1)
                        dve.wait_ge(sc_read, 2 * (g0 + g) + half + 1)

                route(l, lambda: gathered(0))
                dve.wait_ge(comb_ready, l + 1)
                hidden(e0, comb[:, 0, 0:1])
                split(c0 + 1 + AHEAD)
                for g in range(NG):
                    c = c0 + 2 + 3 * EG * g
                    end = g == NG - 1
                    turn(e0 + EG * g, c, 0, comb[:, g, 1:2])
                    turn(e0 + EG * g + 1, c + 3, 0, comb[:, g, 2:3], False, (lambda: add(g - 1)) if g else None)
                    for b in range(2):
                        turn(e0 + EG * g + 2 + b, c + 6 + 3 * b, 0, comb[:, g, 3 + b:4 + b], False,
                             None if end else lambda: gathered(g + 1, (b,)))
                    with dve.Fori(4, EG - 1 - end) as i:
                        turn(i + (e0 + EG * g), c, i, comb[:, g, bass.ds(i + 1, 1)])
                    turn(e0 + EG * (g + 1) - 1 - end, c + 3 * (EG - 1 - end), 0,
                         comb[:, g, EG - 1:EG] if end else comb[:, g + 1, 0:1], end)
                overflow = dve.value_load(route_i[0:1, 0:1], min_val=0, max_val=1)
                low_part(e0 + NE - 1)
                split(c0 + 3 * NE - 2 + AHEAD)
                split(c0 + 3 * NE - 1 + AHEAD)
                add(NG - 1)

                with dve.If(overflow):
                    turn_is = over_turn[l]
                    for t in range(NT):
                        ins = ts(pick[:, t, 0, :], cs("slot"), rw[:, 7, t:t + 1], -float(P), ALU.subtract, ALU.is_equal)
                    ins.then_inc(turn_is, 1)
                    with dve.Fori(0, EG) as e:
                        dve.wait_ge(turn_is, e * 7 + 6)
                        stt(hid[:, 0, :], gate[:, 0, :], comb[:, 0, bass.ds(e, 1)], B[4][:, DE:2 * DE], ALU.mult, ALU.mult)\
                            .then_inc(turn_is, 1)
                    dve.wait_ge(turn_is, 5 + 7 * EG)
                    for half in range(2):
                        for t in range(NT):
                            cols = slice(half * 512, half * 512 + 512)
                            ins = tt(h[:, t, cols], h[:, t, cols], B[((5, 7), (2, 3))[half][t]][:, :], ALU.add)
                    ins.then_inc(turn_is, 1)
                    dve.wait_ge(turn_is, 6 + 7 * EG)
                nc.vector.engine_nop().then_inc(h_ready, 4)

            def gained(n, ready):
                dve.wait_ge(fg_in, 16 * ready)
                for t in range(NT):
                    dve.wait_ge(rstd_ready, 2 * n + t + 1)
                    stt(h[:, t, :], h[:, t, :], rstd[:, t:t + 1], fg[:, :], ALU.mult, ALU.mult).then_inc(h_ready, 2)

            nc.vector.memset(zero[:, :].bitcast(F32), 0.0).then_inc(zero_ready, 1)
            for t in range(NT):
                dve.wait_ge(x_in[t], 16)
            normed(0)
            split(C_FB)
            dve.wait_ge(head_in, 16)
            dve.wait_ge(small_in, 16)
            low(T_L0, xl, xh, lambda k: ps("attn_g", k, k + 1))
            split(1)
            split(AHEAD)
            for j in range(2):
                lo = SMALL["lam"][0] + 2 * j * HD
                link(nc.vector.tensor_tensor_reduce(lamw[:, :], sml[:, lo:lo + HD], sml[:, lo + HD:lo + 2 * HD], 1.0, 0.0,
                                                    ALU.mult, ALU.add, lamb[:, j:j + 1]))
            ts(gain_sub[:, :], ps("subln"), 1.0 - LAM_INIT, None, ALU.mult).then_inc(lam_sum, 1)
            dve.wait_ge(const_in, 16)
            dve.wait_ge(f_z, 1)
            stt(f_w[1], f_w[0], -1.0, f_w[0], ALU.mult, ALU.min).then_inc(f_neg, 1)
            link(ts(f_w[4], f_w[0], -1.0, 0.0, ALU.mult, ALU.max))
            dve.wait_ge(f_ln, 1)
            dve.wait_ge(f_neg, 1)
            link(tt(f_w[5], f_w[4], f_w[3], ALU.add))
            link(nc.vector.memset(f_w[2], 1.0))
            nc.vector.tensor_tensor_scan(f_w[4], f_w[2], f_w[5], 0.0, ALU.mult, ALU.add)\
                .then_inc(negc_ready, 1)

            def projections(c0, qk_first, kinds, start):
                for g in range(6):
                    c = c0 + 2 * g
                    split(c + AHEAD)
                    if g == 5:
                        start()
                    split(c + 1 + AHEAD)
                    if g < 4:
                        kinds(g, qk_first + g, c + 1, 2 * (g % 2))

            def kinds0(g, n, c, banks):
                if g < 2:
                    rope(n, c, banks, *(("cos_q", "sin_q"), ("cos_k", "sin_k"))[g])
                else:
                    scaled(n, c, banks, [(0, 512, HD ** -0.5 if g == 2 else 1.0)])

            def kinds1(g, n, c, banks):
                rope(n, c, banks, *(("cos_q", "sin_q"), ("cos_k", "sin_k"))[g % 2])

            start, rest = attention(0, 16, lambda a: "dilated" if a < 8 else "causal", 1.0, HD, False)
            projections(C_HYB, 0, kinds0, start)
            rest()
            nc.vector.engine_nop().then_inc(tok_ready, 2)
            low(T_L0O, xl, xh, one)
            out_projection(C_HYB_OUT)
            normed(1)
            low(T_F0, xl, xh, lambda k: ps("ffn_g", k, k + 1))
            split(C_FFN[0] - 1 + AHEAD)
            glu(0)

            normed(2)
            low(T_L1, xl, xh, lambda k: ps("attn_g", KT + k, KT + k + 1))
            dve.wait_ge(lam_exp, 1)
            link(tt(lamb[:, 5:6], lamb[:, 3:4], lamb[:, 2:3], ALU.subtract))
            link(ts(lamb[:, 6:7], lamb[:, 5:6], -LAM_INIT, None, ALU.add))
            start, rest = attention(16, 16, lambda a: "causal", 1.0, P, True, head_norms)
            projections(C_DIFF, 4, kinds1, start)
            rest()
            head_norms(17)
            low(T_L1O, xl, xh, lambda k: gain_sub[:, 0:1])
            out_projection(C_DIFF_OUT)
            normed(3)
            low(T_F1, xl, xh, lambda k: ps("ffn_g", KT + k, KT + k + 1))
            split(C_FFN[1] - 1 + AHEAD)
            glu(1)
            gained(4, 1)

            for l in range(LAYERS):
                c0 = C_LAYER[l]
                n = 8 + 5 * l
                normed(5 + 2 * l)
                low(t_layer(l, 0), xl, xh, lambda k: ps("norm1_g", l * KT + k, l * KT + k + 1))
                plain(c0, 4)
                dve.wait_ge(c_rstd_ready, l + 1)
                for t in range(NT):
                    ts(c_tok[:, t, 0:256], B[t][:, 0:256], crs[:, 2 * t:2 * t + 1], None, ALU.mult)
                    ts(c_tok[:, t, 256:384], B[t][:, 256:384], crs[:, 2 * t + 1:2 * t + 2], None, ALU.mult)
                    kr = B[t][:, 384:416]
                    tt(rope_a[:, t, 0:32], kr, cs("cos_m", 32 * t, 32 * t + 32), ALU.mult)
                    tt(rope_b[:, t, 0:16], kr[:, 16:32], cs("sin_m", 32 * t, 32 * t + 16), ALU.mult)
                    link(tt(rope_b[:, t, 16:32], kr[:, 0:16], cs("sin_m", 32 * t + 16, 32 * t + 32), ALU.mult))
                    tt(kr_tok[:, t, :], rope_a[:, t, 0:32], rope_b[:, t, 0:32], ALU.add).then_inc(c_tok_ready, 1)
                scaled(n, c0 + 3, 2, [(0, 256, HD ** -0.5), (256, 512, 1.0)])
                low(t_layer(l, 1), cl, ch, lambda k: ps("c_g", l * 3 + k, l * 3 + k + 1))

                def stick_masked(first):
                    for i in range(first, first + 2):
                        dve.wait_ge(z_done, 4 * l + i + 1)
                        link(tt(zm[:, i, :], B[4 + i % 2][:, 0:384], cs("strict"), ALU.add))
                        stt(sw[:, i, :], zm[:, i, :], -1.0, zm[:, i, :], ALU.mult, ALU.min).then_inc(na_ready, 1)

                def mla_rotated(i):
                    first = MLA_BANKS[i]
                    for t in range(NT):
                        dve.wait_ge(mla_q_copied, 8 * l + 2 * i + t + 1)
                        src = B[first + t][:, 0:384].rearrange("p (a d) -> p a d", a=4)
                        a = rope_a[:, t, 0:128].rearrange("p (a d) -> p a d", a=4)
                        b = rope_b[:, t, 0:128].rearrange("p (a d) -> p a d", a=4)
                        co = cs("cos_m", 32 * t, 32 * t + 32).unsqueeze(1).broadcast_to([P, 4, 32])
                        si = cs("sin_m", 32 * t, 32 * t + 32).unsqueeze(1).broadcast_to([P, 4, 32])
                        tt(a, src[:, :, 64:96], co, ALU.mult)
                        tt(b[:, :, 0:16], src[:, :, 80:96], si[:, :, 0:16], ALU.mult)
                        link(tt(b[:, :, 16:32], src[:, :, 64:80], si[:, :, 16:32], ALU.mult))
                        tt(mla_tok[i][:, t, :].rearrange("p (a d) -> p a d", a=4)[:, :, 64:96], a, b, ALU.add)\
                            .then_inc(qk_tok_ready, 1)

                def mla_shared(i):
                    for t in range(NT):
                        dve.wait_ge(mla_q_copied, 8 * l + 4 + 2 * i + t + 1)
                        nc.vector.tensor_copy(mla_tok[i][:, t, :].rearrange("p (a d) -> p a d", a=4)[:, :, 64:96],
                                              kr_tok[:, t, :].unsqueeze(1).broadcast_to([P, 4, 32]))\
                            .then_inc(qk_tok_ready, 1)

                def stick_minus(first):
                    for i in range(first, first + 2):
                        dve.wait_ge(cum_done, 4 * l + i + 1)
                        tt(zm[:, i, :], zm[:, i, :], B[4 + i % 2][:, 0:384], ALU.subtract).then_inc(d_ready, 1)

                split(c0 + 4 + AHEAD)
                split(c0 + 5 + AHEAD)
                stick_masked(0)
                mla_rotated(0)
                stick_masked(2)
                mla_rotated(1)
                for i in range(4):
                    dve.wait_ge(ln_ready, 4 * l + i + 1)
                    stt(sw[:, i, :], zm[:, i, :], 0.0, sw[:, i, :], ALU.max, ALU.add).then_inc(sp_ready, 1)
                mla_shared(0)
                stick_minus(0)
                mla_shared(1)
                stick_minus(2)

                def other_outputs(a):
                    if a == 6:
                        dve.wait_ge(pool_y, l + 1)
                        scale = ps("pool_scale", l * 256, l * 256 + 256).unsqueeze(1).broadcast_to([P, NT, 256])
                        tt(tok[:, :, 768:1024], B[6][:, :].rearrange("p (t d) -> p t d", t=NT), scale, ALU.mult)
                        dve.wait_ge(spv_done, l + 1)
                        nc.vector.tensor_copy(tok[:, :, 512:768], B[7][:, :].rearrange("p (t d) -> p t d", t=NT))

                start, rest = attention(32 + 8 * l, 8, lambda a: "chunked", MLA_SCALE, HD, False, other_outputs, 2, 0)
                start()
                rest()
                nc.vector.engine_nop().then_inc(tok_ready, 2)
                split(c0 + C_OUT2)
                low(t_layer(l, 2), xl, xh, one)
                split(c0 + C_OUT2 + 1)
                dve.wait_ge(router_high, l + 1)
                tt(router_wl[:, :], router_raw, router_wh[:, :].bitcast(F32), ALU.subtract).then_inc(router_low, 1)
                out_projection(c0 + C_OUT2)
                normed(6 + 2 * l)
                low(t_layer(l, 3), xl, xh, lambda k: ps("norm2_g", l * KT + k, l * KT + k + 1))
                plain(c0 + C_MOE - 1, 2)
                moe(l)
            gained(9, 2)

        @block.tensor
        def _(pe):
            mm = nc.tensor.matmul

            def product(o, ah, al, bh, bl, start, stop, **kw):
                mm(o, ah, bh, start=start, stop=False, **kw)
                mm(o, ah, bl, start=False, stop=False, **kw)
                return mm(o, al, bh, start=False, stop=stop, **kw)

            def group(c0, n, banks, width, q=None, done=None):
                kt = KT // n
                for j in range(n):
                    u = (c0 + j) % RING
                    pe.wait_ge(w_low, c0 + j + 1)
                    for t in range(NT):
                        for kk in range(kt):
                            k = j * kt + kk
                            if q is not None and t == 0:
                                pe.wait_ge(t_low, T_BASE[q] + k + 1)
                            ins = product(banks[t], xh[:, k, t * P:(t + 1) * P], xl[:, k, t * P:(t + 1) * P],
                                          wh[:, u, kk * width:(kk + 1) * width], wl[:, u, kk * width:(kk + 1) * width],
                                          k == 0, k == KT - 1)
                        if done is not None and j == n - 1 and t < NT - 1:
                            ins.then_inc(done, 1)
                    ins.then_inc(chunk_used, 1)
                    yield j

            def narrow(high, low, width, o, q):
                for k in range(KT):
                    lo = k * width
                    pe.wait_ge(t_low, T_BASE[q] + k + 1)
                    ins = product(o[0:width, 0:S], high[:, lo:lo + width], low[:, lo:lo + width], xh[:, k, :], xl[:, k, :],
                                  k == 0, k == KT - 1)
                return ins

            def run(steps):
                for _ in steps:
                    pass

            def normed_transposes(q):
                n = toks[0]
                toks[0] += 3
                pe.wait_ge(tok_ready, n + 1)
                for t in range(NT):
                    for b in range(4):
                        if t and b % 2 == 0:
                            pe.wait_ge(tok_ready, n + 2 + b // 2)
                        first = 4 * (b // 2) + b % 2
                        for k in (first, first + 2):
                            at = t_place(k)[1] * S + t * P
                            ins = nc.tensor.transpose(B[4 + b][:, at:at + P], tok[:, t, k * P:(k + 1) * P], ident)
                        if t:
                            ins.then_inc(t_done, 1)

            def transposes(q, src, need, nk=KT, sem=None):
                pe.wait_ge(tok_ready if sem is None else sem, need)
                for b in range(T_BANKS[q]):
                    for k in (k for k in range(nk) if t_place(k)[0] == b):
                        for t in range(NT):
                            at = t_place(k)[1] * S + t * P
                            ins = nc.tensor.transpose(B[4 + b][:, at:at + P], src[:, t, k * P:(k + 1) * P], ident)
                    ins.then_inc(t_done, 1)

            def ready(q):
                pe.wait_ge(t_low, T_BASE[q + 1])

            def qk_transposes(n, width=P, src=qk_tok):
                for t in range(NT):
                    pe.wait_ge(qk_tok_ready, 2 * n + t + 1)
                    if n:
                        pe.wait_ge(qkT_ready, 2 * (n - 1) + t + 1)
                    for j in range(4):
                        ins = nc.tensor.transpose(B[6 + t][0:width, j * P:(j + 1) * P],
                                                  src[:, t, j * width:(j + 1) * width], ident)
                    ins.then_inc(qk_tr, 1)

            def projections(c0, n0, q, start):
                for g in range(6):
                    if g == 1:
                        pe.wait_ge(f_z, 1)
                    if g in (2, 3):
                        pe.wait_ge(qk_tok_ready, 2 * (n0 + g - 2) + 2)
                    if g in (4, 5):
                        pe.wait_ge(qk_tok_ready, 2 * (n0 + g - 2) + 2)
                    b = 2 * (g % 2)
                    for j in group(c0 + 2 * g, 2, [B[b][:, :], B[b + 1][:, :]], 512, q if g == 0 else None):
                        if j == 0 and 1 <= g <= 4:
                            qk_transposes(n0 + g - 1)
                        if j == 0 and g == 5:
                            pe.wait_ge(qkT_ready, 2 * (n0 + 4))
                            pe.wait_ge(v_ready, n0 + 2)
                            start()

            def attention(first, n, operands, v_of, dv, forget=None, between=None, score_bank=0, turned_bank=6):
                def scores(a):
                    if a >= 2:
                        pe.wait_ge(nm_ready, first + a - 1)
                    o = B[score_bank + a % 2]
                    q, k = operands(a)
                    f = forget(a) if forget else None
                    for lo, hi, t in ((0, 128, 0), (128, 384, 1)):
                        ins = mm(o[:, lo:hi], q[:, t * P:(t + 1) * P], k[:, 0:hi - lo], start=True, stop=f is None)
                        if f is not None:
                            ins = mm(o[:, lo:hi], f, f_w[4][:, 0:hi - lo], start=False, stop=True)
                    ins.then_inc(s_done, 1)

                def turn(a):
                    pe.wait_ge(p_ready, first + a + 1)
                    if a >= 2:
                        pe.wait_ge(pT_ready, first + a - 1)
                    for j in range(3):
                        ins = nc.tensor.transpose(B[turned_bank + a % 2][:, j * P:(j + 1) * P], pr[:, a % 2, j * P:(j + 1) * P], ident)
                    ins.then_inc(p_tr, 1)

                def values(a):
                    pe.wait_ge(pT_ready, first + a + 1)
                    if a >= 2:
                        pe.wait_ge(o_done, first + a - 1)
                    z = B[4 + a % 2]
                    pt = prT[:, a % 2, :]
                    mm(z[:, 0:dv], pt[:, 0:P], v_of(a, 0), start=True, stop=True)
                    mm(z[:, dv:2 * dv], pt[:, P:2 * P], v_of(a, 0), start=True, stop=False)
                    mm(z[:, dv:2 * dv], pt[:, 2 * P:3 * P], v_of(a, 1), start=False, stop=True).then_inc(pv_done, 1)

                def start():
                    scores(0)
                    scores(1)

                def rest():
                    turn(0)
                    for a in range(n):
                        if a + 2 < n:
                            scores(a + 2)
                        if between is not None:
                            between(a)
                        if a + 1 < n:
                            turn(a + 1)
                        values(a)

                return start, rest

            def out_projection(c0, q):
                for half in range(2):
                    run(group(c0 + 2 * half, 2, [B[2 * half][:, :], B[2 * half + 1][:, :]], 512, None if half else q,
                              bank_done))

            def clear():
                for i in range(4):
                    for j in range(4):
                        mm(B[i][:, j * P:(j + 1) * P], zero[:, :], zero[:, :], start=True, stop=False, skip_group_check=True)

            def down(c, off, buf, last):
                u = c % RING
                pe.wait_ge(w_low, off * RING + (c + 1))
                for t in range(NT):
                    for half in range(2):
                        for k in range(2):
                            lo = k * D + half * 512
                            ins = product(B[2 * half + t][:, :], gh[:, buf, k, t * P:(t + 1) * P],
                                          gl[:, buf, k, t * P:(t + 1) * P], wh[:, u, lo:lo + 512], wl[:, u, lo:lo + 512],
                                          False, last and k == 1, skip_group_check=True)
                        if last and not (t and half):
                            ins.then_inc(bank_done, 1)
                ins.then_inc(chunk_used, 1)

            def glu(l):
                c0 = C_FFN[l]
                f0 = l * FT

                def up(fi, u, c, off, q=None):
                    if u is not None and (not isinstance(off, int) or c >= c0 + 2):
                        pe.wait_ge(hid_ready, fi - 1)
                    s = c % RING
                    pe.wait_ge(w_low, off * RING + (c + 1))
                    for g in range(2):
                        for k in range(KT):
                            lo = k * 2 * P + g * P
                            if q is not None and g == 0:
                                pe.wait_ge(t_low, T_BASE[q] + max(k, 2) + 1)
                            ins = product(B[4 + u][:, g * S:(g + 1) * S], wh[:, s, lo:lo + P], wl[:, s, lo:lo + P],
                                          xh[:, k, :], xl[:, k, :], k == 0, k == KT - 1)
                    ins.then_inc(chunk_used, 1)

                clear()
                up(f0, 0, c0, 0, (T_F0, T_F1)[l])
                up(f0 + 1, 1, c0 + 1, 0)
                with pe.Fori(0, (NFB - 1) // 2) as i:
                    for j in range(2):
                        c = c0 + 2 + 3 * j
                        for u in range(2):
                            up(i * 4 + (f0 + 2 + 2 * j + u), u, c + u, i * 2)
                        pe.wait_ge(g_low, i * 4 + (f0 + 2 * j + 2))
                        down(c + 2, i * 2, j, False)
                pe.wait_ge(g_low, f0 + FT)
                down(c0 + 3 * NFB - 1, 0, 0, True)

            def moe(l):
                c0 = C_LAYER[l] + C_MOE
                e0, g0 = l * NE, l * NG

                def gather(g, halves=(0, 1)):
                    if g >= 1:
                        pe.wait_ge(gx_low, 2 * (g0 + g))
                    if g >= 2:
                        pe.wait_ge(sc_read, 2 * (g0 + g - 1))
                    for b in halves:
                        for k in range(4 * b, 4 * b + 4):
                            for t in range(NT):
                                ins = mm(B[2 + b][:, (k % 4) * P:(k % 4 + 1) * P], tok[:, t, k * P:(k + 1) * P],
                                         pick[:, t, g, :], start=t == 0, stop=t == NT - 1)
                        ins.then_inc(gx_done, 1)

                def scatter(g):
                    for half in range(2):
                        pe.wait_ge(ys_ready, 2 * (g0 + g) + half + 1)
                        if half:
                            pe.wait_ge(gx_low, 2 * min(g0 + NG, g0 + g + 2))
                        for t in range(NT):
                            ins = mm(B[((5, 7), (2, 3))[half][t]][:, :], spread[:, g, t * P:(t + 1) * P],
                                     ys[:, half * 512:(half + 1) * 512], start=True, stop=True)
                        ins.then_inc(sc_done, 1)

                def clear_sums():
                    for half in range(2):
                        for j in range(4):
                            mm(B[half][:, j * P:(j + 1) * P], zero[:, :], zero[:, :], start=True, stop=False,
                               skip_group_check=True)

                def up(e, c, off, g, between=None):
                    for j in range(2):
                        s = (c + j) % RING
                        pe.wait_ge(w_low, off * RING + (c + j + 1))
                        if e is None:
                            pe.wait_ge(gx_low, 2 * g0 + j + 1)
                        elif j == 0:
                            pe.wait_ge(m_hid, e)
                        for kk in range(4):
                            k = 4 * j + kk
                            x_of = slice((g % 2) * P, (g % 2 + 1) * P)
                            ins = product(B[4][:, :], xh[:, k, x_of], xl[:, k, x_of],
                                          wh[:, s, kk * 512:(kk + 1) * 512], wl[:, s, kk * 512:(kk + 1) * 512],
                                          k == 0, k == KT - 1)
                        ins.then_inc(chunk_used, 1)
                        if j == 0 and between is not None:
                            between()

                def turn_hid(e):
                    pe.wait_ge(m_hid, e + 1)
                    for k in range(2):
                        ins = nc.tensor.transpose(B[6][:, k * P:(k + 1) * P], hid[:, 0, k * P:(k + 1) * P], ident)
                    ins.then_inc(m_tr, 1)

                def down_sums(e, c, off, last):
                    u = c % RING
                    pe.wait_ge(m_low, e + 1)
                    pe.wait_ge(w_low, off * RING + (c + 1))
                    for half in range(2):
                        for k in range(2):
                            lo = k * D + half * 512
                            ins = product(B[half][:, :], gh[:, 0, k, 0:P], gl[:, 0, k, 0:P], wh[:, u, lo:lo + 512],
                                          wl[:, u, lo:lo + 512], False, last and k == 1, skip_group_check=True)
                        if last and half == 0:
                            ins.then_inc(sums_half, 1)
                    ins.then_inc(chunk_used, 1)

                def turn(e, c, off, g, last=False, first=None):
                    up(e + 1, c, off, g, lambda: turn_hid(e))
                    if first is not None:
                        if first:
                            pe.wait_ge(ys_ready, 2 * (g0 + first))
                        clear_sums()
                    down_sums(e, c + 2, off, last)

                pe.wait_ge(goh_ready, l + 1)
                hot = [rw[:, 5, t * NG:(t + 1) * NG] for t in range(NT)]
                o = B[0]
                mm(o[:, 128:132], cs("before"), hot[0], start=True, stop=True)
                mm(o[:, 132:136], cs("ones"), hot[0], start=True, stop=False)
                mm(o[:, 132:136], cs("before"), hot[1], start=False, stop=True)
                mm(o[:, 136:140], cs("ones"), hot[0], start=True, stop=False)
                mm(o[:, 136:140], cs("ones"), hot[1], start=False, stop=True).then_inc(place_done, 1)
                pe.wait_ge(pick_ready, g0 + 1)
                gather(0)

                def shares():
                    pe.wait_ge(pick_ready, g0 + NG)
                    for g in range(NG):
                        for t in range(NT):
                            at = (g % 2) * S + t * P
                            ins = nc.tensor.transpose(B[5 + g // 2][:, at:at + P], pick[:, t, g, :], ident)
                    ins.then_inc(spread_done, 1)
                    pe.wait_ge(share_ready, l + 1)
                    for g in range(NG):
                        for t in range(NT):
                            ins = mm(o[:, g * EG:(g + 1) * EG], pick[:, t, g, :], rw[:, 22, t * EG:(t + 1) * EG],
                                     start=t == 0, stop=t == NT - 1)
                    ins.then_inc(comb_done, 1)

                up(None, c0, 0, 0, shares)
                pe.wait_ge(spread_ready, l + 1)
                for g in range(NG):
                    c = c0 + 2 + 3 * EG * g
                    end = g == NG - 1
                    turn(e0 + EG * g, c, 0, g, first=g)
                    if g:
                        scatter(g - 1)
                    for b in range(2):
                        turn(e0 + EG * g + 1 + b, c + 3 + 3 * b, 0, g)
                        if not end:
                            gather(g + 1, (b,))
                    with pe.Fori(3, EG - 1) as i:
                        turn(i + (e0 + EG * g), c, i, g)
                    if not end:
                        pe.wait_ge(gx_low, 2 * (g0 + g + 2))
                        turn(e0 + EG * (g + 1) - 1, c + 3 * (EG - 1), 0, g + 1, True)
                overflow = pe.value_load(route_i[0:1, 0:1], min_val=0, max_val=1)
                turn_hid(e0 + NE - 1)
                down_sums(e0 + NE - 1, c0 + 3 * NE - 1, 0, True)
                scatter(NG - 1)

                with pe.If(overflow):
                    turn_is = over_turn[l]
                    pe.wait_ge(turn_is, 1)
                    clear_sums()
                    for k in range(KT):
                        for t in range(NT):
                            mm(B[2 + k // 4][:, (k % 4) * P:(k % 4 + 1) * P], tok[:, t, k * P:(k + 1) * P],
                               pick[:, t, 0, :], start=t == 0, stop=t == NT - 1)
                    for t in range(NT):
                        nc.tensor.transpose(B[6][:, t * P:(t + 1) * P], pick[:, t, 0, :], ident)
                    for t in range(NT):
                        ins = mm(B[7][:, 0:EG], pick[:, t, 0, :], rw[:, 22, t * EG:(t + 1) * EG], start=t == 0, stop=t == NT - 1)
                    ins.then_inc(turn_is, 1)
                    pe.wait_ge(turn_is, 3)
                    with pe.Fori(0, EG) as e:
                        for j in range(2):
                            pe.wait_ge(over_in[l], e * 48 + 16 * (j + 1))
                            for kk in range(4):
                                k = 4 * j + kk
                                ins = mm(B[4][:, :], x_over[:, k, :], chunk_over[:, kk * 512:(kk + 1) * 512],
                                         start=k == 0, stop=k == KT - 1)
                            ins.then_inc(turn_is, 1)
                        pe.wait_ge(turn_is, e * 7 + 7)
                        for k in range(2):
                            ins = nc.tensor.transpose(B[6][:, k * P:(k + 1) * P], hid[:, 0, k * P:(k + 1) * P], ident)
                        ins.then_inc(turn_is, 1)
                        pe.wait_ge(turn_is, e * 7 + 9)
                        pe.wait_ge(over_in[l], e * 48 + 48)
                        for half in range(2):
                            for k in range(2):
                                lo = k * D + half * 512
                                ins = mm(B[half][:, :], hid_over[:, k * P:(k + 1) * P], chunk_over[:, lo:lo + 512],
                                         start=False, stop=k == 1, skip_group_check=True)
                        ins.then_inc(turn_is, 1)
                    pe.wait_ge(turn_is, 4 + 7 * EG)
                    for half in range(2):
                        for t in range(NT):
                            ins = mm(B[((5, 7), (2, 3))[half][t]][:, :], spread[:, 0, t * P:(t + 1) * P],
                                     ys[:, half * 512:(half + 1) * 512], start=True, stop=True)
                    ins.then_inc(turn_is, 1)

            pe.wait_ge(head_in, 16)
            pe.wait_ge(zero_ready, 1)
            toks = [0]

            def tokens_ready():
                toks[0] += 2
                return toks[0]

            normed_transposes(T_L0)
            pe.wait_ge(w_low, C_FB + 1)
            narrow(wh[:, C_FB, :], wl[:, C_FB, :], 8, B[2], T_L0).then_inc(chunk_used, 1)

            def head_rows(a):
                r = (a % 2) * HD
                return qT[r:r + HD, a // 2, :], kT[r:r + HD, a // 2, :]

            def hybrid_heads(a):
                if a == 8:
                    pe.wait_ge(negc_ready, 1)
                return head_rows(a)

            start, rest = attention(0, 16, hybrid_heads, lambda a, t: v[:, t, a * HD:(a + 1) * HD], HD,
                                    lambda a: ident[0:8, a - 8:a - 7].broadcast_to([8, P]) if a >= 8 else None)
            projections(C_HYB, 0, None, start)
            pe.wait_ge(v_ready, 4)
            rest()
            pe.wait_ge(const_in, 16)
            transposes(T_L0O, tok, tokens_ready())
            out_projection(C_HYB_OUT, T_L0O)
            normed_transposes(T_F0)
            glu(0)

            normed_transposes(T_L1)
            start, rest = attention(16, 16, head_rows, lambda a, t: v[:, t, (a // 2) * P:(a // 2 + 1) * P], P)
            projections(C_DIFF, 4, T_L1, start)
            pe.wait_ge(v_ready, 8)
            rest()
            transposes(T_L1O, tok, tokens_ready())
            out_projection(C_DIFF_OUT, T_L1O)
            normed_transposes(T_F1)
            glu(1)

            for l in range(LAYERS):
                c0 = C_LAYER[l]
                n = 8 + 5 * l
                vr = 8 + 6 * l
                normed_transposes(t_layer(l, 0))
                run(group(c0, 2, [B[0][:, 0:G0W], B[1][:, 0:G0W]], G0W, t_layer(l, 0)))
                run(group(c0 + 2, 2, [B[2][:, :], B[3][:, :]], G1W))
                pe.wait_ge(c_tok_ready, 2 * l + 2)
                for j in group(c0 + 4, 2, [B[0][:, :], B[1][:, :]], G2W):
                    if j == 0:
                        transposes(t_layer(l, 1), c_tok, 2 * l + 2, 3, c_tok_ready)
                        qk_transposes(n)
                ready(t_layer(l, 1))

                def stick_scores(first):
                    for i in range(first, first + 2):
                        if i >= 2:
                            pe.wait_ge(na_ready, 4 * l + i - 1)
                        b = B[4 + i % 2]
                        r = (i % 2) * HD
                        q, k = sT[r:r + HD, i // 2, :], sT[r:r + HD, 2 + i // 2, :]
                        mm(b[:, 0:S], k[:, 0:P], q, start=True, stop=True)
                        mm(b[:, S:384], k[:, P:S], q[:, P:S], start=True, stop=True).then_inc(z_done, 1)

                def stick_sums(first):
                    for i in range(first, first + 2):
                        pe.wait_ge(sp_ready, 4 * l + i + 1)
                        if i >= 2:
                            pe.wait_ge(d_ready, 4 * l + i - 1)
                        o = B[4 + i % 2]
                        mm(o[:, 0:S], cs("upper"), sw[:, i, 0:S], start=True, stop=False, skip_group_check=True)
                        mm(o[:, P:S], cs("ones"), sw[:, i, S:384], start=False, stop=True, skip_group_check=True)
                        mm(o[:, S:384], cs("upper"), sw[:, i, S:384], start=True, stop=True, skip_group_check=True)\
                            .then_inc(cum_done, 1)

                def latent_q(g):
                    u = (c0 + C_UQ) % RING
                    for t in range(NT):
                        for k in range(2):
                            lo = k * 768 + g * 384
                            ins = product(B[MLA_BANKS[g] + t][:, 0:384], ch[:, k, t * P:(t + 1) * P],
                                          cl[:, k, t * P:(t + 1) * P], wh[:, u, lo:lo + 384], wl[:, u, lo:lo + 384],
                                          k == 0, k == 1)
                    ins.then_inc(chunk_used if g else mla_group, 1)

                def latent_kv(g):
                    u = (c0 + C_UKV) % RING
                    pe.wait_ge(qk_tok_ready, 2 * (n + 1 + g) + 2)
                    for t in range(NT):
                        lo = g * 512
                        ins = product(B[MLA_BANKS[g] + t][:, :], ch[:, 2, t * P:(t + 1) * P], cl[:, 2, t * P:(t + 1) * P],
                                      wh[:, u, lo:lo + 512], wl[:, u, lo:lo + 512], True, True)
                    ins.then_inc(chunk_used if g else mla_group, 1)

                pe.wait_ge(w_low, c0 + C_UQ + 1)
                pe.wait_ge(qk_tok_ready, 2 * n + 2)
                latent_q(0)
                pe.wait_ge(qkT_ready, 2 * n + 2)
                stick_scores(0)
                pe.wait_ge(v_ready, vr + 2)
                latent_q(1)
                stick_scores(2)
                qk_transposes(n + 1, MLA_QK, mla_tok[0])
                pe.wait_ge(w_low, c0 + C_UKV + 1)
                latent_kv(0)
                qk_transposes(n + 2, MLA_QK, mla_tok[1])
                latent_kv(1)
                stick_sums(0)
                qk_transposes(n + 3, MLA_QK, mla_tok[0])
                stick_sums(2)

                def other_mixers(a):
                    if a == 0:
                        pe.wait_ge(qkT_ready, 2 * (n + 5))
                        for g in range(4):
                            o = B[6 + g // 2][0:HD, (g % 2) * S:(g % 2 + 1) * S]
                            col = 768 + g * HD
                            mm(o, v[:, 0, col:col + HD], cs("pool", g * 384, g * 384 + S), start=True, stop=False,
                               skip_group_check=True)
                            ins = mm(o[:, P:S], v[:, 1, col:col + HD], cs("pool", g * 384 + S, (g + 1) * 384),
                                     start=False, stop=True, skip_group_check=True)
                        ins.then_inc(pool_d, 1)
                    if a == 3:
                        pe.wait_ge(pool_dT, l + 1)
                        for t in range(NT):
                            for g in range(4):
                                lo = SMALL["pool_w"][0] + (l * 4 + g) * HD
                                at = t * S + g * HD
                                ins = mm(B[6][:, at:at + HD], dT[:, g, t * P:(t + 1) * P], sml[0:HD, lo:lo + HD],
                                         start=True, stop=True)
                        ins.then_inc(pool_y, 1)
                        for i in range(4):
                            pe.wait_ge(a_ready, 4 * l + i + 1)
                            lo, col = i * HD, 512 + i * HD
                            z0, z1 = (B[7][:, t * S + lo:t * S + lo + HD] for t in range(NT))
                            mm(z0, zm[:, i, 0:P], v[:, 0, col:col + HD], start=True, stop=True)
                            mm(z1, zm[:, i, P:S], v[:, 0, col:col + HD], start=True, stop=False)
                            ins = mm(z1, zm[:, i, S:384], v[:, 1, col:col + HD], start=False, stop=True)
                        ins.then_inc(spv_done, 1)

                def latent_heads(a):
                    if a in (0, 4):
                        pe.wait_ge(qkT_ready, 2 * (n + (4 if a == 0 else 5)))
                    return qT[0:MLA_QK, a, :], kT[0:MLA_QK, a, :]

                start, rest = attention(32 + 8 * l, 8, latent_heads, lambda a, t: v[:, t, a * HD:(a + 1) * HD], HD, None,
                                        other_mixers, 2, 0)
                start()
                qk_transposes(n + 4, MLA_QK, mla_tok[1])
                pe.wait_ge(v_ready, vr + 6)
                rest()
                transposes(t_layer(l, 2), tok, tokens_ready())
                out_projection(c0 + C_OUT2, t_layer(l, 2))
                normed_transposes(t_layer(l, 3))
                n = NG + NE
                pe.wait_ge(router_low, l + 1)
                narrow(router_wh, router_wl, n, B[0], t_layer(l, 3)).then_inc(r_products, 1)
                pe.wait_ge(r_biased, l + 1)
                for t in range(NT):
                    ins = nc.tensor.transpose(B[0][:, S + t * n:S + (t + 1) * n], rT[:, t * P:(t + 1) * P], ident[0:n, 0:n])
                ins.then_inc(r_done, 1)
                moe(l)

        @block.sync
        def _(sync):
            sync.wait_ge(h_ready, 20)
            sync.dma_start(fg[:, :], fgain[1]).then_inc(fg_in, 16)
            for t in range(NT):
                sync.wait_ge(h_ready, 38 + 2 * t)
                sync.dma_start(out[t * P:(t + 1) * P, :], h[:, t, :]).then_inc(out_done, 16)
            sync.wait_ge(out_done, 16 * NT)




def _constants():
    f = np.float32
    con = np.zeros((P, CONST_N), f)

    def put(name, a):
        lo, hi = CONST[name]
        con[0:a.shape[0], lo:hi] = a.reshape(a.shape[0], hi - lo)

    i = np.arange(P)
    put("ident", np.eye(P, dtype=f))
    put("upper", (i[:, None] >= i[None, :]).astype(f))
    put("ones", np.ones((P, P), f))
    t, s = np.arange(S)[:, None], np.arange(S)[None, :]
    lag = t - s

    def packed(m):
        return np.concatenate([m[0:P, 0:P], m[P:S, 0:S]], axis=1)

    count = sum(((lag >= 0) & (lag % d == 0) & (lag <= w)).astype(np.int64) for w, d in ((128, 1), (512, 4), (2048, 16)))
    put("dilated", packed(np.where(count > 0, np.log(np.maximum(count, 1)), NEG).astype(f)))
    put("causal", packed(np.where(lag >= 0, 0.0, NEG).astype(f)))
    put("chunked", packed(np.where(s // 64 <= t // 64, 0.0, NEG).astype(f)))
    strict = np.where(lag > 0, 0.0, NEG).astype(f).T
    put("strict", np.concatenate([strict[0:P, 0:S], strict[P:S, P:S]], axis=1))

    def tokens(a):
        return a.reshape(NT, P, -1).transpose(1, 0, 2)

    inv = (f(1.0) / (f(10000.0) ** (np.arange(0, HD, 2, dtype=f) / f(HD)))).astype(f)
    ang = np.arange(S, dtype=f)[:, None] * inv[None, :]
    cos, sin = np.cos(ang).astype(f), np.sin(ang).astype(f)
    cos, sin = np.concatenate([cos, cos], 1), np.concatenate([-sin, sin], 1)
    put("cos_q", tokens(cos * f(HD ** -0.5)))
    put("sin_q", tokens(sin * f(HD ** -0.5)))
    put("cos_k", tokens(cos))
    put("sin_k", tokens(sin))
    inv = (f(10000.0) ** (-np.arange(0, 32, 2, dtype=f) / f(32))).astype(f)
    ang = np.arange(S, dtype=f)[:, None] * inv[None, :]
    cos, sin = np.cos(ang).astype(f), np.sin(ang).astype(f)
    put("cos_m", tokens(np.concatenate([cos, cos], 1)))
    put("sin_m", tokens(np.concatenate([-sin, sin], 1)))
    pools = []
    for w in (2, 4, 8, 16):
        m = np.where((lag >= 0) & (lag < w), 1.0 / np.minimum(t + 1, w), 0.0) - np.eye(S)
        m = m.T.astype(f)
        pools.append(np.concatenate([m[0:P, 0:S], m[P:S, P:S]], axis=1))
    put("pool", np.stack(pools, axis=1))
    put("iota", np.tile(np.arange(8, dtype=f), (P, 1)))
    put("iota64", np.tile(np.arange(8, dtype=f) - 64, (P, 1)))
    put("minus_half", np.full((P, 16), -0.5, f))
    put("before", (i[:, None] < i[None, :]).astype(f))
    put("slot", np.tile(np.arange(P, dtype=f), (P, 1)))
    e = np.arange(EG, dtype=f)
    put("chunk_of", np.tile(np.concatenate([3 * e - 1, 3 * e, 3 * e + 4]), (P, 1)))
    put("inv_c", np.tile(np.array([1 / 256, 1 / 128] * 2, f), (P, 1)))
    return con


def _stream(a):
    out = np.zeros((NCHUNK, P, CH), np.float32)

    def tiles(w):
        return w.reshape(-1, P, w.shape[1]).transpose(1, 0, 2)

    def put(c, part):
        part = part.reshape(P, -1)
        out[c, :, 0:part.shape[1]] = part

    def columns(c, w, groups):
        for lo, hi in groups:
            k = tiles(w[:, lo:hi])
            put(c, k[:, 0:4])
            put(c + 1, k[:, 4:8])
            c += 2

    halves = [(0, 512), (512, 1024)]
    w = a["hyb_w_in"][0]
    put(C_FB, tiles(w[:, 3072:3080]))
    columns(C_HYB, w, [(lo, lo + 512) for lo in (0, 512, 1536, 2048, 1024, 2560)])
    columns(C_HYB_OUT, a["hyb_w_out"][0], halves)
    columns(C_DIFF, a["diff_w_qkv"][0], [(lo, lo + 512) for lo in (0, 1024, 512, 1536, 2048, 2560)])
    columns(C_DIFF_OUT, a["diff_w_out"][0], halves)

    def up_at(c0, j):
        return c0 if j == 0 else c0 + 3 * j - 1

    def down_at(c0, j, n):
        return c0 + 3 * j + 4 if j < n - 1 else c0 + 3 * n - 1

    for l in range(LAYERS):
        up, down = a["ffn_w_up"][l], a["ffn_w_down"][l]
        for j in range(NFB):
            for u in range(2):
                f = (2 * j + u) * P
                put(up_at(C_FFN[l], j) + u, np.stack([tiles(up[:, f:f + P]), tiles(up[:, DFF + f:DFF + f + P])], axis=2))
            put(down_at(C_FFN[l], j, NFB), tiles(down[2 * j * P:(2 * j + 2) * P]))
        c0 = C_LAYER[l]
        columns(c0 + C_IN2, a["w_in_2"][l], [(0, 416), (416, 928), (928, 1440)])
        put(c0 + C_UQ, tiles(a["w_uq_2"][l]))
        put(c0 + C_UKV, tiles(a["w_ukv_2"][l]))
        columns(c0 + C_OUT2, a["w_out_2"][l], halves)
        for e in range(NE):
            gate, up, down = (a[k][l, e // EG, e % EG] for k in ("w_gate_2", "w_up_2", "w_down_2"))
            both = np.concatenate([tiles(gate), tiles(up)], axis=2)
            c = up_at(c0 + C_MOE, e)
            put(c, both[:, 0:4])
            put(c + 1, both[:, 4:8])
            put(down_at(c0 + C_MOE, e, NE), tiles(down))
    return out


def _router(a):
    w = np.concatenate([a["w_group_2"], a["w_expert_2"]], axis=2)
    return np.ascontiguousarray(w.reshape(LAYERS, KT, P, NG + NE).transpose(0, 2, 1, 3).reshape(LAYERS, P, -1))


def _small(a):
    small = np.zeros((P, SMALL_N), np.float32)

    def put(name, part):
        lo, hi = SMALL[name]
        small[0:part.shape[0], lo:hi] = part.reshape(part.shape[0], hi - lo)

    def columns(w):
        return w.reshape(-1, P).T

    def rows(w):
        return np.broadcast_to(w.reshape(1, -1), (P, w.size))

    put("attn_g", columns(a["attn_norm"]))
    put("ffn_g", columns(a["ffn_norm"]))
    put("norm1_g", columns(a["norm1_g_2"]))
    put("norm2_g", columns(a["norm2_g_2"]))
    put("c_g", columns(np.concatenate([a["q_norm_g_2"], a["kv_norm_g_2"]], axis=1)))
    put("subln", columns(a["diff_subln"]))
    put("conv_b", columns(a["ffn_conv_b"]))
    put("conv_w", columns(a["ffn_conv_w"]))
    put("b_f", a["hyb_b_f"].reshape(-1, 1))
    put("router_b", np.concatenate([a["b_group_2"], a["b_expert_2"]], axis=1).T)
    put("pool_scale", rows(a["pool_scale_2"]))
    put("lam", rows(a["diff_lambda"]))
    put("pool_w", a["pool_w_2"].transpose(2, 0, 1, 3).reshape(HD, -1))
    return small


def kernel(**inputs):
    import concourse.bacc as _bacc
    from concourse.bass_utils import run_bass_kernel_spmd as _run

    a = {k: np.asarray(v) for k, v in inputs.items()}
    gains = np.stack([np.broadcast_to(a[k].reshape(1, D), (P, D)) for k in ("final_norm", "final_g_2")])
    arrays = {
        "x": np.ascontiguousarray(a["x"].reshape(S, D)), "stream": _stream(a), "router": _router(a), "small": _small(a),
        "const": _constants(), "fgain": np.ascontiguousarray(gains),
    }
    nc = _bacc.Bacc("TRN2", target_bir_lowering=False, num_devices=1)
    args = [nc.dram_tensor(n, v.shape, F32, kind="ExternalInput").ap() for n, v in arrays.items()]
    args.append(nc.dram_tensor("out", (S, D), F32, kind="ExternalOutput").ap())
    build(nc, *args)
    r = _run(nc, [arrays], core_ids=[0])
    return r.results[0]["out"].reshape(1, S, D)
```
